# Optimizing a Trainium2 kernel written in Bass

```python
import jax, jax.numpy as jnp
from jax import lax
import numpy as np

D_MODEL = 1024
BATCH = 1
SEQ = 256
DEPTH = 2

GRID_W = 64
CTX_LEN = 256
M_HEADS = 4
M_HEAD_DIM = 128
M_WIDTH = M_HEADS * M_HEAD_DIM
M_CHUNK = 128
M_CONV = 5
MLA_HEADS = 8
MLA_Q_RANK = 256
MLA_KV_RANK = 128
MLA_NOPE = 64
MLA_ROPE = 32
MLA_V = 64
MLA_QK = MLA_NOPE + MLA_ROPE
G_HEADS = 8
G_KV_HEADS = 2
G_HEAD_DIM = 64
N_BRANCH = 3
BRANCH_W = 512
D_FF = 2816
Q_BLOCK = 128
ROPE_THETA = 10000.0
EPS = 1e-6
IN_SPLITS = (M_WIDTH, M_WIDTH, M_WIDTH, M_WIDTH, 4 * M_HEADS,
             MLA_Q_RANK, MLA_KV_RANK, MLA_ROPE,
             G_HEADS * G_HEAD_DIM, G_KV_HEADS * G_HEAD_DIM, G_KV_HEADS * G_HEAD_DIM,
             N_BRANCH * D_MODEL)
D_IN = sum(IN_SPLITS)

kernel_name = 'hybrid_mlstm_mla_gqa_prefix_block'

def _rms(x, g):
    xf = x.astype(jnp.float32)
    y = xf * lax.rsqrt(jnp.mean(xf * xf, axis=-1, keepdims=True) + EPS)
    return (y * g.astype(jnp.float32)).astype(x.dtype)

def _modulate(x, g, shift, scale):
    return _rms(x, g) * (1.0 + scale) + shift

def _swiglu(h, w_in, w_out):
    a, b = jnp.split(h @ w_in, 2, axis=-1)
    return (jax.nn.silu(a) * b) @ w_out

def _split_in(z):
    offs = np.cumsum(IN_SPLITS)[:-1].tolist()
    return jnp.split(z, offs, axis=-1)

def _dwconv(x, w):
    pad = w.shape[0] // 2
    return lax.conv_general_dilated(x, w, (1,), [(pad, pad)],
                                    dimension_numbers=('NWC', 'WIO', 'NWC'),
                                    feature_group_count=x.shape[-1])

def _rope_tables(rows, cols, rot_dim):
    quarter = rot_dim // 4
    inv = ROPE_THETA ** (-jnp.arange(quarter, dtype=jnp.float32) / quarter)
    ang = jnp.concatenate([rows[:, None] * inv, cols[:, None] * inv], axis=-1)
    return jnp.cos(ang), jnp.sin(ang)

def _rope(x, cos, sin):
    r = 2 * cos.shape[-1]
    d = x.shape[-1]
    xp, x1, x2 = x[..., :d - r], x[..., d - r:d - r // 2], x[..., d - r // 2:]
    c = cos[None, :, None, :].astype(x.dtype)
    s = sin[None, :, None, :].astype(x.dtype)
    return jnp.concatenate([xp, x1 * c - x2 * s, x2 * c + x1 * s], axis=-1)

def _attend(q, k, v):
    B, T, KH, G, dk = q.shape
    nb = T // Q_BLOCK
    qb = jnp.moveaxis(q.reshape(B, nb, Q_BLOCK, KH, G, dk), 1, 0)
    scale = dk ** -0.5

    def block(qi):
        s = jnp.einsum('bqhgd,bkhd->bhgqk', qi, k).astype(jnp.float32) * scale
        p = jax.nn.softmax(s, axis=-1).astype(v.dtype)
        return jnp.einsum('bhgqk,bkhe->bqhge', p, v)

    o = lax.map(block, qb)
    return jnp.moveaxis(o, 0, 1).reshape(B, T, KH * G * v.shape[-1])

def _mlstm_scan(q, k, v, ig, flog, state):
    B, T, H, dk = q.shape
    nc = T // M_CHUNK
    f32 = jnp.float32

    def chunks(a):
        return jnp.moveaxis(a.astype(f32).reshape((B, nc, M_CHUNK) + a.shape[2:]), 1, 0)

    lower = jnp.tril(jnp.ones((M_CHUNK, M_CHUNK), dtype=bool))[None, :, :, None]

    def step(carry, xs):
        C, n, m = carry
        qc, kc, vc, ic, fc = xs
        b = jnp.cumsum(fc, axis=1)
        dmat = jnp.where(lower, b[:, :, None, :] - b[:, None, :, :] + ic[:, None, :, :], -jnp.inf)
        m_inter = b + m[:, None, :]
        m_t = jnp.maximum(m_inter, jnp.max(dmat, axis=2))
        s = jnp.einsum('bthd,bshd->btsh', qc, kc) * jnp.exp(dmat - m_t[:, :, None, :])
        a = jnp.exp(m_inter - m_t)
        num = jnp.einsum('btsh,bshe->bthe', s, vc) + a[..., None] * jnp.einsum('bthd,bhde->bthe', qc, C)
        den = jnp.sum(s, axis=2) + a * jnp.einsum('bthd,bhd->bth', qc, n)
        h = num / jnp.maximum(jnp.abs(den), jnp.exp(-m_t))[..., None]
        b_end = b[:, -1, :]
        w_log = b_end[:, None, :] - b + ic
        m_new = jnp.maximum(b_end + m, jnp.max(w_log, axis=1))
        decay = jnp.exp(b_end + m - m_new)
        w = jnp.exp(w_log - m_new[:, None, :])
        C = decay[..., None, None] * C + jnp.einsum('bsh,bshd,bshe->bhde', w, kc, vc)
        n = decay[..., None] * n + jnp.einsum('bsh,bshd->bhd', w, kc)
        return (C, n, m_new), h

    state, hs = lax.scan(step, state, (chunks(q), chunks(k), chunks(v), chunks(ig), chunks(flog)))
    h = jnp.moveaxis(hs, 0, 1).reshape(B, T, H, v.shape[-1]).astype(v.dtype)
    return h, state

def _mlstm_prep(q, k, v, gates, w_conv, b_gate):
    B, T, _ = q.shape
    qk = jax.nn.silu(_dwconv(jnp.concatenate([q, k], axis=-1), w_conv))
    q, k = jnp.split(qk, 2, axis=-1)
    q = q.reshape(B, T, M_HEADS, M_HEAD_DIM)
    k = k.reshape(B, T, M_HEADS, M_HEAD_DIM) * (M_HEAD_DIM ** -0.5)
    v = v.reshape(B, T, M_HEADS, M_HEAD_DIM)
    gt = gates.reshape(B, T, 4, M_HEADS).astype(jnp.float32) + b_gate.astype(jnp.float32)
    fwd = (gt[:, :, 0], jax.nn.log_sigmoid(gt[:, :, 1]))
    bwd = (gt[:, :, 2], jax.nn.log_sigmoid(gt[:, :, 3]))
    return q, k, v, fwd, bwd

def _mlstm_out(h, o, g_head):
    B, T = o.shape[:2]
    return _rms(h, g_head.reshape(M_HEADS, M_HEAD_DIM)).reshape(B, T, M_WIDTH) * jax.nn.sigmoid(o)

def _mlstm_branch(pl, pc, w_conv, b_gate, g_head, ctx_out):
    ql, kl, vl, fl, bl = _mlstm_prep(pl[0], pl[1], pl[2], pl[4], w_conv, b_gate)
    qc, kc, vc, fc, bc = _mlstm_prep(pc[0], pc[1], pc[2], pc[4], w_conv, b_gate)
    B = ql.shape[0]
    f32 = jnp.float32
    zero = (jnp.zeros((B, M_HEADS, M_HEAD_DIM, M_HEAD_DIM), f32),
            jnp.zeros((B, M_HEADS, M_HEAD_DIM), f32),
            jnp.zeros((B, M_HEADS), f32))

    def flip(a):
        return jnp.flip(a, axis=1)

    hcf, s_f = _mlstm_scan(qc, kc, vc, fc[0], fc[1], zero)
    hlf, _ = _mlstm_scan(ql, kl, vl, fl[0], fl[1], s_f)
    hcb, s_b = _mlstm_scan(flip(qc), flip(kc), flip(vc), flip(bc[0]), flip(bc[1]), zero)
    hlb, _ = _mlstm_scan(flip(ql), flip(kl), flip(vl), flip(bl[0]), flip(bl[1]), s_b)
    y = _mlstm_out(hlf + flip(hlb), pl[3], g_head)
    yc = _mlstm_out(hcf + flip(hcb), pc[3], g_head) if ctx_out else None
    return y, yc

def _mla_qkv(cq, ckv, kr, g_cq, g_ckv, w_uq, w_ukv, g_q, g_k):
    B, T, _ = cq.shape
    q = (_rms(cq, g_cq) @ w_uq).reshape(B, T, MLA_HEADS, MLA_QK)
    kv = (_rms(ckv, g_ckv) @ w_ukv).reshape(B, T, MLA_HEADS, MLA_NOPE + MLA_V)
    k_rope = jnp.broadcast_to(kr[:, :, None, :], (B, T, MLA_HEADS, MLA_ROPE))
    k = jnp.concatenate([kv[..., :MLA_NOPE], k_rope], axis=-1)
    return _rms(q, g_q), _rms(k, g_k), kv[..., MLA_NOPE:]

def _gqa_qkv(q, k, v, g_q, g_k):
    B, T, _ = q.shape
    q = _rms(q.reshape(B, T, G_HEADS, G_HEAD_DIM), g_q)
    k = _rms(k.reshape(B, T, G_KV_HEADS, G_HEAD_DIM), g_k)
    return q, k, v.reshape(B, T, G_KV_HEADS, G_HEAD_DIM)

def _group(q, n_kv):
    B, T, H, d = q.shape
    return q.reshape(B, T, n_kv, H // n_kv, d)

def _merge(ys, gate_pre, w_branch, w_out):
    B, T, _ = gate_pre.shape
    y = jnp.stack(ys, axis=2)
    proj = jnp.einsum('btnw,nwd->btnd', y, w_branch)
    g = jax.nn.sigmoid(gate_pre.reshape(B, T, N_BRANCH, D_MODEL))
    return jnp.einsum('btnd,btnd->btd', g, proj) @ w_out

def _token_mixer(h, hc, w_in, b_gate, w_conv, g_head, g_cq, g_ckv, w_uq, w_ukv, g_qm, g_km, g_qg, g_kg,
                 w_branch, w_out, rope_mla, rope_gqa, ctx_out):
    pl = _split_in(h @ w_in)
    pc = _split_in(hc @ w_in)
    y_m, yc_m = _mlstm_branch(pl, pc, w_conv, b_gate, g_head, ctx_out)
    qa, ka, va = _mla_qkv(pl[5], pl[6], pl[7], g_cq, g_ckv, w_uq, w_ukv, g_qm, g_km)
    qa_c, ka_c, va_c = _mla_qkv(pc[5], pc[6], pc[7], g_cq, g_ckv, w_uq, w_ukv, g_qm, g_km)
    qa = _rope(qa, *rope_mla)
    ka = _rope(ka, *rope_mla)
    y_a = _attend(qa[:, :, :, None, :], jnp.concatenate([ka, ka_c], axis=1), jnp.concatenate([va, va_c], axis=1))
    qg, kg, vg = _gqa_qkv(pl[8], pl[9], pl[10], g_qg, g_kg)
    qg_c, kg_c, vg_c = _gqa_qkv(pc[8], pc[9], pc[10], g_qg, g_kg)
    qg = _rope(qg, *rope_gqa)
    kg = _rope(kg, *rope_gqa)
    y_g = _attend(_group(qg, G_KV_HEADS), jnp.concatenate([kg, kg_c], axis=1), jnp.concatenate([vg, vg_c], axis=1))
    y = _merge((y_m, y_a, y_g), pl[11], w_branch, w_out)
    if not ctx_out:
        return y, None
    yc_a = _attend(qa_c[:, :, :, None, :], ka_c, va_c)
    yc_g = _attend(_group(qg_c, G_KV_HEADS), kg_c, vg_c)
    yc = _merge((yc_m, yc_a, yc_g), pc[11], w_branch, w_out)
    return y, yc

def setup_inputs(seed: int = 0) -> dict:
    key = jax.random.key(seed)
    ks = jax.random.split(key, 24)
    f32 = jnp.float32
    D = D_MODEL

    def nrm(k, shape, scale):
        return jax.random.normal(k, shape, f32) * scale

    def gain(k, shape):
        return 1.0 + 0.02 * jax.random.normal(k, shape, f32)

    gk = jax.random.split(ks[8], 4)
    b_mgate = jnp.stack([
        nrm(gk[0], (DEPTH, M_HEADS), 0.1),
        jax.random.uniform(gk[1], (DEPTH, M_HEADS), f32, 3.0, 6.0),
        nrm(gk[2], (DEPTH, M_HEADS), 0.1),
        jax.random.uniform(gk[3], (DEPTH, M_HEADS), f32, 3.0, 6.0),
    ], axis=1)
    return {
        'x': nrm(ks[0], (BATCH, SEQ, D), 1.0),
        'c': nrm(ks[1], (BATCH, D), 1.0),
        'ctx': nrm(ks[2], (BATCH, CTX_LEN, D), 1.0),
        'c_ctx': nrm(ks[3], (D,), 1.0),
        'w_mod': nrm(ks[4], (DEPTH, D, 9 * D), 0.5 * D ** -0.5),
        'b_mod': nrm(ks[5], (DEPTH, 9 * D), 0.01),
        'g_norm': gain(ks[6], (DEPTH, 3, D)),
        'w_ffn_in': nrm(ks[7], (DEPTH, 2, D, 2 * D_FF), D ** -0.5),
        'w_ffn_out': nrm(ks[9], (DEPTH, 2, D_FF, D), D_FF ** -0.5),
        'w_in': nrm(ks[10], (DEPTH, D, D_IN), D ** -0.5),
        'b_mgate': b_mgate,
        'w_conv': nrm(ks[11], (DEPTH, M_CONV, 1, 2 * M_WIDTH), M_CONV ** -0.5),
        'g_mhead': gain(ks[12], (DEPTH, M_WIDTH)),
        'g_cq': gain(ks[13], (DEPTH, MLA_Q_RANK)),
        'g_ckv': gain(ks[14], (DEPTH, MLA_KV_RANK)),
        'w_uq': nrm(ks[15], (DEPTH, MLA_Q_RANK, MLA_HEADS * MLA_QK), MLA_Q_RANK ** -0.5),
        'w_ukv': nrm(ks[16], (DEPTH, MLA_KV_RANK, MLA_HEADS * (MLA_NOPE + MLA_V)), MLA_KV_RANK ** -0.5),
        'g_q_mla': gain(ks[17], (DEPTH, MLA_QK)),
        'g_k_mla': gain(ks[18], (DEPTH, MLA_QK)),
        'g_q_gqa': gain(ks[19], (DEPTH, G_HEAD_DIM)),
        'g_k_gqa': gain(ks[20], (DEPTH, G_HEAD_DIM)),
        'w_branch': nrm(ks[21], (DEPTH, N_BRANCH, BRANCH_W, D), BRANCH_W ** -0.5),
        'w_out': nrm(ks[22], (DEPTH, D, D), D ** -0.5),
    }

def reference(x, c, ctx, c_ctx, w_mod, b_mod, g_norm, w_ffn_in, w_ffn_out, w_in, b_mgate, w_conv, g_mhead,
              g_cq, g_ckv, w_uq, w_ukv, g_q_mla, g_k_mla, g_q_gqa, g_k_gqa, w_branch, w_out):
    n_tok = x.shape[1]
    ROWS = n_tok // GRID_W
    rows = jnp.broadcast_to(jnp.arange(ROWS, dtype=jnp.float32)[:, None], (ROWS, GRID_W)).reshape(-1)
    cols = jnp.broadcast_to(jnp.arange(GRID_W, dtype=jnp.float32)[None, :], (ROWS, GRID_W)).reshape(-1)
    rope_mla = _rope_tables(rows, cols, MLA_ROPE)
    rope_gqa = _rope_tables(rows, cols, G_HEAD_DIM)
    s_lat = jax.nn.silu(c)
    s_ctx = jax.nn.silu(c_ctx)
    xc = ctx
    for l in range(DEPTH):
        last = l == DEPTH - 1
        mod = jnp.split((s_lat @ w_mod[l] + b_mod[l])[:, None, :], 9, axis=-1)
        modc = jnp.split((s_ctx @ w_mod[l] + b_mod[l])[None, None, :], 9, axis=-1)
        x = x + 0.5 * mod[2] * _swiglu(_modulate(x, g_norm[l, 0], mod[0], mod[1]), w_ffn_in[l, 0], w_ffn_out[l, 0])
        xc = xc + 0.5 * modc[2] * _swiglu(_modulate(xc, g_norm[l, 0], modc[0], modc[1]), w_ffn_in[l, 0], w_ffn_out[l, 0])
        h = _modulate(x, g_norm[l, 1], mod[3], mod[4])
        hc = _modulate(xc, g_norm[l, 1], modc[3], modc[4])
        y, yc = _token_mixer(h, hc, w_in[l], b_mgate[l], w_conv[l], g_mhead[l], g_cq[l], g_ckv[l], w_uq[l], w_ukv[l],
                             g_q_mla[l], g_k_mla[l], g_q_gqa[l], g_k_gqa[l], w_branch[l], w_out[l],
                             rope_mla, rope_gqa, not last)
        x = x + mod[5] * y
        if not last:
            xc = xc + modc[5] * yc
            xc = xc + 0.5 * modc[8] * _swiglu(_modulate(xc, g_norm[l, 2], modc[6], modc[7]), w_ffn_in[l, 1], w_ffn_out[l, 1])
        x = x + 0.5 * mod[8] * _swiglu(_modulate(x, g_norm[l, 2], mod[6], mod[7]), w_ffn_in[l, 1], w_ffn_out[l, 1])
    return x


_drawn_inputs = setup_inputs


def setup_inputs(seed=0):
    import zlib

    import numpy as np

    out = dict(_drawn_inputs(seed))
    spreads = {}
    factors = {'b_mod': 5.123,
     'g_norm': 8.0,
     'g_mhead': 44.571,
     'g_cq': 8.0,
     'g_ckv': 8.0,
     'g_q_mla': 8.0,
     'g_k_mla': 8.0,
     'g_q_gqa': 8.0,
     'g_k_gqa': 8.0}
    for name, (base, spread) in spreads.items():
        noise = np.random.default_rng([zlib.crc32(name.encode()), seed]).standard_normal(out[name].shape)
        drawn = base * np.exp(spread * noise) if base else spread * noise
        out[name] = __import__('jax').numpy.asarray(drawn.astype(out[name].dtype))
    for name, factor in factors.items():
        out[name] = (out[name] * factor).astype(out[name].dtype)
    return out
```

```python
from contextlib import ExitStack

import concourse.bass as bass
import numpy as np
from concourse import mybir

D, T, DEPTH = 1024, 512, 2
CTX = 256
KT = D // 128
DFF = 2816
FT = DFF // 128
MH, MD, MW = 4, 128, 512
TAPS = 5
NT = T // 128
QR, KVR = 256, 128
AH, NOPE, ROPE, AV = 8, 64, 32, 64
AQK = NOPE + ROPE
GH, GKV, GD = 8, 2, 64
NBR, BW = 3, 512
EPS = 1e-6
THETA = 10000.0
GRID_W = 64
RING = 4
UNIT = 512
NEG = -1e30
CQ_, CK_, CV_, CO_ = 0, 512, 1024, 1536
CGATE = 2048
CCQ = CGATE + 4 * MH
CCKV = CCQ + QR
CKR = CCKV + KVR
CGQ = CKR + ROPE
CGK = CGQ + GH * GD
CGV = CGK + GKV * GD
CBG = CGV + GKV * GD
P_NORM, P_CONV = 0, 3 * KT
P_MH = P_CONV + TAPS * 2 * MH
P_CQ = P_MH + MH
P_CKV = P_CQ + QR // 128
P_QG, P_KG, P_QM, P_KM = P_CKV + 1, P_CKV + 2, P_CKV + 3, P_CKV + 4
P_ROWS = P_KM + 1
M_ROWS = 9 * KT
VECTORS = DEPTH * (5 + 6 + 1 + 4)


def tables():
    def rope(dim):
        quarter = dim // 4
        inv = np.float32(THETA) ** (-np.arange(quarter, dtype=np.float32) / np.float32(quarter))
        t = np.arange(T - CTX)
        rows, cols = (t // GRID_W).astype(np.float32), (t % GRID_W).astype(np.float32)
        ang = np.concatenate([rows[:, None] * inv, cols[:, None] * inv], -1).astype(np.float32)
        return np.cos(ang).T, np.sin(ang).T

    def full(dim, head, copies):
        c, s = rope(dim)
        half = dim // 2
        cos, sin = np.ones((head, T), np.float32), np.zeros((head, T), np.float32)
        cos[head - dim:, CTX:] = np.concatenate([c, c])
        sin[head - dim:, CTX:] = np.concatenate([s, s])
        rot = np.zeros((head, head), np.float32)
        for i in range(half):
            a, b = head - dim + i, head - half + i
            rot[b, a] = -1.0
            rot[a, b] = 1.0
        return (np.tile(cos, (copies, 1)), np.tile(sin, (copies, 1)),
                np.kron(np.eye(copies, dtype=np.float32), rot))

    parts = {}
    parts["ident"] = np.eye(128, dtype=np.float32)
    s, t = np.arange(128)[:, None], np.arange(128)[None, :]
    parts["mask"] = np.concatenate([np.where(s <= t, 0.0, NEG), np.where(s >= t, 0.0, NEG)], 1)
    parts["ones"] = np.ones((128, 128))
    parts["ones64"] = np.kron(np.eye(2), np.ones((64, 64)))
    parts["cosg"], parts["sing"], parts["rotg"] = full(GD, GD, 2)
    parts["cosm"], parts["sinm"], parts["rotm"] = full(ROPE, AQK, 1)
    sel = np.zeros((16, 4, 36))
    for h in range(MH):
        sel[h, 0, h] = sel[2 * MH + h, 1, 32 + h] = 1
        sel[MH + h, 2, h] = sel[3 * MH + h, 3, 32 + h] = 1
    parts["sel"] = sel.reshape(16, -1)
    parts["comb"] = np.array([[1, 0], [0, 1], [1, 0], [0, 1]])
    at, width = {}, 0
    for name, a in parts.items():
        at[name] = (width, a.shape[0], a.shape[1])
        width += a.shape[1]
    out = np.zeros((128, width), np.float32)
    for name, a in parts.items():
        w, r, c = at[name]
        out[:r, w:w + c] = a
    return out, at


def make_plan():
    plan, size, ends = {}, [], []

    def add(key, units, n_groups=1, width=UNIT):
        plan[key] = (len(size), len(ends))
        for _ in range(n_groups):
            size.extend([width] * (units // n_groups))
            ends.append(len(size))

    for l in range(DEPTH):
        add((l, "mod"), 18 * KT, 18)
        add((l, "in", 0), FT // 2 * KT, FT // 2)
        add((l, "out", 0), 2 * FT, 2)
        for name in ("q", "k", "v"):
            add((l, name), KT)
        add((l, "cqkv"), KT, 1, QR + KVR)
        size.append(KT * ROPE)
        ends[-1] += 1
        add((l, "gates"), 1, 1, KT * 4 * MH)
        add((l, "o"), KT)
        add((l, "uq", 0), 2, 1, 4 * AQK)
        add((l, "uq", 1), 2, 1, 4 * AQK)
        add((l, "kn"), 1)
        add((l, "kv"), 1)
        add((l, "gq"), KT)
        add((l, "gkv"), KT, 1, 2 * GKV * GD)
        for og in range(2):
            for n in range(NBR):
                add((l, "gate", og, n), KT)
                add((l, "branch", og, n), BW // 128)
        add((l, "wout"), 2 * KT, 2)
        add((l, "in", 1), FT // 2 * KT, FT // 2)
        add((l, "out", 1), 2 * FT, 2)
    plan["end"] = (len(size), len(ends))
    return plan, size, ends


def build(nc, t, out, tab_at):
    fp32, f32r = mybir.dt.float32, mybir.dt.float32r
    ALU, ACT, AX = mybir.AluOpType, mybir.ActivationFunctionType, mybir.AxisListType
    plan, size, ends = make_plan()
    U = len(size)
    ctx = ExitStack()

    with ctx:
        def sb(name, shape, dt=fp32, where=ctx):
            return where.enter_context(nc.sbuf_tensor(name, shape, dt))

        sems = {}

        def sem(name):
            if name not in sems:
                sems[name] = ctx.enter_context(nc.semaphore(name))
            return sems[name]

        x = sb("x", [128, KT, T])
        h_hi = sb("h_hi", [128, KT, T], f32r)
        h_lo = sb("h_lo", [128, KT, T], f32r)
        w_raw = sb("w_raw", [128, RING, UNIT])
        w_hi = sb("w_hi", [128, RING, UNIT], f32r)
        w_lo = sb("w_lo", [128, RING, UNIT], f32r)
        tab = sb("tab", [128, t["tab"].shape[1]])
        cst = sb("cst", [128, 3])
        prm = sb("prm", [128, DEPTH, P_ROWS])
        bmod = sb("bmod", [128, DEPTH, M_ROWS])
        bgate = sb("bgate", [36, DEPTH, 2])
        mod = sb("mod", [128, 9, KT, 2])
        gain = sb("gain", [128, 3, KT, 2])
        s_in = sb("s_in", [2 * KT, 128])
        s_act = sb("s_act", [2 * KT, 128])
        s_fm = sb("s_fm", [128, 2 * KT])
        s4 = sb("s4", [128, KT, 4], f32r)
        mrow = sb("mrow", [4, 2, UNIT])

        y0h = y0l = None
        big = ExitStack()

        def region(stack, specs):
            return [sb(n, s, d, stack) for n, s, d in specs]

        mid_hi, mid_lo, sil, mt, sq, acc, rms, t1, hn = region(big, [
            ("mid_hi", [128, FT, T], f32r), ("mid_lo", [128, FT, T], f32r),
            ("sil", [128, 2, T], fp32), ("mt", [128, 2, T], fp32),
            ("sq", [128, 2, T], fp32), ("acc", [128, T], fp32), ("rms", [128, T], fp32),
            ("t1", [128, 2, T], fp32), ("hn", [128, 2, T], fp32)])
        big.close()
        big = ExitStack()
        xin, vrow, mvrow = region(big, [("xin", [128, NT, D], fp32), ("vrow", [P_ROWS, DEPTH, 128], fp32),
                                        ("mvrow", [M_ROWS, DEPTH, 128], fp32)])
        big.close()
        big = ExitStack()
        xout, = region(big, [("xout", [128, 2, D], fp32)])
        big.close()
        mix = ExitStack()
        y_hi, y_lo = [None] * 3, [None] * 3
        y_hi[0], y_lo[0], craw, krs = region(mix, [("y0h", [128, MH, T], f32r), ("y0l", [128, MH, T], f32r),
                                                   ("craw", [128, 3, T], fp32), ("krs", [96, T], fp32)])
        s1 = ExitStack()
        qk, vaug, R, RN, tok, hsn, dec, mprev, dlog = region(s1, [
            ("qk", [128, 2 * MH, T], fp32), ("vaug", [128, NT, MH, MD + 1], fp32),
            ("R", [36, 6, T], fp32), ("RN", [36, 5, T], fp32), ("tok", [128, 16, 36], fp32),
            ("hsn", [128, MH, NT, MD], fp32), ("dec", [128, 8, 4], fp32), ("mprev", [36, 5], fp32),
            ("dlog", [36, 4], fp32)])
        s2 = ExitStack()
        cpad, cacc, gz = region(s2, [("cpad", [128, 4, 2, CTX + 4], fp32), ("cacc", [128, 2, 2, CTX], fp32),
                                     ("gz", [16, T], fp32)])
        s2.close()
        s2 = ExitStack()
        dt_, P_, kw, HN, an, C_, sqt, dn, rn = region(s2, [
            ("dt_", [128, 2, NT, 128], fp32), ("P_", [128, 2, NT, 128], fp32), ("kw", [128, 2, NT, 128], fp32),
            ("HN", [128, 2, NT, MD + 1], fp32), ("an", [128, 2, MD + 1], fp32), ("C_", [128, 2, MD + 1], fp32),
            ("sqt", [128, NT, MD], fp32), ("dn", [128, 2, 4], fp32), ("rn", [128, 4], fp32)])
        s2.close()
        s2 = ExitStack()
        sigo, yt = region(s2, [("sigo", [128, MH, T], fp32), ("yt", [128, 2, T], fp32)])
        s2.close()
        s1.close()
        s1 = ExitStack()
        y_hi[1], y_lo[1] = region(mix, [("y1h", [128, 4, T], f32r), ("y1l", [128, 4, T], f32r)])
        q96, k96, vm = region(s1, [("q96", [AQK, AH, T], fp32), ("k96", [AQK, AH, T], fp32),
                                   ("vm", [128, NT, AH * AV], fp32)])
        s2 = ExitStack()
        cn, cn_hi, cn_lo, csq, crm = region(s2, [
            ("cn", [128, 3, T], fp32), ("cn_hi", [128, 3, T], f32r), ("cn_lo", [128, 3, T], f32r),
            ("csq", [128, 3, T], fp32), ("crm", [128, 2, T], fp32)])
        s2.close()

        def attention_scratch(stack, k):
            return region(stack, [
                (f"nsq{k}", [128, 2, T], fp32), (f"nrm{k}", [128, 2, T], fp32), (f"nxn{k}", [128, 2, T], fp32),
                (f"nco{k}", [128, 2, T], fp32), (f"nsi{k}", [128, 2, T], fp32),
                (f"pb{k}", [128, 2, T], fp32), (f"pt{k}", [128, 2, NT, 128], fp32), (f"ob{k}", [128, 8, 64], fp32),
                (f"mx{k}", [128, 2, 2], fp32), (f"rs{k}", [128, 2, 8], fp32)])
        s2 = ExitStack()
        scr = [attention_scratch(s2, 0)]
        s2.close()
        s1.close()
        s1 = ExitStack()
        y_hi[2], y_lo[2] = region(mix, [("y2h", [128, 4, T], f32r), ("y2l", [128, 4, T], f32r)])
        qg, kg, vg = region(s1, [("qg", [128, 4, T], fp32), ("kg", [128, GKV, T], fp32), ("vg", [128, NT, 128], fp32)])
        scr.append(attention_scratch(s1, 1))
        s1.close()
        s1 = ExitStack()
        g_hi, g_lo, sg, mg, mtmp = region(s1, [
            ("g_hi", [128, KT, T], f32r), ("g_lo", [128, KT, T], f32r),
            ("sg", [128, 4, T], fp32), ("mg", [128, 4, T], fp32), ("mtmp", [128, 4, T], fp32)])
        s1.close()
        mix.close()

        ps = ctx.enter_context(nc.psum_tensor("ps", [128, 8, 512], fp32))

        def tb(name, rows=None):
            w, r, c = tab_at[name]
            return tab[0:r, w:w + c]

        ident = tb("ident")

        landed = [sem(f"landed{i}") for i in range(RING)]
        hi_done, lo_done = sem("hi_done"), sem("lo_done")
        unit_used = sem("unit_used")
        banks_free = [sem("banks_free0"), sem("banks_free1")]

        def freed(g):
            return banks_free[g % 2], g // 2 + 1

        def first_col(l, only_latent):
            return CTX if l == DEPTH - 1 and only_latent else 0

        def streams(c0):
            return [(s, a, b) for s, a, b in ((1, 0, CTX), (0, CTX, T)) if a >= c0]

        class Chain:

            def __init__(self, eng, name):
                self.eng, self.order, self.counts = eng, sem(name), {}

            def __call__(self, ins, name=None):
                s = sem(name) if name else self.order
                key = name or "order"
                self.counts[key] = self.counts.get(key, 0) + 1
                ins.then_inc(s, 1)
                self.eng.wait_ge(s, self.counts[key])

        def scan_tile(d, j):
            return j if d == 0 else (1, 0, 3, 2)[j]

        def rope_setup(l, a):
            nsq, nrm, nxn, nco, nsi = scr[a][:5]
            cq = first_col(l, True)
            if a == 0:
                tiles = [(q96[:, h, :], cq, P_QM) for h in range(AH)] + [(k96[:, h, :], 0, P_KM) for h in range(AH)]
                return AQK, nxn, nco, nsi, tb("cosm"), tiles
            tiles = [(qg[:, i, :], cq, P_QG) for i in range(4)] + [(kg[:, i, :], 0, P_KG) for i in range(GKV)]
            return 128, nxn, nco, nsi, tb("cosg"), tiles

        def items(l):
            return [(qt, h) for qt in range(first_col(l, True) // 128, NT) for h in range(8)]

        def before(l, a):
            tiles = l * (2 * AH + 4 + GKV) + a * 2 * AH
            return tiles, sum(2 * len(items(p)) for p in range(l)) + a * len(items(l))

        def key_tiles(qt):
            return 2 if qt < 2 else NT

        def y0_bank(l, h):
            return (plan[l, "o"][1] + 1) % 2 * 4 + h

        block = ctx.enter_context(nc.Block())

        @block.sync
        def _(sp):
            sp.dma_start(tab[:, :], t["tab"]).then_inc(sem("tab_in"), 16)
            sp.dma_start(s_in[0:KT, :], t["c"].rearrange("b (k p) -> (b k) p", p=128)).then_inc(sem("s_in"), 16)
            sp.dma_start(s_in[KT:2 * KT, :], t["c_ctx"].rearrange("(k p) -> k p", p=128)).then_inc(sem("s_in"), 16)

            def unit(u, src, shape=None, it=None, per=0):
                if u >= RING:
                    need = u - RING + 1
                    sp.wait_ge(lo_done, need if it is None else need + it * per)
                n = size[u]
                dst = w_raw[:, u % RING, 0:n]
                if shape:
                    dst = dst.rearrange(shape[0], **shape[1])
                sp.dma_start(dst, src).then_inc(landed[u % RING], 16)

            def ffn_loads(l, f):
                u0, _ = plan[l, "in", f]
                w = t["w_ffn_in"][l, f].rearrange("k (s n) -> k s n", s=2)
                with sp.Fori(0, FT // 2) as g:
                    for k in range(KT):
                        unit(u0 + k, w[k * 128:(k + 1) * 128, :, bass.ds(g * 256, 256)],
                             ("p (s n) -> p s n", {"s": 2}), g, KT)
                u0, _ = plan[l, "out", f]
                w = t["w_ffn_out"][l, f].rearrange("(k p) n -> p k n", p=128)
                for g in range(2):
                    u = u0 + g * FT
                    cols = slice(g * 512, g * 512 + 512)
                    loops = FT // RING
                    with sp.Fori(0, loops) as i:
                        for j in range(RING):
                            unit(u + j, w[:, bass.ds(i * RING + j, 1), cols], ("p (a n) -> p a n", {"a": 1}), i, RING)
                    for k in range(loops * RING, FT):
                        unit(u + k, w[:, k, cols])

            def in_units(l, key, col, width, **kw_):
                u0, _ = plan[(l,) + key]
                for k in range(KT):
                    unit(u0 + k, t["w_in"][l, k * 128:(k + 1) * 128, col:col + width], **kw_)

            for l in range(DEPTH):
                u0, _ = plan[l, "mod"]
                for k in range(KT):
                    unit(u0 + k, t["w_mod"][l, k * 128:(k + 1) * 128, 0:512])
                with sp.Fori(0, 17) as g:
                    for k in range(KT):
                        unit(u0 + KT + k, t["w_mod"][l, k * 128:(k + 1) * 128, bass.ds(g * 512 + 512, 512)],
                             None, g, KT)
                ffn_loads(l, 0)
                in_units(l, ("q",), CQ_, 512)
                in_units(l, ("k",), CK_, 512)
                in_units(l, ("v",), CV_, 512)
                in_units(l, ("cqkv",), CCQ, QR + KVR)
                by_k = t["w_in"][l].rearrange("(k p) n -> p k n", p=128)
                unit(plan[l, "cqkv"][0] + KT, by_k[:, :, CKR:CKR + ROPE], ("p (k n) -> p k n", {"k": KT}))
                unit(plan[l, "gates"][0], by_k[:, :, CGATE:CGATE + 4 * MH], ("p (k n) -> p k n", {"k": KT}))
                in_units(l, ("o",), CO_, 512)
                for half in range(2):
                    for k in range(2):
                        unit(plan[l, "uq", half][0] + k,
                             t["w_uq"][l, k * 128:(k + 1) * 128, half * 4 * AQK:(half + 1) * 4 * AQK])
                kvw = t["w_ukv"][l].rearrange("k (h s e) -> k s h e", h=AH, s=2)
                unit(plan[l, "kn"][0], kvw[:, 0], ("p (h e) -> p h e", {"h": AH}))
                unit(plan[l, "kv"][0], kvw[:, 1], ("p (h e) -> p h e", {"h": AH}))
                in_units(l, ("gq",), CGQ, 512)
                in_units(l, ("gkv",), CGK, 2 * GKV * GD)
                for og in range(2):
                    for n in range(NBR):
                        in_units(l, ("gate", og, n), CBG + n * D + og * 512, 512)
                        for k in range(BW // 128):
                            unit(plan[l, "branch", og, n][0] + k,
                                 t["w_branch"][l, n, k * 128:(k + 1) * 128, og * 512:og * 512 + 512])
                for og in range(2):
                    for k in range(KT):
                        unit(plan[l, "wout"][0] + og * KT + k,
                             t["w_out"][l, k * 128:(k + 1) * 128, og * 512:og * 512 + 512])
                ffn_loads(l, 1)
            for i in range(2):
                sp.wait_ge(sem("out_ready"), 2 * (i + 1))
                sp.dma_start(out[0, i * 128:(i + 1) * 128, :], xout[:, i, :]).then_inc(sem("stored"), 16)
            sp.wait_ge(sem("stored"), 32)

        @block.gpsimd
        def _(pool):
            link = Chain(pool, "pool_order")
            link(nc.gpsimd.memset(vrow[:, :, :], 0.0))
            link(nc.gpsimd.memset(bgate[:, :, :], 0.0))
            vec = sem("vectors_in")
            for i in range(2):
                pool.dma_start(xin[:, i, :], t["ctx"][0, i * 128:(i + 1) * 128, :]).then_inc(sem("x_in"), 16)
                pool.dma_start(xin[:, 2 + i, :], t["x"][0, i * 128:(i + 1) * 128, :]).then_inc(sem("x_in"), 16)
            n = 0
            for l in range(DEPTH):
                for row, src in (
                    (P_NORM, t["g_norm"][l].rearrange("j (k p) -> (j k) p", p=128)),
                    (P_CONV, t["w_conv"][l].rearrange("j o (k p) -> (j o k) p", p=128)),
                    (P_MH, t["g_mhead"][l].rearrange("(k p) -> k p", p=128)),
                    (P_CQ, t["g_cq"][l].rearrange("(k p) -> k p", p=128)),
                    (P_CKV, t["g_ckv"][l].rearrange("(k p) -> k p", p=128)),
                ):
                    pool.dma_start(vrow[row:row + src.shape[0], l, :], src).then_inc(vec, 16)
                    n += 1
                for row, name, width, copies in ((P_QG, "g_q_gqa", GD, 2), (P_KG, "g_k_gqa", GD, 2),
                                                 (P_QM, "g_q_mla", AQK, 1), (P_KM, "g_k_mla", AQK, 1)):
                    for c in range(copies):
                        pool.dma_start(vrow[row:row + 1, l, c * width:(c + 1) * width],
                                       t[name][l].rearrange("(a n) -> a n", a=1)).then_inc(vec, 16)
                        n += 1
                pool.dma_start(mvrow[:, l, :], t["b_mod"][l].rearrange("(k p) -> k p", p=128)).then_inc(vec, 16)
                n += 1
                for q in range(4):
                    at = 32 * (q // 2)
                    pool.dma_start(bgate[at:at + MH, l, q % 2:q % 2 + 1],
                                   t["b_mgate"][l, q].rearrange("(h a) -> h a", a=1)).then_inc(vec, 16)
                    n += 1
            assert n == VECTORS

            for l in range(DEPTH):
                pool.wait_ge(*freed(plan[l, "out", 0][1] + 1))
                link(nc.gpsimd.memset(RN[:, :, :], 0.0))
                link(nc.gpsimd.memset(vaug[:, :, :, MD:MD + 1], 1.0), f"mixer_filled_{l}")
                pool.wait_ge(sem(f"y0_{l}"), MH)
                link(nc.gpsimd.tensor_copy(k96[NOPE:AQK, :, :],
                                           krs[NOPE:AQK, :].rearrange("p (a n) -> p a n", a=1)
                                           .to_broadcast([ROPE, AH, T])), f"kr_spread_{l}")
                for a in (0, 1):
                    P, xn, co, si, cos, tiles = rope_setup(l, a)
                    for i, (dst, c0, _) in enumerate(tiles):
                        tb_, ib_ = before(l, a)
                        pool.wait_ge(sem("qn"), tb_ + i + 1)
                        nc.gpsimd.tensor_tensor(co[0:P, i % 2, c0:T], xn[0:P, i % 2, c0:T], cos[:, c0:T],
                                                ALU.mult).then_inc(sem("qcos"), 1)
                        pool.wait_ge(sem("qcos"), tb_ + i + 1)
                        pool.wait_ge(sem("qsin"), tb_ + i + 1)
                        nc.gpsimd.tensor_tensor(dst[:, c0:T], co[0:P, i % 2, c0:T], si[0:P, i % 2, c0:T],
                                                ALU.add).then_inc(sem("qk_final"), 1)
                        pool.wait_ge(sem("qk_final"), tb_ + i + 1)

        @block.scalar
        def _(act):
            A = nc.scalar.activation
            link = Chain(act, "act_order")
            pos = [0]

            def split(u, it=None, per=0):
                off = (lambda v, m: v if it is None else v + it * m)
                act.wait_ge(landed[u % RING], off(16 * (u // RING + 1), 16 * per // RING))
                if u >= RING:
                    act.wait_ge(unit_used, off(u - RING + 1, per))
                n = size[u]
                A(w_hi[:, u % RING, 0:n], w_raw[:, u % RING, 0:n], ACT.Copy).then_inc(hi_done, 1)

            def advance(n):
                for _ in range(n):
                    if pos[0] < U:
                        split(pos[0])
                    pos[0] += 1

            def wait_group(g, it=None, per=0):
                act.wait_ge(unit_used, ends[g] if it is None else ends[g] + it * (per * KT))

            def norm(l, j, g_prev):
                m_ = 3 * l + j
                c0 = first_col(l, j == 2)
                for i in range(KT):
                    if g_prev is None:
                        act.wait_ge(sem("x_ready"), NT)
                    else:
                        act.wait_ge(*freed(g_prev + i // 4))
                    if i >= 3:
                        act.wait_ge(sem("sq_added"), (KT - 1) * m_ + i - 2)
                    dst = acc[:, c0:T] if i == 0 else sq[:, i % 2, c0:T]
                    A(dst, x[:, i, c0:T], ACT.Square).then_inc(sem("sq"), 1)
                act.wait_ge(sem("ss"), m_ + 1)
                A(rms[:, c0:T], ps[:, 0, c0:T], ACT.Sqrt, bias=cst[:, 0:1], scale=1.0 / D).then_inc(sem("rms"), 1)
                for i in range(KT):
                    act.wait_ge(sem("scaled"), KT * m_ + i + 1)
                    if i >= 2:
                        act.wait_ge(sem("h"), KT * m_ + i - 1)
                    for s, a, b in streams(c0):
                        ins = A(hn[:, i % 2, a:b], t1[:, i % 2, a:b], ACT.Identity, bias=mod[:, 3 * j, i, s:s + 1])
                    ins.then_inc(sem("hn"), 1)
                    act.wait_ge(sem("hn"), KT * m_ + i + 1)
                    A(h_hi[:, i, c0:T], hn[:, i % 2, c0:T], ACT.Copy).then_inc(sem("h_hi"), 1)

            def ffn(l, f):
                done = FT // 2 * (2 * l + f)
                c0 = first_col(l, f == 1)
                n = T - c0
                u0, g0 = plan[l, "in", f]

                def evac(b, g, it=None):
                    wait_group(g0 + b, it, 2)
                    s4_ = (g0 + b) % 2 * 4
                    A(sil[:, :, 0:n], ps[:, s4_:s4_ + 2, 0:n], ACT.Silu).then_inc(sem("sil"), 1)
                    fs, fv = freed(g0 + b)
                    act.wait_ge(fs, fv if it is None else fv + it)
                    A(mid_hi[:, bass.ds(2 * g, 2) if it is not None else slice(2 * g, 2 * g + 2), 0:n],
                      mt[:, :, 0:n], ACT.Copy).then_inc(sem("mid_hi"), 1)

                advance(KT)
                evac(0, 0)
                with act.Fori(0, FT // 4) as i:
                    for b in (1, 2):
                        for j in range(KT):
                            split(pos[0] + (b - 1) * KT + j, i, 2 * KT)
                        evac(b, i * 2 + b, i)
                pos[0] += 2 * KT * (FT // 4)
                _, g0 = plan[l, "out", f]
                for g in range(2):
                    loops = FT // RING - (l == DEPTH - 1 and f == 1 and g == 1)
                    with act.Fori(0, loops) as i:
                        for j in range(RING):
                            split(pos[0] + j, i, RING)
                    pos[0] += loops * RING
                    advance(FT - loops * RING)

            def qk_norm(l, a):
                P, xn, co, si, cos, tiles = rope_setup(l, a)
                nsq, nrm = scr[a][:2]
                tb_, ib_ = before(l, a)
                per = AQK if a == 0 else GD
                if a == 0:
                    act.wait_ge(sem(f"kr_spread_{l}"), 1)

                def square(i):
                    dst, c0, _ = tiles[i]
                    A(nsq[0:P, i % 2, c0:T], dst[:, c0:T], ACT.Square).then_inc(sem("qsq"), 1)

                square(0)
                for i in range(len(tiles)):
                    if i + 1 < len(tiles):
                        if i >= 1:
                            act.wait_ge(sem("qss"), tb_ + i)
                        square(i + 1)
                    c0 = tiles[i][1]
                    act.wait_ge(sem("qss"), tb_ + i + 1)
                    if i >= 2:
                        act.wait_ge(sem("qn"), tb_ + i - 1)
                    A(nrm[0:P, i % 2, c0:T], ps[0:P, i % 2, c0:T], ACT.Sqrt, bias=cst[0:P, 0:1],
                      scale=1.0 / per).then_inc(sem("qrms"), 1)

            def attention(l, a):
                pb, pt, ob, mx, rs = scr[a][5:]
                tb_, ib_ = before(l, a)
                scale = (AQK if a == 0 else GD) ** -0.5
                its = items(l)
                for i, (qt, h) in enumerate(its):
                    n = key_tiles(qt) * 128
                    act.wait_ge(sem("amax"), ib_ + i + 1)
                    if i >= 2:
                        act.wait_ge(sem("apt"), ib_ + i - 1)
                    A(pb[:, i % 2, 0:n], ps[:, i % 3, 0:n], ACT.Exp, bias=mx[:, i % 2, 1:2], scale=scale,
                      accum_out=rs[:, qt % 2, h:h + 1]).then_inc(sem("aexp"), 1)
                    if h == 1 and i >= 8:
                        output(l, a, qt - 1, i // 8 - 1)
                output(l, a, its[-1][0], len(its) // 8 - 1)

            def output(l, a, qt, n):
                tb_, ib_ = before(l, a)
                act.wait_ge(sem("aot"), ib_ // 8 + n + 1)
                A(y_hi[1 + a][:, :, qt * 128:(qt + 1) * 128],
                  ps[:, 7, :].rearrange("p (k n) -> p k n", n=128), ACT.Copy).then_inc(sem("ayh"), 1)

            act.wait_ge(sem("cst"), 1)
            act.wait_ge(sem("s_in"), 32)
            A(s_act[:, :], s_in[:, :], ACT.Silu).then_inc(sem("s_act"), 1)
            act.wait_ge(sem("x_t"), 1)
            A(s_fm[:, :], ps[:, 0, 0:2 * KT], ACT.Copy).then_inc(sem("s_fm"), 1)
            act.wait_ge(sem("s_fm"), 1)
            A(s4[:, :, 0:2].rearrange("p k s -> p s k"), s_fm[:, :].rearrange("p (s k) -> p s k", s=2),
              ACT.Copy).then_inc(sem("s_hi"), 1)
            for i in range(NT):
                act.wait_ge(sem("x_t"), 2 + i)
                b = 2 + 2 * (i % 2)
                A(x[:, :, i * 128:(i + 1) * 128], ps[:, b:b + 2, :].rearrange("p a (k n) -> p (a k) n", n=128),
                  ACT.Copy).then_inc(sem("x_ready"), 1)
            advance(RING)

            g_prev = None
            for l in range(DEPTH):
                _, g0 = plan[l, "mod"]
                with act.Fori(0, 9) as i:
                    for b in range(2):
                        for j in range(KT):
                            split(pos[0] + b * KT + j, i, 2 * KT)
                        wait_group(g0 + b, i, 2)
                        A(mrow[:, b, :], ps[0:4, (g0 + b) % 2 * 4, :], ACT.Copy).then_inc(banks_free[(g0 + b) % 2], 1)
                pos[0] += 18 * KT
                norm(l, 0, g_prev)
                ffn(l, 0)
                g_prev = plan[l, "out", 0][1]
                norm(l, 1, g_prev)

                cq = first_col(l, True)
                act.wait_ge(sem(f"pads_{l}"), 1)
                for part, name in enumerate(("q", "k")):
                    c0 = cq if part == 0 else 0
                    s0 = c0 // CTX
                    advance(KT)
                    g = plan[l, name][1]
                    wait_group(g)
                    for i in range(4):
                        if part == 1:
                            act.wait_ge(sem(f"conv_{l}"), i + 1)
                        ins = A(cpad[:, i, s0:2, 2:2 + CTX],
                                ps[:, g % 2 * 4 + i, 0:T - c0].rearrange("p (s n) -> p s n", n=CTX), ACT.Copy)
                        ins.then_inc(banks_free[g % 2] if i == 3 else sem(f"cpad_{l}"), 1)
                    for i in range(4):
                        n = part * 4 + i
                        act.wait_ge(sem(f"conv_{l}"), n + 1)
                        A(qk[:, n, c0:T].rearrange("p (s n) -> p s n", n=CTX), cacc[:, n % 2, s0:2, :],
                          ACT.Silu).then_inc(sem(f"qk_{l}"), 1)
                advance(KT)
                g = plan[l, "v"][1]
                wait_group(g)
                act.wait_ge(sem(f"mixer_filled_{l}"), 1)
                A(vaug[:, :, :, 0:MD], ps[:, g % 2 * 4:g % 2 * 4 + 4, :].rearrange("p t (h e) -> p t h e", h=MH),
                  ACT.Copy).then_inc(banks_free[g % 2], 1)
                advance(KT + 1)
                g = plan[l, "cqkv"][1]
                b0 = g % 2 * 4
                wait_group(g)
                link(A(craw[:, 0:2, cq:T], ps[:, b0:b0 + 2, 0:T - cq], ACT.Copy))
                link(A(craw[:, 2, :], ps[:, b0 + 2, :], ACT.Copy))
                A(krs[NOPE:AQK, :], ps[0:ROPE, b0 + 3, :], ACT.Copy).then_inc(banks_free[g % 2], 1)
                advance(1)
                g = plan[l, "gates"][1]
                wait_group(g)
                A(gz[:, :], ps[0:16, g % 2 * 4, :], ACT.Copy).then_inc(banks_free[g % 2], 1)

                act.wait_ge(sem(f"rows_{l}"), 2)
                link(A(R[:, 4, :], R[:, 1, :], ACT.Abs))
                link(A(R[:, 4, :], R[:, 4, :], ACT.Exp, scale=-1.0))
                A(R[:, 4, :], R[:, 4, :], ACT.Ln, bias=cst[0:36, 2:3]).then_inc(sem(f"softplus_{l}"), 1)

                def natural(q, src, **kw_):
                    A(RN[0:MH, q, :], src[0:MH, :], ACT.Exp, **{a: v[0:MH] if a == "bias" else v for a, v in kw_.items()})
                    return A(RN[32:36, q, :].rearrange("p (s n) -> p s n", s=2)[:, :, ::-1],
                             src[32:36, :].rearrange("p (s n) -> p s n", s=2), ACT.Exp,
                             **{a: v[32:36] if a == "bias" else v for a, v in kw_.items()})

                for q in range(3):
                    act.wait_ge(sem(f"explog_{l}"), q + 1)
                    if q == 0:
                        natural(1, R[:, 4, :], scale=-1.0).then_inc(sem(f"exprow_{l}"), 1)
                    elif q == 1:
                        natural(2, R[:, 5, :]).then_inc(sem(f"exprow_{l}"), 1)
                    else:
                        natural(3, R[:, 0, :], scale=-1.0, bias=cst[0:36, 1:2]).then_inc(sem(f"exprow_{l}"), 1)
                act.wait_ge(sem(f"explog_{l}"), 4)
                A(dlog[:, :], dlog[:, :], ACT.Exp).then_inc(sem(f"exprow_{l}"), 1)
                act.wait_ge(sem(f"tokt_{l}"), 1)
                A(tok[:, 0:8, :], ps[:, 2, 0:288].rearrange("p (a b) -> p a b", b=36), ACT.Copy)
                link(A(tok[:, 8:16, :], ps[:, 3, 0:288].rearrange("p (a b) -> p a b", b=36), ACT.Copy))
                A(dec[:, :, :], ps[:, 4, 0:32].rearrange("p (a b) -> p a b", b=4), ACT.Copy).then_inc(sem(f"tok_{l}"), 1)

                t0 = cq // 128
                outs = [j for j in range(NT) if scan_tile(0, j) >= t0]
                for h in range(MH):
                    for d in range(2):
                        act.wait_ge(sem(f"dlog_{l}"), 2 * h + d + 1)
                        A(dt_[:, d, t0:, :], dt_[:, d, t0:, :], ACT.Exp).then_inc(sem(f"dexp_{l}"), 1)
                    if h:
                        act.wait_ge(sem(f"cupd_{l}"), 6 * h)
                    act.wait_ge(sem(f"headmm_{l}"), h + 1)
                    for d in range(2):
                        for j in range(NT - 1):
                            tt = scan_tile(d, j)
                            ins = A(kw[:, d, tt, :], ps[:, 3, tt * 128:(tt + 1) * 128], ACT.Copy,
                                    scale=tok[:, 8 + tt, 32 * d + h:32 * d + h + 1])
                    ins.then_inc(sem(f"kw_{l}"), 1)
                    for j in range(1, NT):
                        for d in range(2):
                            if j not in outs:
                                continue
                            tt = scan_tile(d, j)
                            n = 2 * (len(outs) * h + outs.index(j)) + d + 1
                            act.wait_ge(sem(f"nmm_{l}"), n)
                            A(an[:, d, :], ps[:, 6 + d, 0:MD + 1], ACT.Copy,
                              scale=tok[:, 4 + tt, 32 * d + h:32 * d + h + 1]).then_inc(sem(f"an_{l}"), 1)
                    act.wait_ge(sem(f"hsum_{l}"), h + 1)
                    link(A(sqt[:, t0:, :], hsn[:, h, t0:, :], ACT.Square), f"hsq_{l}")
                    act.wait_ge(sem(f"hss_{l}"), h + 1)
                    A(rn[:, t0:], rn[:, t0:], ACT.Sqrt, bias=cst[:, 0:1], scale=1.0 / MD).then_inc(sem(f"hrms_{l}"), 1)
                advance(KT)
                g = plan[l, "o"][1]
                wait_group(g)
                act.wait_ge(sem(f"hout_{l}"), MH)
                A(sigo[:, :, cq:T], ps[:, g % 2 * 4:g % 2 * 4 + 4, 0:T - cq], ACT.Sigmoid).then_inc(banks_free[g % 2], 1)
                for h in range(MH):
                    act.wait_ge(sem(f"yt_{l}"), h + 1)
                    A(y_hi[0][:, h, cq:T], yt[:, h % 2, cq:T], ACT.Copy).then_inc(sem(f"y0h_{l}"), 1)

                act.wait_ge(sem(f"y0_{l}"), MH)
                A(csq[:, 0:2, cq:T], craw[:, 0:2, cq:T], ACT.Square)
                A(csq[:, 2, :], craw[:, 2, :], ACT.Square).then_inc(sem(f"csq_{l}"), 1)
                act.wait_ge(sem(f"css_{l}"), 1)
                A(crm[:, 0, cq:T], ps[:, 0, cq:T], ACT.Sqrt, bias=cst[:, 0:1], scale=1.0 / QR)
                A(crm[:, 1, :], ps[:, 1, :], ACT.Sqrt, bias=cst[:, 0:1], scale=1.0 / KVR).then_inc(sem(f"crm_{l}"), 1)
                act.wait_ge(sem(f"cn_{l}"), 1)
                A(cn_hi[:, 0:2, cq:T], cn[:, 0:2, cq:T], ACT.Copy)
                A(cn_hi[:, 2, :], cn[:, 2, :], ACT.Copy).then_inc(sem(f"cn_hi_{l}"), 1)
                for half in range(2):
                    advance(2)
                    g = plan[l, "uq", half][1]
                    wait_group(g)
                    A(q96[:, half * 4:half * 4 + 4, cq:T], ps[0:AQK, g % 2 * 4:g % 2 * 4 + 4, 0:T - cq],
                      ACT.Copy).then_inc(banks_free[g % 2], 1)
                advance(1)
                g = plan[l, "kn"][1]
                b0 = g % 2 * 4
                wait_group(g)
                k2 = k96[0:NOPE].rearrange("p (i s) n -> p i s n", s=2)
                link(A(k2[:, :, 0, :], ps[0:NOPE, b0:b0 + 4, :], ACT.Copy))
                A(k2[:, :, 1, :], ps[NOPE:128, b0:b0 + 4, :], ACT.Copy).then_inc(banks_free[g % 2], 1)
                advance(1)
                g = plan[l, "kv"][1]
                wait_group(g)
                A(vm[:, :, :], ps[:, g % 2 * 4:g % 2 * 4 + 4, :], ACT.Copy).then_inc(banks_free[g % 2], 1)
                act.wait_ge(*freed(g))
                qk_norm(l, 0)
                attention(l, 0)

                act.wait_ge(sem("ay"), before(l, 0)[1] // 8 + len(items(l)) // 8)
                advance(KT)
                g = plan[l, "gq"][1]
                wait_group(g)
                A(qg[:, :, cq:T], ps[:, g % 2 * 4:g % 2 * 4 + 4, 0:T - cq], ACT.Copy).then_inc(banks_free[g % 2], 1)
                advance(KT)
                g = plan[l, "gkv"][1]
                b0 = g % 2 * 4
                wait_group(g)
                for m in range(GKV):
                    for r in (0, GD):
                        link(A(kg[r:r + GD, m, :], ps[m * GD:(m + 1) * GD, b0, :], ACT.Copy))
                A(vg[:, :, :], ps[:, b0 + 1, :].rearrange("p (t n) -> p t n", n=128), ACT.Copy).then_inc(banks_free[g % 2], 1)
                act.wait_ge(*freed(g))
                qk_norm(l, 1)
                attention(l, 1)

                act.wait_ge(sem("ay"), before(l, 1)[1] // 8 + len(items(l)) // 8)
                for og in range(2):
                    for n in range(NBR):
                        advance(KT)
                        g = plan[l, "gate", og, n][1]
                        wait_group(g)
                        if og or n:
                            act.wait_ge(*freed(g - 1))
                        A(sg[:, :, 0:T - cq], ps[:, g % 2 * 4:g % 2 * 4 + 4, 0:T - cq],
                          ACT.Sigmoid).then_inc(banks_free[g % 2], 1)
                        advance(BW // 128)
                    act.wait_ge(sem(f"mg_{l}"), og + 1)
                    A(g_hi[:, og * 4:og * 4 + 4, 0:T - cq], mg[:, :, 0:T - cq], ACT.Copy).then_inc(sem(f"g_hi_{l}"), 1)
                advance(2 * KT)
                g_prev = plan[l, "wout"][1]
                norm(l, 2, g_prev)
                ffn(l, 1)
                g_prev = plan[l, "out", 1][1]
            for i in range(2):
                for b in range(2):
                    act.wait_ge(sem("out_t"), i + 1)
                    A(xout[:, i, b * 512:(b + 1) * 512], ps[:, 2 * i + b, :], ACT.Copy).then_inc(sem("out_ready"), 1)

        @block.vector
        def _(dve):
            V = nc.vector
            link = Chain(dve, "dve_order")
            pos = [0]

            def split(u, it=None, per=0):
                n = size[u]
                dve.wait_ge(hi_done, u + 1 if it is None else u + 1 + it * per)
                V.tensor_tensor(w_lo[:, u % RING, 0:n], w_raw[:, u % RING, 0:n],
                                w_hi[:, u % RING, 0:n].bitcast(fp32), ALU.subtract).then_inc(lo_done, 1)

            def advance(n):
                for _ in range(n):
                    if pos[0] < U:
                        split(pos[0])
                    pos[0] += 1

            def norm(l, j):
                m_ = 3 * l + j
                c0 = first_col(l, j == 2)
                for i in range(1, KT):
                    dve.wait_ge(sem("sq"), KT * m_ + i + 1)
                    link(V.tensor_tensor(acc[:, c0:T], acc[:, c0:T], sq[:, i % 2, c0:T], ALU.add), "sq_added")
                dve.wait_ge(sem("rms"), m_ + 1)
                link(V.reciprocal(rms[:, c0:T], rms[:, c0:T]))
                for i in range(KT + 1):
                    if i < KT:
                        if i >= 2:
                            dve.wait_ge(sem("hn"), KT * m_ + i - 1)
                        for s, a, b in streams(c0):
                            ins = V.scalar_tensor_tensor(out=t1[:, i % 2, a:b], in0=x[:, i, a:b],
                                                         scalar=gain[:, j, i, s:s + 1], in1=rms[:, a:b],
                                                         op0=ALU.mult, op1=ALU.mult)
                        ins.then_inc(sem("scaled"), 1)
                    if i >= 1:
                        dve.wait_ge(sem("h_hi"), KT * m_ + i)
                        V.tensor_tensor(h_lo[:, i - 1, c0:T], hn[:, (i - 1) % 2, c0:T],
                                        h_hi[:, i - 1, c0:T].bitcast(fp32), ALU.subtract).then_inc(sem("h"), 1)

            def residual(l, m, g0, c0, gate):
                g = g0 + m
                dve.wait_ge(unit_used, ends[g])
                for i in range(4):
                    for s, a, b in streams(c0):
                        ins = V.scalar_tensor_tensor(out=x[:, 4 * m + i, a:b], in0=ps[:, g % 2 * 4 + i, a - c0:b - c0],
                                                     scalar=mod[:, gate, 4 * m + i, s:s + 1],
                                                     in1=x[:, 4 * m + i, a:b], op0=ALU.mult, op1=ALU.add)
                ins.then_inc(banks_free[g % 2], 1)

            def ffn(l, f):
                done = FT // 2 * (2 * l + f)
                c0 = first_col(l, f == 1)
                n = T - c0
                u0, g0 = plan[l, "in", f]

                def evac(b, g, it=None):
                    off = (lambda v: v if it is None else v + it * 2)
                    s4_ = (g0 + b) % 2 * 4
                    dve.wait_ge(sem("sil"), off(done + b + 1))
                    if b:
                        dve.wait_ge(sem("mid"), off(done + b))
                    V.tensor_tensor(mt[:, :, 0:n], ps[:, s4_ + 2:s4_ + 4, 0:n], sil[:, :, 0:n],
                                    ALU.mult).then_inc(banks_free[(g0 + b) % 2], 1)
                    dve.wait_ge(sem("mid_hi"), off(done + b + 1))
                    at = bass.ds(2 * g, 2) if it is not None else slice(2 * g, 2 * g + 2)
                    V.tensor_tensor(mid_lo[:, at, 0:n], mt[:, :, 0:n], mid_hi[:, at, 0:n].bitcast(fp32),
                                    ALU.subtract).then_inc(sem("mid"), 1)

                advance(KT)
                evac(0, 0)
                with dve.Fori(0, FT // 4) as i:
                    for b in (1, 2):
                        for j in range(KT):
                            split(pos[0] + (b - 1) * KT + j, i, 2 * KT)
                        evac(b, i * 2 + b, i)
                pos[0] += 2 * KT * (FT // 4)
                _, g0 = plan[l, "out", f]
                for g in range(2):
                    loops = FT // RING - (l == DEPTH - 1 and f == 1 and g == 1)
                    with dve.Fori(0, loops) as i:
                        for j in range(RING):
                            split(pos[0] + j, i, RING)
                    pos[0] += loops * RING
                    advance(FT - loops * RING)
                    residual(l, g, g0, c0, 2 if f == 0 else 8)

            def qk_norm(l, a):
                P, xn, co, si, cos, tiles = rope_setup(l, a)
                nrm = scr[a][1]
                sin = tb("sinm" if a == 0 else "sing")
                tb_, ib_ = before(l, a)

                def normed(i):
                    dst, c0, row = tiles[i]
                    dve.wait_ge(sem("qrms"), tb_ + i + 1)
                    if i >= 2:
                        dve.wait_ge(sem("qcos"), tb_ + i - 1)
                        dve.wait_ge(sem("qsin"), tb_ + i - 1)
                    link(V.reciprocal(nrm[0:P, i % 2, c0:T], nrm[0:P, i % 2, c0:T]))
                    V.scalar_tensor_tensor(out=xn[0:P, i % 2, c0:T], in0=dst[:, c0:T], scalar=prm[0:P, l, row:row + 1],
                                           in1=nrm[0:P, i % 2, c0:T], op0=ALU.mult,
                                           op1=ALU.mult).then_inc(sem("qn"), 1)

                normed(0)
                for i in range(len(tiles)):
                    if i + 1 < len(tiles):
                        normed(i + 1)
                    c0 = tiles[i][1]
                    dve.wait_ge(sem("qrot"), tb_ + i + 1)
                    if i >= 2:
                        dve.wait_ge(sem("qk_final"), tb_ + i - 1)
                    V.tensor_tensor(si[0:P, i % 2, c0:T], ps[0:P, 2 + i % 2, c0:T], sin[:, c0:T],
                                    ALU.mult).then_inc(sem("qsin"), 1)

            def attention(l, a):
                pb, pt, ob, mx, rs = scr[a][5:]
                tb_, ib_ = before(l, a)
                scale = (AQK if a == 0 else GD) ** -0.5
                its = items(l)

                def maxima(i):
                    n = key_tiles(its[i][0]) * 128
                    dve.wait_ge(sem("asc"), ib_ + i + 1)
                    if i >= 2:
                        dve.wait_ge(sem("aexp"), ib_ + i - 1)
                    link(V.reduce_max(mx[:, i % 2, 0:1], ps[:, i % 3, 0:n], AX.X))
                    V.tensor_scalar(mx[:, i % 2, 1:2], mx[:, i % 2, 0:1], -scale, None, ALU.mult).then_inc(sem("amax"), 1)

                maxima(0)
                for i, (qt, h) in enumerate(its):
                    if i + 1 < len(its):
                        maxima(i + 1)
                    n = key_tiles(qt)
                    dve.wait_ge(sem("atr"), ib_ + i + 1)
                    if i >= 2:
                        dve.wait_ge(sem("apv"), ib_ + i - 1)
                    V.tensor_copy(pt[:, i % 2, 0:n, :], ps[:, 3 + i % 2, 0:n * 128].rearrange("p (k n) -> p k n", n=128))\
                        .then_inc(sem("apt"), 1)
                    if h == 1 and i >= 8:
                        collect(l, a, i // 8 - 1, qt - 1, i - 2)
                collect(l, a, len(its) // 8 - 1, its[-1][0], len(its) - 1)

            def collect(l, a, n, qt, last_item):
                pb, pt, ob, mx, rs = scr[a][5:]
                tb_, ib_ = before(l, a)
                dve.wait_ge(sem("apv"), ib_ + last_item + 1)
                link(V.reciprocal(rs[:, qt % 2, :], rs[:, qt % 2, :]))
                V.tensor_tensor(ob[:, :, :], ps[:, 5 + n % 2, :].rearrange("p (h e) -> p h e", h=8),
                                rs[:, qt % 2, :].rearrange("p (h a) -> p h a", a=1).to_broadcast([128, 8, 64]),
                                ALU.mult).then_inc(sem("aob"), 1)
                dve.wait_ge(sem("ayh"), ib_ // 8 + n + 1)
                cols = slice(qt * 128, (qt + 1) * 128)
                V.tensor_tensor(y_lo[1 + a][:, :, cols], ps[:, 7, :].rearrange("p (k n) -> p k n", n=128),
                                y_hi[1 + a][:, :, cols].bitcast(fp32), ALU.subtract).then_inc(sem("ay"), 1)

            link(V.memset(cst[:, 0:1], EPS))
            link(V.memset(cst[:, 1:2], 0.5 * float(np.log(MD))))
            V.memset(cst[:, 2:3], 1.0).then_inc(sem("cst"), 1)
            dve.wait_ge(sem("s_hi"), 1)
            V.tensor_tensor(s4[:, :, 2:4].rearrange("p k s -> p s k"), s_fm[:, :].rearrange("p (s k) -> p s k", s=2),
                            s4[:, :, 0:2].rearrange("p k s -> p s k").bitcast(fp32), ALU.subtract).then_inc(sem("s4"), 1)
            dve.wait_ge(sem("vec_t"), 1)
            V.tensor_copy(prm[:, :, :], ps[:, 6, 0:DEPTH * P_ROWS].rearrange("p (l n) -> p l n", l=DEPTH))
            V.tensor_copy(bmod[:, :, :], ps[:, 7, 0:DEPTH * M_ROWS].rearrange("p (l n) -> p l n", l=DEPTH))\
                .then_inc(sem("params"), 1)
            dve.wait_ge(sem("params"), 1)
            advance(RING)

            for l in range(DEPTH):
                cq = first_col(l, True)
                with dve.Fori(0, 9) as i:
                    for j in range(2 * KT):
                        split(pos[0] + j, i, 2 * KT)
                pos[0] += 18 * KT
                dve.wait_ge(sem("mod_t"), 18 * (l + 1))
                m3 = mod[:, :, :, :].rearrange("p a k s -> p (a k) s")
                link(V.tensor_tensor(m3, ps[:, 7, 0:2 * M_ROWS].rearrange("p (a s) -> p a s", s=2),
                                     bmod[:, l, :].rearrange("p (a s) -> p a s", s=1).to_broadcast([128, M_ROWS, 2]),
                                     ALU.add))
                for j in range(3):
                    link(V.scalar_tensor_tensor(
                        out=gain[:, j, :, :], in0=mod[:, 3 * j + 1, :, :], scalar=1.0,
                        in1=prm[:, l, P_NORM + j * KT:P_NORM + (j + 1) * KT].rearrange("p (k s) -> p k s", s=1)
                        .to_broadcast([128, KT, 2]), op0=ALU.add, op1=ALU.mult))
                for gate in (2, 8):
                    link(V.tensor_scalar(mod[:, gate, :, :], mod[:, gate, :, :], 0.5, None, ALU.mult),
                         "mods")
                norm(l, 0)
                ffn(l, 0)
                norm(l, 1)

                dve.wait_ge(*freed(plan[l, "out", 0][1] + 1))
                V.memset(cpad[:, :, :, 0:2], 0.0)
                V.memset(cpad[:, :, :, 2 + CTX:4 + CTX], 0.0).then_inc(sem(f"pads_{l}"), 1)
                for part, name in enumerate(("q", "k")):
                    c0 = cq if part == 0 else 0
                    s0 = c0 // CTX
                    g = plan[l, name][1]
                    advance(RING)
                    for i in range(4):
                        n = part * 4 + i
                        if i < 3:
                            dve.wait_ge(sem(f"cpad_{l}"), 3 * part + i + 1)
                        else:
                            dve.wait_ge(*freed(g))
                        if n >= 2:
                            dve.wait_ge(sem(f"qk_{l}"), n - 1)
                        dst = cacc[:, n % 2, s0:2, :]
                        w = [prm[:, l, P_CONV + j * 2 * MH + n:P_CONV + j * 2 * MH + n + 1] for j in range(TAPS)]
                        link(V.tensor_scalar(dst, cpad[:, i, s0:2, 0:CTX], w[0], None, ALU.mult))
                        for j in range(1, TAPS):
                            ins = V.scalar_tensor_tensor(out=dst, in0=cpad[:, i, s0:2, j:j + CTX], scalar=w[j],
                                                         in1=dst, op0=ALU.mult, op1=ALU.add)
                            link(ins, f"conv_{l}" if j == TAPS - 1 else None)
                        advance(1)
                advance(KT)
                advance(KT + 1)
                advance(1)

                dve.wait_ge(sem(f"sel_{l}"), 1)
                link(V.tensor_scalar(R[:, 0, :], ps[0:36, 0, :], bgate[:, l, 0:1], None, ALU.add), f"rows_{l}")
                link(V.tensor_scalar(R[:, 1, :], ps[0:36, 1, :], bgate[:, l, 1:2], None, ALU.add), f"rows_{l}")
                dve.wait_ge(sem(f"softplus_{l}"), 1)
                link(V.scalar_tensor_tensor(out=R[:, 1, :], in0=R[:, 1, :], scalar=0.0, in1=R[:, 4, :],
                                            op0=ALU.min, op1=ALU.subtract))
                for j in range(NT):
                    c = slice(j * 128, (j + 1) * 128)
                    link(V.tensor_tensor_scan(R[:, 2, c], tb("ones")[0:36, :], R[:, 1, c], 0.0, ALU.mult, ALU.add))
                link(V.tensor_tensor(R[:, 3, :], R[:, 0, :], R[:, 2, :], ALU.subtract))
                link(V.memset(mprev[:, :], 0.0))
                for j in range(NT):
                    c = slice(j * 128, (j + 1) * 128)
                    e = (j + 1) * 128 - 1
                    link(V.tensor_tensor_scan(R[:, 1, c], R[:, 3, c], R[:, 3, c], mprev[:, j:j + 1], ALU.max, ALU.max))
                    link(V.tensor_tensor(mprev[:, j + 1:j + 2], R[:, 1, e:e + 1], R[:, 2, e:e + 1], ALU.add))

                def chunks(row):
                    return R[:, row, :].rearrange("p (j n) -> p j n", n=128)

                def spread(ap):
                    return ap.to_broadcast([36, NT, 128])

                last_m = chunks(1)[:, :, 127:128]
                starts = mprev[:, 0:NT].rearrange("p (j a) -> p j a", a=1)
                link(V.tensor_tensor(chunks(4), chunks(1), spread(starts), ALU.subtract), f"explog_{l}")
                link(V.tensor_tensor(chunks(5), chunks(3), spread(last_m), ALU.subtract), f"explog_{l}")
                link(V.tensor_tensor(R[:, 0, :], R[:, 2, :], R[:, 1, :], ALU.add), f"explog_{l}")
                link(V.tensor_tensor(dlog[:, :].rearrange("p (j a) -> p j a", a=1), starts, last_m, ALU.subtract),
                     f"explog_{l}")
                dve.wait_ge(sem(f"mixer_filled_{l}"), 1)
                for q, row, by in ((0, 3, 1.0), (4, 1, -1.0)):
                    V.tensor_scalar(RN[0:MH, q, :], R[0:MH, row, :], by, None, ALU.mult)
                    ins = V.tensor_scalar(RN[32:36, q, :].rearrange("p (s n) -> p s n", s=2)[:, :, ::-1],
                                          R[32:36, row, :].rearrange("p (s n) -> p s n", s=2), by, None, ALU.mult)
                    link(ins, f"rown_{l}")

                t0 = cq // 128
                nt = NT - t0
                outs = [j for j in range(NT) if scan_tile(0, j) >= t0]
                dve.wait_ge(sem(f"tok_{l}"), 1)
                mask = tb("mask").rearrange("p (d a n) -> p d a n", d=2, a=1)
                for h in range(MH):
                    dve.wait_ge(sem(f"headmm_{l}"), h + 1)
                    for d in range(2):
                        col = 32 * d + h
                        link(V.tensor_tensor(dt_[:, d, t0:, :], ps[:, 1 + d, t0 * 128:].rearrange("p (t n) -> p t n", n=128),
                                             tok[:, t0:4, col:col + 1].to_broadcast([128, nt, 128]), ALU.add))
                        link(V.tensor_tensor(dt_[:, d, t0:, :], dt_[:, d, t0:, :],
                                             mask[:, d].to_broadcast([128, nt, 128]), ALU.min), f"dlog_{l}")
                    for d in range(2):
                        dve.wait_ge(sem(f"dexp_{l}"), 2 * h + d + 1)
                        link(V.tensor_tensor(P_[:, d, t0:, :], dt_[:, d, t0:, :],
                                             ps[:, 0, t0 * 128:].rearrange("p (t n) -> p t n", n=128), ALU.mult),
                             f"P_{l}")
                    an_n = [j for j in outs if j >= 1]
                    for j in range(NT):
                        for d in range(2):
                            tt = scan_tile(d, j)
                            if j in outs:
                                n = 2 * (len(outs) * h + outs.index(j)) + d + 1
                                dve.wait_ge(sem(f"nmm_{l}"), n)
                                if j == 0:
                                    link(V.tensor_copy(HN[:, d, tt, :], ps[:, 4 + d, 0:MD + 1]), f"hn_{l}")
                                else:
                                    dve.wait_ge(sem(f"an_{l}"), 2 * (len(an_n) * h + an_n.index(j)) + d + 1)
                                    link(V.tensor_tensor(HN[:, d, tt, :], ps[:, 4 + d, 0:MD + 1], an[:, d, :], ALU.add),
                                         f"hn_{l}")
                            if j < NT - 1:
                                dve.wait_ge(sem(f"dcmm_{l}"), 2 * (3 * h + j) + d + 1)
                                if j == 0:
                                    link(V.tensor_copy(C_[:, d, :], ps[:, 1 + d, 0:MD + 1]), f"cupd_{l}")
                                else:
                                    link(V.scalar_tensor_tensor(out=C_[:, d, :], in0=C_[:, d, :],
                                                                scalar=dec[:, 4 * d + h, j:j + 1],
                                                                in1=ps[:, 1 + d, 0:MD + 1], op0=ALU.mult, op1=ALU.add),
                                         f"cupd_{l}")
                    den = HN[:, :, t0:, MD:MD + 1].rearrange("p d t a -> p d (t a)")
                    dnt = dn[:, :, t0:]
                    floor = tok[:, 12 + t0:16, :].rearrange("p t c -> p c t")[:, h:h + 33:32, :]
                    link(V.scalar_tensor_tensor(out=dnt, in0=den, scalar=-1.0, in1=den, op0=ALU.mult, op1=ALU.max))
                    link(V.tensor_tensor(dnt, dnt, floor, ALU.max))
                    link(V.reciprocal(dnt, dnt))
                    for d in range(2):
                        r = dn[:, d, t0:].rearrange("p (t a) -> p t a", a=1).to_broadcast([128, nt, MD])
                        link(V.tensor_tensor(HN[:, d, t0:, 0:MD], HN[:, d, t0:, 0:MD], r, ALU.mult))
                    link(V.tensor_tensor(hsn[:, h, t0:, :], HN[:, 0, t0:, 0:MD], HN[:, 1, t0:, 0:MD], ALU.add), f"hsum_{l}")
                    dve.wait_ge(sem(f"hsq_{l}"), h + 1)
                    link(V.reduce_sum(rn[:, t0:], sqt[:, t0:, :], AX.X), f"hss_{l}")
                    dve.wait_ge(sem(f"hrms_{l}"), h + 1)
                    link(V.reciprocal(rn[:, t0:], rn[:, t0:]))
                    link(V.tensor_tensor(hsn[:, h, t0:, :], hsn[:, h, t0:, :],
                                         rn[:, t0:].rearrange("p (t a) -> p t a", a=1).to_broadcast([128, nt, MD]),
                                         ALU.mult), f"hout_{l}")
                advance(KT)
                dve.wait_ge(*freed(plan[l, "o"][1]))
                for h in range(MH):
                    dve.wait_ge(sem(f"ht_{l}"), h + 1)
                    if h >= 2:
                        dve.wait_ge(sem(f"y0_{l}"), h - 1)
                    V.scalar_tensor_tensor(out=yt[:, h % 2, cq:T], in0=ps[:, y0_bank(l, h), cq:T],
                                           scalar=prm[:, l, P_MH + h:P_MH + h + 1], in1=sigo[:, h, cq:T],
                                           op0=ALU.mult, op1=ALU.mult).then_inc(sem(f"yt_{l}"), 1)
                    dve.wait_ge(sem(f"y0h_{l}"), h + 1)
                    V.tensor_tensor(y_lo[0][:, h, cq:T], yt[:, h % 2, cq:T], y_hi[0][:, h, cq:T].bitcast(fp32),
                                    ALU.subtract).then_inc(sem(f"y0_{l}"), 1)

                dve.wait_ge(sem(f"y0_{l}"), MH)
                dve.wait_ge(sem(f"crm_{l}"), 1)
                link(V.reciprocal(crm[:, 0, cq:T], crm[:, 0, cq:T]))
                link(V.reciprocal(crm[:, 1, :], crm[:, 1, :]))
                for i in range(3):
                    c0 = cq if i < 2 else 0
                    ins = V.scalar_tensor_tensor(out=cn[:, i, c0:T], in0=craw[:, i, c0:T],
                                                 scalar=prm[:, l, P_CQ + i:P_CQ + i + 1], in1=crm[:, i // 2, c0:T],
                                                 op0=ALU.mult, op1=ALU.mult)
                ins.then_inc(sem(f"cn_{l}"), 1)
                dve.wait_ge(sem(f"cn_hi_{l}"), 1)
                V.tensor_tensor(cn_lo[:, 0:2, cq:T], cn[:, 0:2, cq:T], cn_hi[:, 0:2, cq:T].bitcast(fp32), ALU.subtract)
                V.tensor_tensor(cn_lo[:, 2, :], cn[:, 2, :], cn_hi[:, 2, :].bitcast(fp32),
                                ALU.subtract).then_inc(sem(f"cn_lo_{l}"), 1)
                advance(6)
                qk_norm(l, 0)
                attention(l, 0)
                advance(2 * KT)
                qk_norm(l, 1)
                attention(l, 1)
                for og in range(2):
                    for n in range(NBR):
                        advance(KT)
                        advance(BW // 128)
                        g = plan[l, "branch", og, n][1]
                        src = ps[:, g % 2 * 4:g % 2 * 4 + 4, 0:T - cq]
                        dve.wait_ge(unit_used, ends[g])
                        dve.wait_ge(*freed(g - 1))
                        if n == 0:
                            if og:
                                dve.wait_ge(sem(f"g_hi_{l}"), og)
                                dve.wait_ge(sem(f"g_{l}"), og)
                            V.tensor_tensor(mg[:, :, 0:T - cq], src, sg[:, :, 0:T - cq],
                                            ALU.mult).then_inc(banks_free[g % 2], 1)
                            dve.wait_ge(*freed(g))
                        else:
                            V.tensor_tensor(mtmp[:, :, 0:T - cq], src, sg[:, :, 0:T - cq],
                                            ALU.mult).then_inc(banks_free[g % 2], 1)
                            dve.wait_ge(*freed(g))
                            link(V.tensor_tensor(mg[:, :, 0:T - cq], mg[:, :, 0:T - cq], mtmp[:, :, 0:T - cq], ALU.add),
                                 f"mg_{l}" if n == NBR - 1 else None)
                    dve.wait_ge(sem(f"g_hi_{l}"), og + 1)
                    V.tensor_tensor(g_lo[:, og * 4:og * 4 + 4, 0:T - cq], mg[:, :, 0:T - cq],
                                    g_hi[:, og * 4:og * 4 + 4, 0:T - cq].bitcast(fp32),
                                    ALU.subtract).then_inc(sem(f"g_{l}"), 1)
                for m in range(2):
                    advance(KT)
                    residual(l, m, plan[l, "wout"][1], cq, 5)
                norm(l, 2)
                ffn(l, 1)

        @block.tensor
        def _(pe):
            M = nc.tensor.matmul
            TR = nc.tensor.transpose

            def all_free(g):
                for b in (g - 1, g - 2):
                    if b >= 0:
                        pe.wait_ge(*freed(b))

            def banks(g, it=None, per=0):
                if g >= 2:
                    v = g // 2
                    pe.wait_ge(banks_free[g % 2], v if it is None else v + it * per)
                return g % 2 * 4

            def ready(u, it=None, per=0):
                pe.wait_ge(lo_done, u + 1 if it is None else u + 1 + it * per)
                return u % RING

            def passes(dst, pairs, first, final, **kw_):
                for i, (a, b) in enumerate(pairs):
                    ins = M(dst, a, b, start=first and i == 0, stop=final and i == len(pairs) - 1, **kw_)
                return ins

            def three(w, r):
                return ((w[0], r[0]), (w[0], r[1]), (w[1], r[0]))

            def weight(slot, a, b):
                return w_hi[:, slot, a:b], w_lo[:, slot, a:b]

            def tiles4(b0, slot, rhs, n, first, final, count=4, width=128):
                for m in range(count):
                    ins = passes(ps[0:width, b0 + m, 0:n], three(weight(slot, m * width, (m + 1) * width), rhs),
                                 first, final)
                return ins

            def h_rhs(k, c0):
                return h_hi[:, k, c0:T], h_lo[:, k, c0:T]

            def feature_group(key, g, c0, norm_no=None, count=4):
                u0 = plan[key][0]
                b0 = banks(g)
                for k in range(KT):
                    if norm_no is not None:
                        pe.wait_ge(sem("h"), KT * norm_no + k + 1)
                    ins = tiles4(b0, ready(u0 + k), h_rhs(k, c0), T - c0, k == 0, k == KT - 1, count)
                    if k < KT - 1 or key[1] == "cqkv":
                        ins.then_inc(unit_used, 1)
                return ins

            def norm_stats(l, j, g):
                m_ = 3 * l + j
                c0 = first_col(l, j == 2)
                all_free(g)
                pe.wait_ge(sem("sq_added"), (KT - 1) * (m_ + 1))
                M(ps[:, 0, c0:T], tb("ones"), acc[:, c0:T], start=True, stop=True).then_inc(sem("ss"), 1)
                pe.wait_ge(sem("rms"), m_ + 1)

            def ffn(l, f):
                done = FT // 2 * (2 * l + f)
                c0 = first_col(l, f == 1)
                n = T - c0
                u0, g0 = plan[l, "in", f]

                def group(b, first, it=None):
                    b0 = banks(g0 + b, it, 1)
                    for k in range(KT):
                        if first:
                            pe.wait_ge(sem("h"), KT * (3 * l + 2 * f) + k + 1)
                        slot = ready(u0 + b * KT + k, it, 2 * KT)
                        ins = tiles4(b0, slot, h_rhs(k, c0), n, k == 0, k == KT - 1)
                        if k < KT - 1:
                            ins.then_inc(unit_used, 1)
                    finish(ins, g0 + b)

                group(0, True)
                with pe.Fori(0, FT // 4) as i:
                    for b in (1, 2):
                        group(b, False, i)
                u0, g0 = plan[l, "out", f]
                for g in range(2):
                    b0 = banks(g0 + g)
                    u = u0 + g * FT
                    if g == 0:
                        pe.wait_ge(sem("mid"), done + FT // 2)

                    def unit(slot, rhs, first, final):
                        return tiles4(b0, slot, rhs, n, first, final)

                    unit(ready(u), (mid_hi[:, 0, 0:n], mid_lo[:, 0, 0:n]), True, False).then_inc(unit_used, 1)
                    loops = (FT - 2) // RING
                    with pe.Fori(0, loops) as i:
                        for j in range(RING):
                            slot = ready(u + 1 + j, i, RING)
                            kk = bass.ds(i * RING + (1 + j), 1)
                            unit(slot, (mid_hi[:, kk, 0:n], mid_lo[:, kk, 0:n]), False, False).then_inc(unit_used, 1)
                    ins = unit(ready(u + FT - 1), (mid_hi[:, FT - 1, 0:n], mid_lo[:, FT - 1, 0:n]), False, True)
                    finish(ins, g0 + g)

            def qk_norm_attend(l, a, g_next):
                P, xn, co, si, cos, tiles = rope_setup(l, a)
                nsq = scr[a][0]
                pb, pt, ob = scr[a][5:8]
                tb_, ib_ = before(l, a)
                ones_, rot = (tb("ones")[0:P, 0:P], tb("rotm")) if a == 0 else (tb("ones64"), tb("rotg"))
                all_free(g_next)

                def squares(i):
                    c0 = tiles[i][1]
                    pe.wait_ge(sem("qsq"), tb_ + i + 1)
                    if i >= 2:
                        pe.wait_ge(sem("qrms"), tb_ + i - 1)
                    M(ps[0:P, i % 2, c0:T], ones_, nsq[0:P, i % 2, c0:T], start=True, stop=True)\
                        .then_inc(sem("qss"), 1)

                squares(0)
                for i in range(len(tiles)):
                    if i + 1 < len(tiles):
                        squares(i + 1)
                    c0 = tiles[i][1]
                    pe.wait_ge(sem("qn"), tb_ + i + 1)
                    if i >= 2:
                        pe.wait_ge(sem("qsin"), tb_ + i - 1)
                    M(ps[0:P, 2 + i % 2, c0:T], rot, xn[0:P, i % 2, c0:T], start=True, stop=True)\
                        .then_inc(sem("qrot"), 1)
                pe.wait_ge(sem("qk_final"), tb_ + len(tiles))

                its = items(l)

                def scores(i):
                    qt, h = its[i]
                    n = key_tiles(qt) * 128
                    if i >= 3:
                        pe.wait_ge(sem("aexp"), ib_ + i - 2)
                    cols = slice(qt * 128, (qt + 1) * 128)
                    if a == 0:
                        q_, k_ = q96[:, h, cols], k96[:, h, 0:n]
                    else:
                        r = slice(64 * (h % 2), 64 * (h % 2) + 64)
                        q_, k_ = qg[r, h // 2, cols], kg[r, h // 4, 0:n]
                    M(ps[:, i % 3, 0:n], q_, k_, start=True, stop=True).then_inc(sem("asc"), 1)

                def turned(i):
                    pe.wait_ge(sem("aexp"), ib_ + i + 1)
                    if i >= 2:
                        pe.wait_ge(sem("apt"), ib_ + i - 1)
                    for kt in range(key_tiles(its[i][0])):
                        c = slice(kt * 128, (kt + 1) * 128)
                        ins = TR(ps[:, 3 + i % 2, c], pb[:, i % 2, c], ident)
                    ins.then_inc(sem("atr"), 1)

                def values(i):
                    qt, h = its[i]
                    n = i // 8
                    pe.wait_ge(sem("apt"), ib_ + i + 1)
                    if h == 0 and n >= 2:
                        pe.wait_ge(sem("aob"), ib_ // 8 + n - 1)
                    for kt in range(key_tiles(qt)):
                        v = vm[:, kt, h * AV:(h + 1) * AV] if a == 0 else vg[:, kt, h // 4 * GD:(h // 4 + 1) * GD]
                        ins = M(ps[:, 5 + n % 2, h * 64:(h + 1) * 64], pt[:, i % 2, kt, :], v, start=kt == 0,
                                stop=kt == key_tiles(qt) - 1)
                    ins.then_inc(sem("apv"), 1)

                def turn_output(n):
                    pe.wait_ge(sem("aob"), ib_ // 8 + n + 1)
                    if n >= 1:
                        pe.wait_ge(sem("ay"), ib_ // 8 + n)
                    for q in range(4):
                        ins = TR(ps[:, 7, q * 128:(q + 1) * 128],
                                 ob[:, 2 * q:2 * q + 2, :].rearrange("p h e -> p (h e)"), ident)
                    ins.then_inc(sem("aot"), 1)

                scores(0)
                scores(1)
                for i, (qt, h) in enumerate(its):
                    if i + 2 < len(its):
                        scores(i + 2)
                    turned(i)
                    if i:
                        values(i - 1)
                    if h == 1 and i >= 8:
                        turn_output(i // 8 - 1)
                values(len(its) - 1)
                turn_output(len(its) // 8 - 1)
                pe.wait_ge(sem("ay"), ib_ // 8 + len(its) // 8)

            def finish(ins, g):
                ins.then_inc(unit_used, 1)

            pe.wait_ge(sem("tab_in"), 16)
            pe.wait_ge(sem("s_act"), 1)
            TR(ps[:, 0, 0:2 * KT], s_act[:, :], ident[0:2 * KT, 0:2 * KT]).then_inc(sem("x_t"), 1)
            pe.wait_ge(sem("x_in"), 16 * NT)
            for i in range(NT):
                b = 2 + 2 * (i % 2)
                if i >= 2:
                    pe.wait_ge(sem("x_ready"), i - 1)
                for k in range(KT):
                    ins = TR(ps[:, b + k // 4, k % 4 * 128:(k % 4 + 1) * 128], xin[:, i, k * 128:(k + 1) * 128], ident)
                ins.then_inc(sem("x_t"), 1)
            pe.wait_ge(sem("vectors_in"), 16 * VECTORS)
            for l in range(DEPTH):
                TR(ps[:, 6, l * P_ROWS:(l + 1) * P_ROWS], vrow[:, l, :], ident[0:P_ROWS, 0:P_ROWS])
                ins = TR(ps[:, 7, l * M_ROWS:(l + 1) * M_ROWS], mvrow[:, l, :], ident[0:M_ROWS, 0:M_ROWS])
            ins.then_inc(sem("vec_t"), 1)
            pe.wait_ge(sem("s4"), 1)
            pe.wait_ge(sem("x_ready"), NT)
            pe.wait_ge(sem("params"), 1)

            for l in range(DEPTH):
                cq = first_col(l, True)
                n_q = T - cq
                u0, g0 = plan[l, "mod"]

                def turn(b, j):
                    for q in range(4):
                        at = slice(j * 8 + 2 * q, j * 8 + 2 * q + 2) if isinstance(j, int) else bass.ds(j * 8 + 2 * q, 2)
                        ins = M(ps[:, 7, at], mrow[:, b, q * 128:(q + 1) * 128], tb("comb"),
                                start=True, stop=True)
                    return ins

                def mod_pair(u, g, j, it=None):
                    for b in range(2):
                        b0 = banks(g + b, it, 1)
                        for k in range(KT):
                            slot = ready(u + b * KT + k, it, 2 * KT)
                            M(ps[0:4, b0, :], s4[:, k, :], w_hi[:, slot, :], start=k == 0, stop=False)
                            M(ps[0:4, b0, :], s4[:, k, :], w_lo[:, slot, :], start=False,
                              stop=k == KT - 1).then_inc(unit_used, 1)
                    for b in range(2):
                        fs, fv = freed(g + b)
                        pe.wait_ge(fs, fv if it is None else fv + it)
                        turn(b, j + b).then_inc(sem("mod_t"), 1)

                all_free(g0)
                mod_pair(u0, g0, 0)
                with pe.Fori(0, 8) as i:
                    mod_pair(u0 + 2 * KT, g0 + 2, i * 2 + 2, i)
                norm_stats(l, 0, g0 + 18)
                ffn(l, 0)
                norm_stats(l, 1, plan[l, "q"][1])

                for name, c0 in (("q", cq), ("k", 0)):
                    g = plan[l, name][1]
                    finish(feature_group((l, name), g, c0, 3 * l + 1 if name == "q" else None), g)
                u0, g = plan[l, "v"]
                b0 = banks(g)
                for k in range(KT):
                    slot = ready(u0 + k)
                    for tt in range(NT):
                        c = slice(tt * 128, (tt + 1) * 128)
                        ins = passes(ps[:, b0 + tt, :], three((h_hi[:, k, c], h_lo[:, k, c]), weight(slot, 0, 512)),
                                     k == 0, k == KT - 1)
                    if k < KT - 1:
                        ins.then_inc(unit_used, 1)
                finish(ins, g)
                u0, g = plan[l, "cqkv"]
                b0 = banks(g)
                for k in range(KT):
                    slot = ready(u0 + k)
                    for m in range(3):
                        c0 = cq if m < 2 else 0
                        ins = passes(ps[:, b0 + m, 0:T - c0], three(weight(slot, m * 128, (m + 1) * 128), h_rhs(k, c0)),
                                     k == 0, k == KT - 1)
                    ins.then_inc(unit_used, 1)
                slot = ready(u0 + KT)
                for k in range(KT):
                    ins = passes(ps[0:ROPE, b0 + 3, :], three(weight(slot, k * ROPE, (k + 1) * ROPE), h_rhs(k, 0)),
                                 k == 0, k == KT - 1)
                finish(ins, g)
                u0, g = plan[l, "gates"]
                b0 = banks(g)
                slot = ready(u0)
                for k in range(KT):
                    ins = passes(ps[0:16, b0, :], three(weight(slot, k * 16, (k + 1) * 16), h_rhs(k, 0)),
                                 k == 0, k == KT - 1)
                finish(ins, g)

                all_free(plan[l, "o"][1])
                sel = tb("sel").rearrange("p (a n) -> p a n", n=36)
                back = gz[:, :].rearrange("p (s n) -> p s n", s=2)[:, :, ::-1]
                for b in range(2):
                    M(ps[0:36, b, :], sel[:, 2 * b, :], gz[:, :], start=True, stop=False)
                    ins = M(ps[0:36, b, :], sel[:, 2 * b + 1, :], back, start=False, stop=True)
                ins.then_inc(sem(f"sel_{l}"), 1)
                pe.wait_ge(sem(f"exprow_{l}"), 4)
                pe.wait_ge(sem(f"rown_{l}"), 2)
                for q in range(4):
                    for tt in range(NT):
                        TR(ps[:, 2 + q // 2, ((q % 2) * 4 + tt) * 36:((q % 2) * 4 + tt + 1) * 36],
                           RN[:, q, tt * 128:(tt + 1) * 128], ident[0:36, 0:36])
                for d in range(2):
                    for h in range(MH):
                        r = 32 * d + h
                        ins = M(ps[:, 4, (4 * d + h) * 4:(4 * d + h) * 4 + 4],
                                ident[0:36, r:r + 1].to_broadcast([36, 128]), dlog[:, :], start=True, stop=True)
                ins.then_inc(sem(f"tokt_{l}"), 1)

                t0 = cq // 128
                outs = [j for j in range(NT) if scan_tile(0, j) >= t0]
                pe.wait_ge(sem(f"tok_{l}"), 1)
                pe.wait_ge(sem(f"qk_{l}"), 2 * MH)
                for h in range(MH):
                    if h:
                        pe.wait_ge(sem(f"P_{l}"), 2 * h)
                        pe.wait_ge(sem(f"cupd_{l}"), 6 * h)
                        pe.wait_ge(sem(f"kw_{l}"), h)
                    q_h, k_h = qk[:, h, :], qk[:, MH + h, :]
                    for tt in range(t0, NT):
                        c = slice(tt * 128, (tt + 1) * 128)
                        M(ps[:, 0, c], k_h[:, c], q_h[:, c], start=True, stop=True)
                    for d in range(2):
                        r = 32 * d + h
                        M(ps[:, 1 + d, t0 * 128:], ident[0:36, r:r + 1].to_broadcast([36, 128]), RN[:, 4, t0 * 128:],
                          start=True, stop=True)
                    for tt in range(NT):
                        c = slice(tt * 128, (tt + 1) * 128)
                        ins = TR(ps[:, 3, c], k_h[:, c], ident)
                    ins.then_inc(sem(f"headmm_{l}"), 1)
                    pe.wait_ge(sem(f"P_{l}"), 2 * h + 2)
                    pe.wait_ge(sem(f"kw_{l}"), h + 1)
                    for j in range(NT):
                        for d in range(2):
                            tt = scan_tile(d, j)
                            c = slice(tt * 128, (tt + 1) * 128)
                            if j >= 1:
                                pe.wait_ge(sem(f"cupd_{l}"), 2 * (3 * h + j - 1) + d + 1)
                            if j in outs:
                                n = 2 * (len(outs) * h + outs.index(j)) + d
                                if n >= 2:
                                    pe.wait_ge(sem(f"hn_{l}"), n - 1)
                                ins = M(ps[:, 4 + d, 0:MD + 1], P_[:, d, tt, :], vaug[:, tt, h, :], start=True, stop=True)
                                if j >= 1:
                                    ins = M(ps[:, 6 + d, 0:MD + 1], q_h[:, c], C_[:, d, :], start=True, stop=True)
                                ins.then_inc(sem(f"nmm_{l}"), 1)
                            if j < NT - 1:
                                M(ps[:, 1 + d, 0:MD + 1], kw[:, d, tt, :], vaug[:, tt, h, :],
                                  start=True, stop=True).then_inc(sem(f"dcmm_{l}"), 1)
                pe.wait_ge(sem(f"hn_{l}"), 2 * len(outs) * MH)
                pe.wait_ge(sem(f"hout_{l}"), MH)
                g = plan[l, "o"][1]
                finish(feature_group((l, "o"), g, cq), g)
                for h in range(MH):
                    for tt in range(t0, NT):
                        ins = TR(ps[:, y0_bank(l, h), tt * 128:(tt + 1) * 128], hsn[:, h, tt, :], ident)
                    ins.then_inc(sem(f"ht_{l}"), 1)

                pe.wait_ge(sem(f"y0_{l}"), MH)
                pe.wait_ge(sem(f"csq_{l}"), 1)
                all_free(plan[l, "uq", 0][1])
                M(ps[:, 0, cq:T], tb("ones"), csq[:, 0, cq:T], start=True, stop=False)
                M(ps[:, 0, cq:T], tb("ones"), csq[:, 1, cq:T], start=False, stop=True)
                M(ps[:, 1, :], tb("ones"), csq[:, 2, :], start=True, stop=True).then_inc(sem(f"css_{l}"), 1)
                pe.wait_ge(sem(f"cn_lo_{l}"), 1)
                for half in range(2):
                    u0, g = plan[l, "uq", half]
                    b0 = banks(g)
                    for k in range(2):
                        ins = tiles4(b0, ready(u0 + k), (cn_hi[:, k, cq:T], cn_lo[:, k, cq:T]), n_q, k == 0, k == 1,
                                     4, AQK)
                        if k == 0:
                            ins.then_inc(unit_used, 1)
                    finish(ins, g)
                u0, g = plan[l, "kn"]
                b0 = banks(g)
                finish(tiles4(b0, ready(u0), (cn_hi[:, 2, :], cn_lo[:, 2, :]), T, True, True), g)
                u0, g = plan[l, "kv"]
                b0 = banks(g)
                slot = ready(u0)
                for tt in range(NT):
                    c = slice(tt * 128, (tt + 1) * 128)
                    ins = passes(ps[:, b0 + tt, :], three((cn_hi[:, 2, c], cn_lo[:, 2, c]), weight(slot, 0, 512)),
                                 True, True)
                finish(ins, g)
                qk_norm_attend(l, 0, plan[l, "gq"][1])

                g = plan[l, "gq"][1]
                finish(feature_group((l, "gq"), g, cq), g)
                u0, g = plan[l, "gkv"]
                b0 = banks(g)
                for k in range(KT):
                    slot = ready(u0 + k)
                    passes(ps[:, b0, :], three(weight(slot, 0, 128), h_rhs(k, 0)), k == 0, k == KT - 1)
                    for tt in range(NT):
                        c = slice(tt * 128, (tt + 1) * 128)
                        ins = passes(ps[:, b0 + 1, c], three((h_hi[:, k, c], h_lo[:, k, c]), weight(slot, 128, 256)),
                                     k == 0 and tt == 0, k == KT - 1, skip_group_check=True)
                    if k < KT - 1:
                        ins.then_inc(unit_used, 1)
                finish(ins, g)
                qk_norm_attend(l, 1, g + 1)

                pe.wait_ge(sem("ay"), before(l, 1)[1] // 8 + len(items(l)) // 8)
                for og in range(2):
                    for n in range(NBR):
                        g = plan[l, "gate", og, n][1]
                        finish(feature_group((l, "gate", og, n), g, cq), g)
                        u0, g = plan[l, "branch", og, n]
                        b0 = banks(g)
                        for k in range(BW // 128):
                            ins = tiles4(b0, ready(u0 + k), (y_hi[n][:, k, cq:T], y_lo[n][:, k, cq:T]), n_q,
                                         k == 0, k == BW // 128 - 1)
                            if k < BW // 128 - 1:
                                ins.then_inc(unit_used, 1)
                        finish(ins, g)
                u0, g0 = plan[l, "wout"]
                for og in range(2):
                    b0 = banks(g0 + og)
                    for k in range(KT):
                        if og == 0:
                            pe.wait_ge(sem(f"g_{l}"), k // 4 + 1)
                        ins = tiles4(b0, ready(u0 + og * KT + k), (g_hi[:, k, 0:n_q], g_lo[:, k, 0:n_q]), n_q,
                                     k == 0, k == KT - 1)
                        if k < KT - 1:
                            ins.then_inc(unit_used, 1)
                    finish(ins, g0 + og)
                norm_stats(l, 2, plan[l, "in", 1][1])
                ffn(l, 1)
            all_free(plan["end"][1])
            for i in range(2):
                for k in range(KT):
                    ins = TR(ps[:, 2 * i + k // 4, k % 4 * 128:(k % 4 + 1) * 128],
                             x[:, k, CTX + i * 128:CTX + (i + 1) * 128], ident)
                ins.then_inc(sem("out_t"), 1)





_INS = ["x", "c", "ctx", "c_ctx", "w_mod", "b_mod", "g_norm", "w_ffn_in", "w_ffn_out", "w_in", "b_mgate", "w_conv",
        "g_mhead", "g_cq", "g_ckv", "w_uq", "w_ukv", "g_q_mla", "g_k_mla", "g_q_gqa", "g_k_gqa", "w_branch", "w_out"]


def kernel(**inputs):
    import concourse.bacc as bacc
    from concourse.bass_utils import run_bass_kernel_spmd

    nc = bacc.Bacc("TRN2", target_bir_lowering=False, num_devices=1)
    arrays, t = {}, {}
    table, tab_at = tables()
    for name, a in [(n, np.ascontiguousarray(inputs[n])) for n in _INS] + [("tab", table)]:
        arrays[f"in_{name}"] = a
        t[name] = nc.dram_tensor(f"in_{name}", a.shape, mybir.dt.from_np(a.dtype), kind="ExternalInput").ap()
    out = nc.dram_tensor("out", (1, T - CTX, D), mybir.dt.float32, kind="ExternalOutput").ap()
    build(nc, t, out, tab_at)
    r = run_bass_kernel_spmd(nc, [arrays], core_ids=[0])
    return r.results[0]["out"]
```

```python
from contextlib import ExitStack

import concourse.bass as bass
import numpy as np
from concourse import mybir

D, T, DEPTH = 1024, 512, 2
CTX = 256
KT = D // 128
DFF = 2816
FT = DFF // 128
MH, MD, MW = 4, 128, 512
TAPS = 5
NT = T // 128
QR, KVR = 256, 128
AH, NOPE, ROPE, AV = 8, 64, 32, 64
AQK = NOPE + ROPE
GH, GKV, GD = 8, 2, 64
NBR, BW = 3, 512
EPS = 1e-6
THETA = 10000.0
GRID_W = 64
RING = 4
LOADS = 8
UNIT = 512
FILL = 0
AB = 4 * (1 - FILL)
NEG = -1e30
STATS = 2 * AH
CQ_, CK_, CV_, CO_ = 0, 512, 1024, 1536
CGATE = 2048
CCQ = CGATE + 4 * MH
CCKV = CCQ + QR
CKR = CCKV + KVR
CGQ = CKR + ROPE
CGK = CGQ + GH * GD
CGV = CGK + GKV * GD
CBG = CGV + GKV * GD
P_NORM, P_CONV = 0, 3 * KT
P_MH = P_CONV + TAPS * 2 * MH
P_CQ = P_MH + MH
P_CKV = P_CQ + QR // 128
P_QG, P_KG, P_QM, P_KM = P_CKV + 1, P_CKV + 2, P_CKV + 3, P_CKV + 4
P_ROWS = P_KM + 1
M_ROWS = 9 * KT
VECTORS = DEPTH * (5 + 6 + 1 + 4)


def tables():
    def rope(dim):
        quarter = dim // 4
        inv = np.float32(THETA) ** (-np.arange(quarter, dtype=np.float32) / np.float32(quarter))
        t = np.arange(T - CTX)
        rows, cols = (t // GRID_W).astype(np.float32), (t % GRID_W).astype(np.float32)
        ang = np.concatenate([rows[:, None] * inv, cols[:, None] * inv], -1).astype(np.float32)
        return np.cos(ang).T, np.sin(ang).T

    def full(dim, head, copies):
        c, s = rope(dim)
        half = dim // 2
        cos, sin = np.ones((head, T - CTX), np.float32), np.zeros((head, T - CTX), np.float32)
        cos[head - dim:] = np.concatenate([c, c])
        sin[head - dim:] = np.concatenate([s, s])
        rot = np.zeros((head, head), np.float32)
        for i in range(half):
            a, b = head - dim + i, head - half + i
            rot[b, a] = -1.0
            rot[a, b] = 1.0
        return (np.tile(cos, (copies, 1)), np.tile(sin, (copies, 1)),
                np.kron(np.eye(copies, dtype=np.float32), rot))

    parts = {}
    parts["ident"] = np.eye(128, dtype=np.float32)
    s, t = np.arange(128)[:, None], np.arange(128)[None, :]
    parts["mask"] = np.concatenate([np.where(s <= t, 0.0, NEG), np.where(s >= t, 0.0, NEG)], 1)
    parts["ones"] = np.ones((128, 128))
    parts["sum1"], parts["sum2"] = np.zeros((128, 2 * STATS - 1)), np.zeros((128, 2 * STATS - 2))
    parts["sum1"][:, STATS - 1] = 1
    parts["sum2"][0:64, STATS - 2] = parts["sum2"][64:128, STATS - 1] = 1
    parts["spread"] = np.kron(np.eye(GH + 2 * GKV), np.ones((1, GD)))
    parts["cosg"], parts["sing"], parts["rotg"] = full(GD, GD, 2)
    parts["cosm"], parts["sinm"], parts["rotm"] = full(ROPE, AQK, 1)
    sel = np.zeros((16, 4, 36))
    for h in range(MH):
        sel[h, 0, h] = sel[2 * MH + h, 1, 32 + h] = 1
        sel[MH + h, 2, h] = sel[3 * MH + h, 3, 32 + h] = 1
    parts["sel"] = sel.reshape(16, -1)
    parts["comb"] = np.array([[1, 0], [0, 1], [1, 0], [0, 1]])
    at, width = {}, 0
    for name, a in parts.items():
        at[name] = (width, a.shape[0], a.shape[1])
        width += a.shape[1]
    out = np.zeros((128, width), np.float32)
    for name, a in parts.items():
        w, r, c = at[name]
        out[:r, w:w + c] = a
    return out, at


def make_plan():
    plan, size, ends, place = {}, [], [], []

    def add(key, units, n_groups=1, width=UNIT, where=None):
        plan[key] = (len(size), len(ends))
        for _ in range(n_groups):
            size.extend([width] * (units // n_groups))
            ends.append(len(size))
            half = where if where is not None else 1 - place[-1][0] if place else 0
            place.append((half, sum(p[0] == half for p in place)))

    def merge(l, n, where=None):
        for og in range(2):
            add((l, "gate", og, n), KT, where=where)
            add((l, "branch", og, n), BW // 128, where=where)

    for l in range(DEPTH):
        add((l, "mod"), 18 * KT, 18)
        add((l, "in", 0), FT // 2 * KT, FT // 2)
        add((l, "out", 0), 2 * FT, 2)
        for name in ("q", "k", "v"):
            add((l, name), KT)
        add((l, "cqkv"), KT, 1, QR + KVR)
        size.append(KT * ROPE)
        ends[-1] += 1
        add((l, "gates"), 1, 1, KT * 4 * MH)
        add((l, "o"), KT)
        add((l, "uq", 0), 2, 1, 4 * AQK)
        add((l, "uq", 1), 2, 1, 4 * AQK)
        add((l, "kn"), 1)
        add((l, "kv"), 1)
        merge(l, 0, FILL)
        add((l, "gq"), KT)
        add((l, "gkv"), KT, 1, 2 * GKV * GD)
        merge(l, 1, FILL)
        merge(l, 2)
        add((l, "wout"), 2 * KT, 2)
        add((l, "in", 1), FT // 2 * KT, FT // 2)
        add((l, "out", 1), 2 * FT, 2)
    plan["end"] = (len(size), len(ends))
    return plan, size, ends, place


MERGE = [(og, name, k) for og in range(2)
         for name, units in (("gate", KT), ("gates out", 1), ("branch", BW // 128), ("branch out", 1))
         for k in range(units)]


def has_unit(step):
    return 0 <= step < len(MERGE) and "out" not in MERGE[step][1]


def build(nc, t, out, tab_at):
    fp32, f32r = mybir.dt.float32, mybir.dt.float32r
    ALU, ACT, AX = mybir.AluOpType, mybir.ActivationFunctionType, mybir.AxisListType
    plan, size, ends, place = make_plan()
    U = len(size)
    ctx = ExitStack()

    with ctx:
        def sb(name, shape, dt=fp32, where=ctx):
            return where.enter_context(nc.sbuf_tensor(name, shape, dt))

        sems = {}

        def sem(name):
            if name not in sems:
                sems[name] = ctx.enter_context(nc.semaphore(name))
            return sems[name]

        x = sb("x", [128, KT, T])
        h_hi = sb("h_hi", [128, KT, T], f32r)
        h_lo = sb("h_lo", [128, KT, T], f32r)
        w_raw = sb("w_raw", [128, LOADS, UNIT])
        w_hi = sb("w_hi", [128, RING, UNIT], f32r)
        w_lo = sb("w_lo", [128, RING, UNIT], f32r)
        tab = sb("tab", [128, t["tab"].shape[1]])
        cst = sb("cst", [128, 3])
        prm = sb("prm", [128, DEPTH, P_ROWS])
        bmod = sb("bmod", [128, DEPTH, M_ROWS])
        bgate = sb("bgate", [36, DEPTH, 2])
        mod = sb("mod", [128, 9, KT, 2])
        gain = sb("gain", [128, 3, KT, 2])
        s_in = sb("s_in", [2 * KT, 128])
        s_act = sb("s_act", [2 * KT, 128])
        s_fm = sb("s_fm", [128, 2 * KT])
        s4 = sb("s4", [128, KT, 4], f32r)

        y0h = y0l = None
        big = ExitStack()

        def region(stack, specs):
            return [sb(n, s, d, stack) for n, s, d in specs]

        sq, acc, rms, t1, hn, mid_hi, mid_lo = region(big, [
            ("sq", [128, 2, T], fp32), ("acc", [128, T], fp32), ("rms", [128, T], fp32),
            ("t1", [128, 2, T], fp32), ("hn", [128, 2, T], fp32),
            ("mid_hi", [128, FT, T], f32r), ("mid_lo", [128, FT, T], f32r)])
        sil, mt, mrow = sq, t1, hn
        big.close()
        big = ExitStack()
        xin, vrow, mvrow = region(big, [("xin", [128, NT, D], fp32), ("vrow", [P_ROWS, DEPTH, 128], fp32),
                                        ("mvrow", [M_ROWS, DEPTH, 128], fp32)])
        big.close()
        big = ExitStack()
        xout, = region(big, [("xout", [128, 2, D], fp32)])
        big.close()
        mix = ExitStack()
        y_hi, y_lo = [None] * 3, [None] * 3
        y_hi[0], y_lo[0], craw, krs = region(mix, [("y0h", [128, MH, T], f32r), ("y0l", [128, MH, T], f32r),
                                                   ("craw", [128, 3, T], fp32), ("krs", [128, T], fp32)])
        s1 = ExitStack()
        qk, vaug, R, RN, tok, hsn, dec, mprev, dlog = region(s1, [
            ("qk", [128, 2 * MH, T], fp32), ("vaug", [128, NT, MH, MD + 1], fp32),
            ("R", [36, 6, T], fp32), ("RN", [36, 5, T], fp32), ("tok", [128, 16, 36], fp32),
            ("hsn", [128, MH, NT, MD], fp32), ("dec", [128, 8, 4], fp32), ("mprev", [36, 5], fp32),
            ("dlog", [36, 4], fp32)])
        s2 = ExitStack()
        cpad, cacc, gz = region(s2, [("cpad", [128, 4, 2, CTX + 4], fp32), ("cacc", [128, 2, 2, CTX], fp32),
                                     ("gz", [16, T], fp32)])
        s2.close()
        s2 = ExitStack()
        dt_, P_, kw, HN, an, C_, sqt, dn, rn = region(s2, [
            ("dt_", [128, 2, NT, 128], fp32), ("P_", [128, 2, NT, 128], fp32), ("kw", [128, 2, NT, 128], fp32),
            ("HN", [128, 2, NT, MD + 1], fp32), ("an", [128, 2, MD + 1], fp32), ("C_", [128, 2, MD + 1], fp32),
            ("sqt", [128, NT, MD], fp32), ("dn", [128, 2, 4], fp32), ("rn", [128, 4], fp32)])
        s2.close()
        s2 = ExitStack()
        sigo, yt = region(s2, [("sigo", [128, MH, T], fp32), ("yt", [128, 2, T], fp32)])
        s2.close()
        s1.close()
        y_hi[1], y_lo[1] = region(mix, [("y1h", [128, 4, T], f32r), ("y1l", [128, 4, T], f32r)])
        s1 = ExitStack()
        cn_hi, cn_lo, cn, csq, crm = region(s1, [
            ("cn_hi", [128, 3, T], f32r), ("cn_lo", [128, 3, T], f32r), ("cn", [128, 3, T], fp32),
            ("csq", [128, 3, T], fp32), ("crm", [128, 2, T], fp32)])
        s1.close()
        mg, sg = region(mix, [("mg", [128, KT, T], fp32), ("sg", [128, 4, T], fp32)])

        def attention_scratch(stack, k):
            two = ExitStack()
            nsq, nrm = region(two, [(f"nsq{k}", [128, 2, T], fp32), (f"nrm{k}", [STATS, T], fp32)])
            two.close()
            rotated = [craw[:, i, :].rearrange("p (a n) -> p a n", a=2) for i in range(3)]
            pb, pt, mx, rs = region(stack, [
                (f"pb{k}", [128, 2, T], fp32), (f"pt{k}", [128, 2, NT, 128], fp32),
                (f"mx{k}", [128, 2, 2], fp32), (f"rs{k}", [128, 2, 8], fp32)])
            ob = krs[:, :].rearrange("p (h e) -> p h e", h=8)
            return [nsq, nrm, *rotated, pb, pt, ob, mx, rs]

        s1 = ExitStack()
        q96, k96, vm = region(s1, [("q96", [AQK, AH, T], fp32), ("k96", [AQK, AH, T], fp32),
                                   ("vm", [128, NT, AH * AV], fp32)])
        scr = [attention_scratch(s1, 0)]
        s1.close()
        s1 = ExitStack()
        y_hi[2], y_lo[2] = region(mix, [("y2h", [128, 4, T], f32r), ("y2l", [128, 4, T], f32r)])
        qg, kg, vg = region(s1, [("qg", [128, 4, T], fp32), ("kg", [128, GKV, T], fp32), ("vg", [128, NT, 128], fp32)])
        scr.append(attention_scratch(s1, 1))
        s1.close()
        s1 = ExitStack()
        g_hi, g_lo = region(s1, [("g_hi", [128, KT, T], f32r), ("g_lo", [128, KT, T], f32r)])
        s1.close()
        mix.close()

        ps = ctx.enter_context(nc.psum_tensor("ps", [128, 8, 512], fp32))

        def tb(name, rows=None):
            w, r, c = tab_at[name]
            return tab[0:r, w:w + c]

        ident = tb("ident")

        landed = [sem(f"landed{i}") for i in range(LOADS)]
        hi_done, lo_done = sem("hi_done"), sem("lo_done")
        unit_used = sem("unit_used")
        banks_free = [sem("banks_free0"), sem("banks_free1")]

        def freed(g):
            return banks_free[place[g][0]], place[g][1] + 1

        def bank(g):
            return 4 * place[g][0]

        def last_groups(g):
            return [max(b for b in range(g) if place[b][0] == half) for half in range(2)
                    if any(place[b][0] == half for b in range(g))]

        def first_col(l, only_latent):
            return CTX if l == DEPTH - 1 and only_latent else 0

        def streams(c0):
            return [(s, a, b) for s, a, b in ((1, 0, CTX), (0, CTX, T)) if a >= c0]

        class Chain:

            def __init__(self, eng, name):
                self.eng, self.order, self.counts = eng, sem(name), {}

            def __call__(self, ins, name=None):
                s = sem(name) if name else self.order
                key = name or "order"
                self.counts[key] = self.counts.get(key, 0) + 1
                ins.then_inc(s, 1)
                self.eng.wait_ge(s, self.counts[key])

        def scan_tile(d, j):
            return j if d == 0 else (1, 0, 3, 2)[j]

        def rope_setup(l, a):
            nsq, nrm, nxn, nco, nsi = scr[a][:5]
            cq = first_col(l, True)
            if a == 0:
                tiles = [(k96[:, h, :], 0, P_KM) for h in range(AH)] + [(q96[:, h, :], cq, P_QM) for h in range(AH)]
                return AQK, nxn, nco, nsi, tb("cosm"), tiles
            tiles = [(kg[:, i, :], 0, P_KG) for i in range(GKV)] + [(qg[:, i, :], cq, P_QG) for i in range(4)]
            return 128, nxn, nco, nsi, tb("cosg"), tiles

        def items(l):
            return [(qt, h) for qt in range(first_col(l, True) // 128, NT) for h in range(8)]

        def before(l, a):
            tiles = l * (2 * AH + 4 + GKV) + a * 2 * AH
            return tiles, sum(2 * len(items(p)) for p in range(l)) + a * len(items(l))

        def key_tiles(qt):
            return 2 if qt < 2 else NT

        def y0_bank(l, h):
            return 4 - bank(plan[l, "o"][1]) + h

        block = ctx.enter_context(nc.Block())

        @block.sync
        def _(sp):
            sp.dma_start(tab[:, :], t["tab"]).then_inc(sem("tab_in"), 16)
            sp.dma_start(s_in[0:KT, :], t["c"].rearrange("b (k p) -> (b k) p", p=128)).then_inc(sem("s_in"), 16)
            sp.dma_start(s_in[KT:2 * KT, :], t["c_ctx"].rearrange("(k p) -> k p", p=128)).then_inc(sem("s_in"), 16)

            def unit(u, src, shape=None, it=None, per=0):
                if u >= LOADS:
                    need = u - LOADS + 1
                    sp.wait_ge(lo_done, need if it is None else need + it * per)
                n = size[u]
                dst = w_raw[:, u % LOADS, 0:n]
                if shape:
                    dst = dst.rearrange(shape[0], **shape[1])
                sp.dma_start(dst, src).then_inc(landed[u % LOADS], 16)

            def ffn_loads(l, f):
                u0, _ = plan[l, "in", f]
                w = t["w_ffn_in"][l, f].rearrange("k (s n) -> k s n", s=2)
                with sp.Fori(0, FT // 2) as g:
                    for k in range(KT):
                        unit(u0 + k, w[k * 128:(k + 1) * 128, :, bass.ds(g * 256, 256)],
                             ("p (s n) -> p s n", {"s": 2}), g, KT)
                u0, _ = plan[l, "out", f]
                w = t["w_ffn_out"][l, f].rearrange("(k p) n -> p k n", p=128)
                for g in range(2):
                    u = u0 + g * FT
                    cols = slice(g * 512, g * 512 + 512)
                    loops = FT // LOADS
                    with sp.Fori(0, loops) as i:
                        for j in range(LOADS):
                            unit(u + j, w[:, bass.ds(i * LOADS + j, 1), cols], ("p (a n) -> p a n", {"a": 1}), i, LOADS)
                    for k in range(loops * LOADS, FT):
                        unit(u + k, w[:, k, cols])

            def in_units(l, key, col, width, **kw_):
                u0, _ = plan[(l,) + key]
                for k in range(KT):
                    unit(u0 + k, t["w_in"][l, k * 128:(k + 1) * 128, col:col + width], **kw_)

            def merge_loads(l, n):
                for og in range(2):
                    in_units(l, ("gate", og, n), CBG + n * D + og * 512, 512)
                    for k in range(BW // 128):
                        unit(plan[l, "branch", og, n][0] + k,
                             t["w_branch"][l, n, k * 128:(k + 1) * 128, og * 512:og * 512 + 512])

            for l in range(DEPTH):
                u0, _ = plan[l, "mod"]
                for k in range(KT):
                    unit(u0 + k, t["w_mod"][l, k * 128:(k + 1) * 128, 0:512])
                with sp.Fori(0, 17) as g:
                    for k in range(KT):
                        unit(u0 + KT + k, t["w_mod"][l, k * 128:(k + 1) * 128, bass.ds(g * 512 + 512, 512)],
                             None, g, KT)
                ffn_loads(l, 0)
                in_units(l, ("q",), CQ_, 512)
                in_units(l, ("k",), CK_, 512)
                in_units(l, ("v",), CV_, 512)
                in_units(l, ("cqkv",), CCQ, QR + KVR)
                by_k = t["w_in"][l].rearrange("(k p) n -> p k n", p=128)
                unit(plan[l, "cqkv"][0] + KT, by_k[:, :, CKR:CKR + ROPE], ("p (k n) -> p k n", {"k": KT}))
                unit(plan[l, "gates"][0], by_k[:, :, CGATE:CGATE + 4 * MH], ("p (k n) -> p k n", {"k": KT}))
                in_units(l, ("o",), CO_, 512)
                for half in range(2):
                    for k in range(2):
                        unit(plan[l, "uq", half][0] + k,
                             t["w_uq"][l, k * 128:(k + 1) * 128, half * 4 * AQK:(half + 1) * 4 * AQK])
                kvw = t["w_ukv"][l].rearrange("k (h s e) -> k s h e", h=AH, s=2)
                unit(plan[l, "kn"][0], kvw[:, 0], ("p (h e) -> p h e", {"h": AH}))
                unit(plan[l, "kv"][0], kvw[:, 1], ("p (h e) -> p h e", {"h": AH}))
                merge_loads(l, 0)
                in_units(l, ("gq",), CGQ, 512)
                in_units(l, ("gkv",), CGK, 2 * GKV * GD)
                merge_loads(l, 1)
                merge_loads(l, 2)
                for og in range(2):
                    for k in range(KT):
                        unit(plan[l, "wout"][0] + og * KT + k,
                             t["w_out"][l, k * 128:(k + 1) * 128, og * 512:og * 512 + 512])
                ffn_loads(l, 1)
            for i in range(2):
                sp.wait_ge(sem("out_ready"), 2 * (i + 1))
                sp.dma_start(out[0, i * 128:(i + 1) * 128, :], xout[:, i, :]).then_inc(sem("stored"), 16)
            sp.wait_ge(sem("stored"), 32)

        @block.gpsimd
        def _(pool):
            link = Chain(pool, "pool_order")
            link(nc.gpsimd.memset(vrow[:, :, :], 0.0))
            link(nc.gpsimd.memset(bgate[:, :, :], 0.0))
            vec = sem("vectors_in")
            for i in range(2):
                pool.dma_start(xin[:, i, :], t["ctx"][0, i * 128:(i + 1) * 128, :]).then_inc(sem("x_in"), 16)
                pool.dma_start(xin[:, 2 + i, :], t["x"][0, i * 128:(i + 1) * 128, :]).then_inc(sem("x_in"), 16)
            n = 0
            for l in range(DEPTH):
                for row, src in (
                    (P_NORM, t["g_norm"][l].rearrange("j (k p) -> (j k) p", p=128)),
                    (P_CONV, t["w_conv"][l].rearrange("j o (k p) -> (j o k) p", p=128)),
                    (P_MH, t["g_mhead"][l].rearrange("(k p) -> k p", p=128)),
                    (P_CQ, t["g_cq"][l].rearrange("(k p) -> k p", p=128)),
                    (P_CKV, t["g_ckv"][l].rearrange("(k p) -> k p", p=128)),
                ):
                    pool.dma_start(vrow[row:row + src.shape[0], l, :], src).then_inc(vec, 16)
                    n += 1
                for row, name, width, copies in ((P_QG, "g_q_gqa", GD, 2), (P_KG, "g_k_gqa", GD, 2),
                                                 (P_QM, "g_q_mla", AQK, 1), (P_KM, "g_k_mla", AQK, 1)):
                    for c in range(copies):
                        pool.dma_start(vrow[row:row + 1, l, c * width:(c + 1) * width],
                                       t[name][l].rearrange("(a n) -> a n", a=1)).then_inc(vec, 16)
                        n += 1
                pool.dma_start(mvrow[:, l, :], t["b_mod"][l].rearrange("(k p) -> k p", p=128)).then_inc(vec, 16)
                n += 1
                for q in range(4):
                    at = 32 * (q // 2)
                    pool.dma_start(bgate[at:at + MH, l, q % 2:q % 2 + 1],
                                   t["b_mgate"][l, q].rearrange("(h a) -> h a", a=1)).then_inc(vec, 16)
                    n += 1
            assert n == VECTORS

            for l in range(DEPTH):
                pool.wait_ge(*freed(plan[l, "out", 0][1] + 1))
                link(nc.gpsimd.memset(RN[:, :, :], 0.0))
                link(nc.gpsimd.memset(vaug[:, :, :, MD:MD + 1], 1.0), f"mixer_filled_{l}")
                pool.wait_ge(sem(f"y0_{l}"), MH)
                link(nc.gpsimd.tensor_copy(k96[NOPE:AQK, :, :],
                                           krs[NOPE:AQK, :].rearrange("p (a n) -> p a n", a=1)
                                           .to_broadcast([ROPE, AH, T])), f"kr_spread_{l}")
                for a in (0, 1):
                    P, xn, co, si, cos, tiles = rope_setup(l, a)
                    for i, (dst, c0, _) in enumerate(tiles):
                        tb_, ib_ = before(l, a)
                        pool.wait_ge(sem("qn"), tb_ + i + 1)
                        nc.gpsimd.tensor_tensor(co[0:P, i % 2, :], xn[0:P, i % 2, :], cos,
                                                ALU.mult).then_inc(sem("qcos"), 1)
                        pool.wait_ge(sem("qcos"), tb_ + i + 1)
                        pool.wait_ge(sem("qsin"), tb_ + i + 1)
                        nc.gpsimd.tensor_tensor(dst[:, CTX:T], co[0:P, i % 2, :], si[0:P, i % 2, :],
                                                ALU.add).then_inc(sem("qk_final"), 1)
                        pool.wait_ge(sem("qk_final"), tb_ + i + 1)

        @block.scalar
        def _(act):
            A = nc.scalar.activation
            link = Chain(act, "act_order")
            pos = [0]

            def split(u, it=None, per=0):
                off = (lambda v, m: v if it is None else v + it * m)
                act.wait_ge(landed[u % LOADS], off(16 * (u // LOADS + 1), 16 * per // LOADS))
                if u >= RING:
                    act.wait_ge(unit_used, off(u - RING + 1, per))
                n = size[u]
                A(w_hi[:, u % RING, 0:n], w_raw[:, u % LOADS, 0:n], ACT.Copy).then_inc(hi_done, 1)

            def advance(n):
                for _ in range(n):
                    if pos[0] < U:
                        split(pos[0])
                    pos[0] += 1

            def wait_group(g, it=None, per=0):
                act.wait_ge(unit_used, ends[g] if it is None else ends[g] + it * (per * KT))

            def norm(l, j, g_prev):
                m_ = 3 * l + j
                c0 = first_col(l, j == 2)
                for i in range(KT):
                    if g_prev is None:
                        act.wait_ge(sem("x_ready"), NT)
                    else:
                        act.wait_ge(*freed(g_prev + i // 4))
                    if i >= 3:
                        act.wait_ge(sem("sq_added"), (KT - 1) * m_ + i - 2)
                    dst = acc[:, c0:T] if i == 0 else sq[:, i % 2, c0:T]
                    A(dst, x[:, i, c0:T], ACT.Square).then_inc(sem("sq"), 1)
                act.wait_ge(sem("ss"), m_ + 1)
                A(rms[:, c0:T], ps[:, 0, c0:T], ACT.Sqrt, bias=cst[:, 0:1], scale=1.0 / D).then_inc(sem("rms"), 1)
                for i in range(KT):
                    act.wait_ge(sem("scaled"), KT * m_ + i + 1)
                    if i >= 2:
                        act.wait_ge(sem("h"), KT * m_ + i - 1)
                    for s, a, b in streams(c0):
                        ins = A(hn[:, i % 2, a:b], t1[:, i % 2, a:b], ACT.Identity, bias=mod[:, 3 * j, i, s:s + 1])
                    ins.then_inc(sem("hn"), 1)
                    act.wait_ge(sem("hn"), KT * m_ + i + 1)
                    A(h_hi[:, i, c0:T], hn[:, i % 2, c0:T], ACT.Copy).then_inc(sem("h_hi"), 1)

            def ffn(l, f):
                done = FT // 2 * (2 * l + f)
                c0 = first_col(l, f == 1)
                n = T - c0
                u0, g0 = plan[l, "in", f]

                def evac(b, g, it=None):
                    wait_group(g0 + b, it, 2)
                    s4_ = bank(g0 + b)
                    A(sil[:, :, 0:n], ps[:, s4_:s4_ + 2, 0:n], ACT.Silu).then_inc(sem("sil"), 1)
                    fs, fv = freed(g0 + b)
                    act.wait_ge(fs, fv if it is None else fv + it)
                    A(mid_hi[:, bass.ds(2 * g, 2) if it is not None else slice(2 * g, 2 * g + 2), 0:n],
                      mt[:, :, 0:n], ACT.Copy).then_inc(sem("mid_hi"), 1)

                advance(KT)
                evac(0, 0)
                with act.Fori(0, FT // 4) as i:
                    for b in (1, 2):
                        for j in range(KT):
                            split(pos[0] + (b - 1) * KT + j, i, 2 * KT)
                        evac(b, i * 2 + b, i)
                pos[0] += 2 * KT * (FT // 4)
                _, g0 = plan[l, "out", f]
                for g in range(2):
                    loops = FT // LOADS
                    with act.Fori(0, loops) as i:
                        for j in range(LOADS):
                            split(pos[0] + j, i, LOADS)
                    pos[0] += loops * LOADS
                    advance(FT - loops * LOADS)

            def qk_norm(l, a, fill):
                P, xn, co, si, cos, tiles = rope_setup(l, a)
                nsq, nrm = scr[a][:2]
                tb_, ib_ = before(l, a)
                per, rows = (AQK, STATS) if a == 0 else (GD, 2 * len(tiles))
                if a == 0:
                    act.wait_ge(sem(f"kr_spread_{l}"), 1)
                for i, (dst, c0, _) in enumerate(tiles):
                    if i >= 2:
                        act.wait_ge(sem("qss"), tb_ + i - 1)
                    A(nsq[0:P, i % 2, c0:T], dst[:, c0:T], ACT.Square).then_inc(sem("qsq"), 1)
                act.wait_ge(sem("qss"), tb_ + len(tiles))
                A(nrm[0:rows, :], ps[0:rows, AB, :], ACT.Sqrt, bias=cst[0:rows, 0:1],
                  scale=1.0 / per).then_inc(sem("qrms"), 1)
                for i in range(len(tiles)):
                    next(fill, None)

            def attention(l, a, fill):
                pb, pt, ob, mx, rs = scr[a][5:]
                tb_, ib_ = before(l, a)
                scale = (AQK if a == 0 else GD) ** -0.5
                its = items(l)

                def weights(i):
                    qt, h = its[i]
                    n = key_tiles(qt) * 128
                    act.wait_ge(sem("amax"), ib_ + i + 1)
                    A(pb[:, i % 2, 0:n], ps[:, AB + i % 2, 0:n], ACT.Exp, bias=mx[:, i % 2, 1:2], scale=scale,
                      accum_out=rs[:, qt % 2, h:h + 1]).then_inc(sem("aexp"), 1)

                def output(qt, n):
                    act.wait_ge(sem("aot"), ib_ // 8 + n + 1)
                    A(y_hi[1 + a][:, :, qt * 128:(qt + 1) * 128],
                      ps[:, AB + 2, :].rearrange("p (k n) -> p k n", n=128), ACT.Copy).then_inc(sem("ayh"), 1)

                weights(0)
                weights(1)
                for i, (qt, h) in enumerate(its):
                    if i + 2 < len(its):
                        weights(i + 2)
                    next(fill, None)
                    if h == 0 and i:
                        output(qt - 1, i // 8 - 1)
                output(its[-1][0], len(its) // 8 - 1)

            def merge_steps(l, n):
                n_q = T - first_col(l, True)
                for s_, (og, name, k) in enumerate(MERGE):
                    if has_unit(s_ - 1):
                        advance(1)
                    if name == "gates out":
                        g = plan[l, "gate", og, n][1]
                        wait_group(g)
                        m = 2 * n + og
                        if m in (1, 2):
                            act.wait_ge(*freed(plan[l, "branch", (m - 1) % 2, (m - 1) // 2][1]))
                        elif m > 2:
                            act.wait_ge(sem("gates_used"), 4 * l + m - 2)
                        A(sg[:, :, 0:n_q], ps[:, bank(g):bank(g) + 4, 0:n_q],
                          ACT.Sigmoid).then_inc(banks_free[place[g][0]], 1)
                    if n == NBR - 1 and (og, name, k) == (1, "gate", 3):
                        merged(l, 0, n_q)
                    yield
                if n == NBR - 1:
                    merged(l, 1, n_q)

            def merged(l, og, n_q):
                act.wait_ge(sem("gates_used"), 4 * l + 3 + og)
                A(g_hi[:, og * 4:og * 4 + 4, 0:n_q], mg[:, og * 4:og * 4 + 4, 0:n_q], ACT.Copy).then_inc(sem("g_hi"), 1)

            act.wait_ge(sem("cst"), 1)
            act.wait_ge(sem("s_in"), 32)
            A(s_act[:, :], s_in[:, :], ACT.Silu).then_inc(sem("s_act"), 1)
            act.wait_ge(sem("x_t"), 1)
            A(s_fm[:, :], ps[:, 0, 0:2 * KT], ACT.Copy).then_inc(sem("s_fm"), 1)
            act.wait_ge(sem("s_fm"), 1)
            A(s4[:, :, 0:2].rearrange("p k s -> p s k"), s_fm[:, :].rearrange("p (s k) -> p s k", s=2),
              ACT.Copy).then_inc(sem("s_hi"), 1)
            for i in range(NT):
                act.wait_ge(sem("x_t"), 2 + i)
                b = 2 + 2 * (i % 2)
                A(x[:, :, i * 128:(i + 1) * 128], ps[:, b:b + 2, :].rearrange("p a (k n) -> p (a k) n", n=128),
                  ACT.Copy).then_inc(sem("x_ready"), 1)
            advance(RING)

            g_prev = None
            for l in range(DEPTH):
                _, g0 = plan[l, "mod"]
                with act.Fori(0, 9) as i:
                    for b in range(2):
                        for j in range(KT):
                            split(pos[0] + b * KT + j, i, 2 * KT)
                        wait_group(g0 + b, i, 2)
                        A(mrow[0:4, b, :], ps[0:4, bank(g0 + b), :], ACT.Copy).then_inc(banks_free[place[g0 + b][0]], 1)
                pos[0] += 18 * KT
                norm(l, 0, g_prev)
                ffn(l, 0)
                g_prev = plan[l, "out", 0][1]
                norm(l, 1, g_prev)

                cq = first_col(l, True)
                act.wait_ge(sem(f"pads_{l}"), 1)
                for part, name in enumerate(("q", "k")):
                    c0 = cq if part == 0 else 0
                    s0 = c0 // CTX
                    advance(KT)
                    g = plan[l, name][1]
                    wait_group(g)
                    for i in range(4):
                        if part == 1:
                            act.wait_ge(sem(f"conv_{l}"), i + 1)
                        ins = A(cpad[:, i, s0:2, 2:2 + CTX],
                                ps[:, bank(g) + i, 0:T - c0].rearrange("p (s n) -> p s n", n=CTX), ACT.Copy)
                        ins.then_inc(banks_free[place[g][0]] if i == 3 else sem(f"cpad_{l}"), 1)
                    for i in range(4):
                        n = part * 4 + i
                        act.wait_ge(sem(f"conv_{l}"), n + 1)
                        A(qk[:, n, c0:T].rearrange("p (s n) -> p s n", n=CTX), cacc[:, n % 2, s0:2, :],
                          ACT.Silu).then_inc(sem(f"qk_{l}"), 1)
                advance(KT)
                g = plan[l, "v"][1]
                wait_group(g)
                act.wait_ge(sem(f"mixer_filled_{l}"), 1)
                A(vaug[:, :, :, 0:MD], ps[:, bank(g):bank(g) + 4, :].rearrange("p t (h e) -> p t h e", h=MH),
                  ACT.Copy).then_inc(banks_free[place[g][0]], 1)
                advance(KT + 1)
                g = plan[l, "cqkv"][1]
                b0 = bank(g)
                wait_group(g)
                link(A(craw[:, 0:2, cq:T], ps[:, b0:b0 + 2, 0:T - cq], ACT.Copy))
                link(A(craw[:, 2, :], ps[:, b0 + 2, :], ACT.Copy))
                A(krs[NOPE:AQK, :], ps[0:ROPE, b0 + 3, :], ACT.Copy).then_inc(banks_free[place[g][0]], 1)
                advance(1)
                g = plan[l, "gates"][1]
                wait_group(g)
                A(gz[:, :], ps[0:16, bank(g), :], ACT.Copy).then_inc(banks_free[place[g][0]], 1)

                act.wait_ge(sem(f"rows_{l}"), 2)
                link(A(R[:, 4, :], R[:, 1, :], ACT.Abs))
                link(A(R[:, 4, :], R[:, 4, :], ACT.Exp, scale=-1.0))
                A(R[:, 4, :], R[:, 4, :], ACT.Ln, bias=cst[0:36, 2:3]).then_inc(sem(f"softplus_{l}"), 1)

                def natural(q, src, **kw_):
                    A(RN[0:MH, q, :], src[0:MH, :], ACT.Exp, **{a: v[0:MH] if a == "bias" else v for a, v in kw_.items()})
                    return A(RN[32:36, q, :].rearrange("p (s n) -> p s n", s=2)[:, :, ::-1],
                             src[32:36, :].rearrange("p (s n) -> p s n", s=2), ACT.Exp,
                             **{a: v[32:36] if a == "bias" else v for a, v in kw_.items()})

                for q in range(3):
                    act.wait_ge(sem(f"explog_{l}"), q + 1)
                    if q == 0:
                        natural(1, R[:, 4, :], scale=-1.0).then_inc(sem(f"exprow_{l}"), 1)
                    elif q == 1:
                        natural(2, R[:, 5, :]).then_inc(sem(f"exprow_{l}"), 1)
                    else:
                        natural(3, R[:, 0, :], scale=-1.0, bias=cst[0:36, 1:2]).then_inc(sem(f"exprow_{l}"), 1)
                act.wait_ge(sem(f"explog_{l}"), 4)
                A(dlog[:, :], dlog[:, :], ACT.Exp).then_inc(sem(f"exprow_{l}"), 1)
                act.wait_ge(sem(f"tokt_{l}"), 1)
                A(tok[:, 0:8, :], ps[:, 2, 0:288].rearrange("p (a b) -> p a b", b=36), ACT.Copy)
                link(A(tok[:, 8:16, :], ps[:, 3, 0:288].rearrange("p (a b) -> p a b", b=36), ACT.Copy))
                A(dec[:, :, :], ps[:, 4, 0:32].rearrange("p (a b) -> p a b", b=4), ACT.Copy).then_inc(sem(f"tok_{l}"), 1)

                t0 = cq // 128
                outs = [j for j in range(NT) if scan_tile(0, j) >= t0]
                for h in range(MH):
                    for d in range(2):
                        act.wait_ge(sem(f"dlog_{l}"), 2 * h + d + 1)
                        A(dt_[:, d, t0:, :], dt_[:, d, t0:, :], ACT.Exp).then_inc(sem(f"dexp_{l}"), 1)
                    if h:
                        act.wait_ge(sem(f"cupd_{l}"), 6 * h)
                    act.wait_ge(sem(f"headmm_{l}"), h + 1)
                    for d in range(2):
                        for j in range(NT - 1):
                            tt = scan_tile(d, j)
                            ins = A(kw[:, d, tt, :], ps[:, 3, tt * 128:(tt + 1) * 128], ACT.Copy,
                                    scale=tok[:, 8 + tt, 32 * d + h:32 * d + h + 1])
                    ins.then_inc(sem(f"kw_{l}"), 1)
                    for j in range(1, NT):
                        for d in range(2):
                            if j not in outs:
                                continue
                            tt = scan_tile(d, j)
                            n = 2 * (len(outs) * h + outs.index(j)) + d + 1
                            act.wait_ge(sem(f"nmm_{l}"), n)
                            A(an[:, d, :], ps[:, 6 + d, 0:MD + 1], ACT.Copy,
                              scale=tok[:, 4 + tt, 32 * d + h:32 * d + h + 1]).then_inc(sem(f"an_{l}"), 1)
                    act.wait_ge(sem(f"hsum_{l}"), h + 1)
                    link(A(sqt[:, t0:, :], hsn[:, h, t0:, :], ACT.Square), f"hsq_{l}")
                    act.wait_ge(sem(f"hss_{l}"), h + 1)
                    A(rn[:, t0:], rn[:, t0:], ACT.Sqrt, bias=cst[:, 0:1], scale=1.0 / MD).then_inc(sem(f"hrms_{l}"), 1)
                advance(KT)
                g = plan[l, "o"][1]
                wait_group(g)
                act.wait_ge(sem(f"hout_{l}"), MH)
                A(sigo[:, :, cq:T], ps[:, bank(g):bank(g) + 4, 0:T - cq], ACT.Sigmoid).then_inc(banks_free[place[g][0]], 1)
                for h in range(MH):
                    act.wait_ge(sem(f"yt_{l}"), h + 1)
                    A(y_hi[0][:, h, cq:T], yt[:, h % 2, cq:T], ACT.Copy).then_inc(sem(f"y0h_{l}"), 1)

                act.wait_ge(sem(f"y0_{l}"), MH)
                A(csq[:, 0:2, cq:T], craw[:, 0:2, cq:T], ACT.Square)
                A(csq[:, 2, :], craw[:, 2, :], ACT.Square).then_inc(sem(f"csq_{l}"), 1)
                act.wait_ge(sem(f"css_{l}"), 1)
                A(crm[:, 0, cq:T], ps[:, 0, cq:T], ACT.Sqrt, bias=cst[:, 0:1], scale=1.0 / QR)
                A(crm[:, 1, :], ps[:, 1, :], ACT.Sqrt, bias=cst[:, 0:1], scale=1.0 / KVR).then_inc(sem(f"crm_{l}"), 1)
                act.wait_ge(sem(f"cn_{l}"), 1)
                A(cn_hi[:, 0:2, cq:T], cn[:, 0:2, cq:T], ACT.Copy)
                A(cn_hi[:, 2, :], cn[:, 2, :], ACT.Copy).then_inc(sem(f"cn_hi_{l}"), 1)
                for half in range(2):
                    advance(2)
                    g = plan[l, "uq", half][1]
                    wait_group(g)
                    A(q96[:, half * 4:half * 4 + 4, cq:T], ps[0:AQK, bank(g):bank(g) + 4, 0:T - cq],
                      ACT.Copy).then_inc(banks_free[place[g][0]], 1)
                advance(1)
                g = plan[l, "kn"][1]
                b0 = bank(g)
                wait_group(g)
                k2 = k96[0:NOPE].rearrange("p (i s) n -> p i s n", s=2)
                link(A(k2[:, :, 0, :], ps[0:NOPE, b0:b0 + 4, :], ACT.Copy))
                A(k2[:, :, 1, :], ps[NOPE:128, b0:b0 + 4, :], ACT.Copy).then_inc(banks_free[place[g][0]], 1)
                advance(1)
                g = plan[l, "kv"][1]
                wait_group(g)
                A(vm[:, :, :], ps[:, bank(g):bank(g) + 4, :], ACT.Copy).then_inc(banks_free[place[g][0]], 1)
                act.wait_ge(*freed(g))
                fill = merge_steps(l, 0)
                qk_norm(l, 0, fill)
                attention(l, 0, fill)
                for _ in fill:
                    pass

                act.wait_ge(sem("ay"), before(l, 0)[1] // 8 + len(items(l)) // 8)
                advance(KT)
                g = plan[l, "gq"][1]
                wait_group(g)
                A(qg[:, :, cq:T], ps[:, bank(g):bank(g) + 4, 0:T - cq], ACT.Copy).then_inc(banks_free[place[g][0]], 1)
                advance(KT)
                g = plan[l, "gkv"][1]
                b0 = bank(g)
                wait_group(g)
                for m in range(GKV):
                    for r in (0, GD):
                        link(A(kg[r:r + GD, m, :], ps[m * GD:(m + 1) * GD, b0, :], ACT.Copy))
                A(vg[:, :, :], ps[:, b0 + 1, :].rearrange("p (t n) -> p t n", n=128), ACT.Copy).then_inc(banks_free[place[g][0]], 1)
                act.wait_ge(*freed(g))
                fill = merge_steps(l, 1)
                qk_norm(l, 1, fill)
                attention(l, 1, fill)
                for _ in fill:
                    pass

                for _ in merge_steps(l, 2):
                    pass
                advance(2 * KT)
                g_prev = plan[l, "wout"][1]
                norm(l, 2, g_prev)
                ffn(l, 1)
                g_prev = plan[l, "out", 1][1]
            for i in range(2):
                for b in range(2):
                    act.wait_ge(sem("out_t"), i + 1)
                    A(xout[:, i, b * 512:(b + 1) * 512], ps[:, 2 * i + b, :], ACT.Copy).then_inc(sem("out_ready"), 1)

        @block.vector
        def _(dve):
            V = nc.vector
            link = Chain(dve, "dve_order")
            pos = [0]

            def split(u, it=None, per=0):
                n = size[u]
                dve.wait_ge(hi_done, u + 1 if it is None else u + 1 + it * per)
                V.tensor_tensor(w_lo[:, u % RING, 0:n], w_raw[:, u % LOADS, 0:n],
                                w_hi[:, u % RING, 0:n].bitcast(fp32), ALU.subtract).then_inc(lo_done, 1)

            def advance(n):
                for _ in range(n):
                    if pos[0] < U:
                        split(pos[0])
                    pos[0] += 1

            def norm(l, j):
                m_ = 3 * l + j
                c0 = first_col(l, j == 2)
                for i in range(1, KT):
                    dve.wait_ge(sem("sq"), KT * m_ + i + 1)
                    link(V.tensor_tensor(acc[:, c0:T], acc[:, c0:T], sq[:, i % 2, c0:T], ALU.add), "sq_added")
                dve.wait_ge(sem("rms"), m_ + 1)
                link(V.reciprocal(rms[:, c0:T], rms[:, c0:T]))
                for i in range(KT + 1):
                    if i < KT:
                        if i >= 2:
                            dve.wait_ge(sem("hn"), KT * m_ + i - 1)
                        for s, a, b in streams(c0):
                            ins = V.scalar_tensor_tensor(out=t1[:, i % 2, a:b], in0=x[:, i, a:b],
                                                         scalar=gain[:, j, i, s:s + 1], in1=rms[:, a:b],
                                                         op0=ALU.mult, op1=ALU.mult)
                        ins.then_inc(sem("scaled"), 1)
                    if i >= 1:
                        dve.wait_ge(sem("h_hi"), KT * m_ + i)
                        V.tensor_tensor(h_lo[:, i - 1, c0:T], hn[:, (i - 1) % 2, c0:T],
                                        h_hi[:, i - 1, c0:T].bitcast(fp32), ALU.subtract).then_inc(sem("h"), 1)

            def residual(l, m, g0, c0, gate):
                g = g0 + m
                dve.wait_ge(unit_used, ends[g])
                for i in range(4):
                    for s, a, b in streams(c0):
                        ins = V.scalar_tensor_tensor(out=x[:, 4 * m + i, a:b], in0=ps[:, bank(g) + i, a - c0:b - c0],
                                                     scalar=mod[:, gate, 4 * m + i, s:s + 1],
                                                     in1=x[:, 4 * m + i, a:b], op0=ALU.mult, op1=ALU.add)
                ins.then_inc(banks_free[place[g][0]], 1)

            def ffn(l, f):
                done = FT // 2 * (2 * l + f)
                c0 = first_col(l, f == 1)
                n = T - c0
                u0, g0 = plan[l, "in", f]

                def evac(b, g, it=None):
                    off = (lambda v: v if it is None else v + it * 2)
                    s4_ = bank(g0 + b)
                    dve.wait_ge(sem("sil"), off(done + b + 1))
                    if b:
                        dve.wait_ge(sem("mid"), off(done + b))
                    V.tensor_tensor(mt[:, :, 0:n], ps[:, s4_ + 2:s4_ + 4, 0:n], sil[:, :, 0:n],
                                    ALU.mult).then_inc(banks_free[place[g0 + b][0]], 1)
                    dve.wait_ge(sem("mid_hi"), off(done + b + 1))
                    at = bass.ds(2 * g, 2) if it is not None else slice(2 * g, 2 * g + 2)
                    V.tensor_tensor(mid_lo[:, at, 0:n], mt[:, :, 0:n], mid_hi[:, at, 0:n].bitcast(fp32),
                                    ALU.subtract).then_inc(sem("mid"), 1)

                advance(KT)
                evac(0, 0)
                with dve.Fori(0, FT // 4) as i:
                    for b in (1, 2):
                        for j in range(KT):
                            split(pos[0] + (b - 1) * KT + j, i, 2 * KT)
                        evac(b, i * 2 + b, i)
                pos[0] += 2 * KT * (FT // 4)
                _, g0 = plan[l, "out", f]
                for g in range(2):
                    loops = FT // LOADS
                    with dve.Fori(0, loops) as i:
                        for j in range(LOADS):
                            split(pos[0] + j, i, LOADS)
                    pos[0] += loops * LOADS
                    advance(FT - loops * LOADS)
                    residual(l, g, g0, c0, 2 if f == 0 else 8)

            def qk_norm(l, a, fill):
                P, xn, co, si, cos, tiles = rope_setup(l, a)
                nrm = scr[a][1]
                sin = tb("sinm" if a == 0 else "sing")
                tb_, ib_ = before(l, a)
                rows = STATS if a == 0 else 2 * len(tiles)

                def normed(i):
                    dst, c0, row = tiles[i]
                    dve.wait_ge(sem("qspread"), tb_ + i + 1)
                    if i >= 2:
                        dve.wait_ge(sem("qcos"), tb_ + i - 1)
                        dve.wait_ge(sem("qsin"), tb_ + i - 1)
                    if c0 < CTX:
                        V.scalar_tensor_tensor(out=dst[:, 0:CTX], in0=dst[:, 0:CTX], scalar=prm[0:P, l, row:row + 1],
                                               in1=ps[0:P, AB + i % 2, 0:CTX], op0=ALU.mult, op1=ALU.mult)
                    V.scalar_tensor_tensor(out=xn[0:P, i % 2, :], in0=dst[:, CTX:T], scalar=prm[0:P, l, row:row + 1],
                                           in1=ps[0:P, AB + i % 2, CTX:T], op0=ALU.mult,
                                           op1=ALU.mult).then_inc(sem("qn"), 1)

                dve.wait_ge(sem("qrms"), 2 * l + a + 1)
                V.reciprocal(nrm[0:rows, :], nrm[0:rows, :]).then_inc(sem("qinv"), 1)
                normed(0)
                for i in range(len(tiles)):
                    next(fill, None)
                    if i + 1 < len(tiles):
                        normed(i + 1)
                    dve.wait_ge(sem("qrot"), tb_ + i + 1)
                    if i >= 2:
                        dve.wait_ge(sem("qk_final"), tb_ + i - 1)
                    V.tensor_tensor(si[0:P, i % 2, :], ps[0:P, AB + 2 + i % 2, 0:T - CTX], sin,
                                    ALU.mult).then_inc(sem("qsin"), 1)

            def attention(l, a, fill):
                pb, pt, ob, mx, rs = scr[a][5:]
                tb_, ib_ = before(l, a)
                scale = (AQK if a == 0 else GD) ** -0.5
                its = items(l)
                dve.wait_ge(sem("qk_final"), tb_ + len(rope_setup(l, a)[5]))

                def maxima(i):
                    n = key_tiles(its[i][0]) * 128
                    dve.wait_ge(sem("asc"), ib_ + i + 1)
                    link(V.reduce_max(mx[:, i % 2, 0:1], ps[:, AB + i % 2, 0:n], AX.X))
                    V.tensor_scalar(mx[:, i % 2, 1:2], mx[:, i % 2, 0:1], -scale, None, ALU.mult).then_inc(sem("amax"), 1)

                def divide(qt, last_item):
                    dve.wait_ge(sem("apv"), ib_ + last_item + 1)
                    link(V.reciprocal(rs[:, qt % 2, :], rs[:, qt % 2, :]))
                    V.tensor_tensor(ob[:, :, :], ps[:, AB + 3, :].rearrange("p (h e) -> p h e", h=8),
                                    rs[:, qt % 2, :].rearrange("p (h a) -> p h a", a=1).to_broadcast([128, 8, 64]),
                                    ALU.mult).then_inc(sem("aob"), 1)

                def output(qt, n):
                    dve.wait_ge(sem("ayh"), ib_ // 8 + n + 1)
                    cols = slice(qt * 128, (qt + 1) * 128)
                    V.tensor_tensor(y_lo[1 + a][:, :, cols], ps[:, AB + 2, :].rearrange("p (k n) -> p k n", n=128),
                                    y_hi[1 + a][:, :, cols].bitcast(fp32), ALU.subtract).then_inc(sem("ay"), 1)

                maxima(0)
                maxima(1)
                for i, (qt, h) in enumerate(its):
                    n = key_tiles(qt)
                    dve.wait_ge(sem("atr"), ib_ + i + 1)
                    V.tensor_copy(pt[:, i % 2, 0:n, :], ps[:, AB + 2, 0:n * 128].rearrange("p (k n) -> p k n", n=128))\
                        .then_inc(sem("apt"), 1)
                    if h == 0 and i:
                        divide(qt - 1, i - 1)
                    if i + 2 < len(its):
                        maxima(i + 2)
                    next(fill, None)
                    if h == 0 and i:
                        output(qt - 1, i // 8 - 1)
                divide(its[-1][0], len(its) - 1)
                output(its[-1][0], len(its) // 8 - 1)

            def merge_steps(l, n):
                n_q = T - first_col(l, True)

                def weighted(og):
                    g = plan[l, "branch", og, n][1]
                    src = ps[:, bank(g):bank(g) + 4, 0:n_q]
                    dst, gates = mg[:, og * 4:og * 4 + 4, 0:n_q], sg[:, :, 0:n_q]
                    dve.wait_ge(unit_used, ends[g])
                    dve.wait_ge(*freed(plan[l, "gate", og, n][1]))
                    V.tensor_tensor(gates if n else dst, src, gates, ALU.mult).then_inc(banks_free[place[g][0]], 1)
                    if n:
                        dve.wait_ge(*freed(g))
                        link(V.tensor_tensor(dst, dst, gates, ALU.add), "gates_used")

                def low(og):
                    dve.wait_ge(sem("g_hi"), 2 * l + og + 1)
                    V.tensor_tensor(g_lo[:, og * 4:og * 4 + 4, 0:n_q], mg[:, og * 4:og * 4 + 4, 0:n_q],
                                    g_hi[:, og * 4:og * 4 + 4, 0:n_q].bitcast(fp32), ALU.subtract).then_inc(sem("g"), 1)

                for s_, (og, name, k) in enumerate(MERGE):
                    if name == "branch out":
                        weighted(og)
                    if has_unit(s_ - 2):
                        advance(1)
                    if n == NBR - 1 and (og, name, k) == (1, "gate", 5):
                        low(0)
                    yield
                advance(1)
                if n == NBR - 1:
                    low(1)

            link(V.memset(cst[:, 0:1], EPS))
            link(V.memset(cst[:, 1:2], 0.5 * float(np.log(MD))))
            V.memset(cst[:, 2:3], 1.0).then_inc(sem("cst"), 1)
            dve.wait_ge(sem("s_hi"), 1)
            V.tensor_tensor(s4[:, :, 2:4].rearrange("p k s -> p s k"), s_fm[:, :].rearrange("p (s k) -> p s k", s=2),
                            s4[:, :, 0:2].rearrange("p k s -> p s k").bitcast(fp32), ALU.subtract).then_inc(sem("s4"), 1)
            dve.wait_ge(sem("vec_t"), 1)
            V.tensor_copy(prm[:, :, :], ps[:, 6, 0:DEPTH * P_ROWS].rearrange("p (l n) -> p l n", l=DEPTH))
            V.tensor_copy(bmod[:, :, :], ps[:, 7, 0:DEPTH * M_ROWS].rearrange("p (l n) -> p l n", l=DEPTH))\
                .then_inc(sem("params"), 1)
            dve.wait_ge(sem("params"), 1)
            advance(RING)

            for l in range(DEPTH):
                cq = first_col(l, True)
                with dve.Fori(0, 9) as i:
                    for j in range(2 * KT):
                        split(pos[0] + j, i, 2 * KT)
                pos[0] += 18 * KT
                dve.wait_ge(sem("mod_t"), 18 * (l + 1))
                m3 = mod[:, :, :, :].rearrange("p a k s -> p (a k) s")
                link(V.tensor_tensor(m3, ps[:, 7, 0:2 * M_ROWS].rearrange("p (a s) -> p a s", s=2),
                                     bmod[:, l, :].rearrange("p (a s) -> p a s", s=1).to_broadcast([128, M_ROWS, 2]),
                                     ALU.add))
                for j in range(3):
                    link(V.scalar_tensor_tensor(
                        out=gain[:, j, :, :], in0=mod[:, 3 * j + 1, :, :], scalar=1.0,
                        in1=prm[:, l, P_NORM + j * KT:P_NORM + (j + 1) * KT].rearrange("p (k s) -> p k s", s=1)
                        .to_broadcast([128, KT, 2]), op0=ALU.add, op1=ALU.mult))
                for gate in (2, 8):
                    link(V.tensor_scalar(mod[:, gate, :, :], mod[:, gate, :, :], 0.5, None, ALU.mult),
                         "mods")
                norm(l, 0)
                ffn(l, 0)
                norm(l, 1)

                dve.wait_ge(*freed(plan[l, "out", 0][1] + 1))
                V.memset(cpad[:, :, :, 0:2], 0.0)
                V.memset(cpad[:, :, :, 2 + CTX:4 + CTX], 0.0).then_inc(sem(f"pads_{l}"), 1)
                for part, name in enumerate(("q", "k")):
                    c0 = cq if part == 0 else 0
                    s0 = c0 // CTX
                    g = plan[l, name][1]
                    advance(RING)
                    for i in range(4):
                        n = part * 4 + i
                        if i < 3:
                            dve.wait_ge(sem(f"cpad_{l}"), 3 * part + i + 1)
                        else:
                            dve.wait_ge(*freed(g))
                        if n >= 2:
                            dve.wait_ge(sem(f"qk_{l}"), n - 1)
                        dst = cacc[:, n % 2, s0:2, :]
                        w = [prm[:, l, P_CONV + j * 2 * MH + n:P_CONV + j * 2 * MH + n + 1] for j in range(TAPS)]
                        link(V.tensor_scalar(dst, cpad[:, i, s0:2, 0:CTX], w[0], None, ALU.mult))
                        for j in range(1, TAPS):
                            ins = V.scalar_tensor_tensor(out=dst, in0=cpad[:, i, s0:2, j:j + CTX], scalar=w[j],
                                                         in1=dst, op0=ALU.mult, op1=ALU.add)
                            link(ins, f"conv_{l}" if j == TAPS - 1 else None)
                        advance(1)
                advance(KT)
                advance(KT + 1)
                advance(1)

                dve.wait_ge(sem(f"sel_{l}"), 1)
                link(V.tensor_scalar(R[:, 0, :], ps[0:36, 0, :], bgate[:, l, 0:1], None, ALU.add), f"rows_{l}")
                link(V.tensor_scalar(R[:, 1, :], ps[0:36, 1, :], bgate[:, l, 1:2], None, ALU.add), f"rows_{l}")
                dve.wait_ge(sem(f"softplus_{l}"), 1)
                link(V.scalar_tensor_tensor(out=R[:, 1, :], in0=R[:, 1, :], scalar=0.0, in1=R[:, 4, :],
                                            op0=ALU.min, op1=ALU.subtract))
                for j in range(NT):
                    c = slice(j * 128, (j + 1) * 128)
                    link(V.tensor_tensor_scan(R[:, 2, c], tb("ones")[0:36, :], R[:, 1, c], 0.0, ALU.mult, ALU.add))
                link(V.tensor_tensor(R[:, 3, :], R[:, 0, :], R[:, 2, :], ALU.subtract))
                link(V.memset(mprev[:, :], 0.0))
                for j in range(NT):
                    c = slice(j * 128, (j + 1) * 128)
                    e = (j + 1) * 128 - 1
                    link(V.tensor_tensor_scan(R[:, 1, c], R[:, 3, c], R[:, 3, c], mprev[:, j:j + 1], ALU.max, ALU.max))
                    link(V.tensor_tensor(mprev[:, j + 1:j + 2], R[:, 1, e:e + 1], R[:, 2, e:e + 1], ALU.add))

                def chunks(row):
                    return R[:, row, :].rearrange("p (j n) -> p j n", n=128)

                def spread(ap):
                    return ap.to_broadcast([36, NT, 128])

                last_m = chunks(1)[:, :, 127:128]
                starts = mprev[:, 0:NT].rearrange("p (j a) -> p j a", a=1)
                link(V.tensor_tensor(chunks(4), chunks(1), spread(starts), ALU.subtract), f"explog_{l}")
                link(V.tensor_tensor(chunks(5), chunks(3), spread(last_m), ALU.subtract), f"explog_{l}")
                link(V.tensor_tensor(R[:, 0, :], R[:, 2, :], R[:, 1, :], ALU.add), f"explog_{l}")
                link(V.tensor_tensor(dlog[:, :].rearrange("p (j a) -> p j a", a=1), starts, last_m, ALU.subtract),
                     f"explog_{l}")
                dve.wait_ge(sem(f"mixer_filled_{l}"), 1)
                for q, row, by in ((0, 3, 1.0), (4, 1, -1.0)):
                    V.tensor_scalar(RN[0:MH, q, :], R[0:MH, row, :], by, None, ALU.mult)
                    ins = V.tensor_scalar(RN[32:36, q, :].rearrange("p (s n) -> p s n", s=2)[:, :, ::-1],
                                          R[32:36, row, :].rearrange("p (s n) -> p s n", s=2), by, None, ALU.mult)
                    link(ins, f"rown_{l}")

                t0 = cq // 128
                nt = NT - t0
                outs = [j for j in range(NT) if scan_tile(0, j) >= t0]
                dve.wait_ge(sem(f"tok_{l}"), 1)
                mask = tb("mask").rearrange("p (d a n) -> p d a n", d=2, a=1)
                for h in range(MH):
                    dve.wait_ge(sem(f"headmm_{l}"), h + 1)
                    for d in range(2):
                        col = 32 * d + h
                        link(V.tensor_tensor(dt_[:, d, t0:, :], ps[:, 1 + d, t0 * 128:].rearrange("p (t n) -> p t n", n=128),
                                             tok[:, t0:4, col:col + 1].to_broadcast([128, nt, 128]), ALU.add))
                        link(V.tensor_tensor(dt_[:, d, t0:, :], dt_[:, d, t0:, :],
                                             mask[:, d].to_broadcast([128, nt, 128]), ALU.min), f"dlog_{l}")
                    for d in range(2):
                        dve.wait_ge(sem(f"dexp_{l}"), 2 * h + d + 1)
                        link(V.tensor_tensor(P_[:, d, t0:, :], dt_[:, d, t0:, :],
                                             ps[:, 0, t0 * 128:].rearrange("p (t n) -> p t n", n=128), ALU.mult),
                             f"P_{l}")
                    an_n = [j for j in outs if j >= 1]
                    for j in range(NT):
                        for d in range(2):
                            tt = scan_tile(d, j)
                            if j in outs:
                                n = 2 * (len(outs) * h + outs.index(j)) + d + 1
                                dve.wait_ge(sem(f"nmm_{l}"), n)
                                if j == 0:
                                    link(V.tensor_copy(HN[:, d, tt, :], ps[:, 4 + d, 0:MD + 1]), f"hn_{l}")
                                else:
                                    dve.wait_ge(sem(f"an_{l}"), 2 * (len(an_n) * h + an_n.index(j)) + d + 1)
                                    link(V.tensor_tensor(HN[:, d, tt, :], ps[:, 4 + d, 0:MD + 1], an[:, d, :], ALU.add),
                                         f"hn_{l}")
                            if j < NT - 1:
                                dve.wait_ge(sem(f"dcmm_{l}"), 2 * (3 * h + j) + d + 1)
                                if j == 0:
                                    link(V.tensor_copy(C_[:, d, :], ps[:, 1 + d, 0:MD + 1]), f"cupd_{l}")
                                else:
                                    link(V.scalar_tensor_tensor(out=C_[:, d, :], in0=C_[:, d, :],
                                                                scalar=dec[:, 4 * d + h, j:j + 1],
                                                                in1=ps[:, 1 + d, 0:MD + 1], op0=ALU.mult, op1=ALU.add),
                                         f"cupd_{l}")
                    den = HN[:, :, t0:, MD:MD + 1].rearrange("p d t a -> p d (t a)")
                    dnt = dn[:, :, t0:]
                    floor = tok[:, 12 + t0:16, :].rearrange("p t c -> p c t")[:, h:h + 33:32, :]
                    link(V.scalar_tensor_tensor(out=dnt, in0=den, scalar=-1.0, in1=den, op0=ALU.mult, op1=ALU.max))
                    link(V.tensor_tensor(dnt, dnt, floor, ALU.max))
                    link(V.reciprocal(dnt, dnt))
                    for d in range(2):
                        r = dn[:, d, t0:].rearrange("p (t a) -> p t a", a=1).to_broadcast([128, nt, MD])
                        link(V.tensor_tensor(HN[:, d, t0:, 0:MD], HN[:, d, t0:, 0:MD], r, ALU.mult))
                    link(V.tensor_tensor(hsn[:, h, t0:, :], HN[:, 0, t0:, 0:MD], HN[:, 1, t0:, 0:MD], ALU.add), f"hsum_{l}")
                    dve.wait_ge(sem(f"hsq_{l}"), h + 1)
                    link(V.reduce_sum(rn[:, t0:], sqt[:, t0:, :], AX.X), f"hss_{l}")
                    dve.wait_ge(sem(f"hrms_{l}"), h + 1)
                    link(V.reciprocal(rn[:, t0:], rn[:, t0:]))
                    link(V.tensor_tensor(hsn[:, h, t0:, :], hsn[:, h, t0:, :],
                                         rn[:, t0:].rearrange("p (t a) -> p t a", a=1).to_broadcast([128, nt, MD]),
                                         ALU.mult), f"hout_{l}")
                advance(KT)
                dve.wait_ge(*freed(plan[l, "o"][1]))
                for h in range(MH):
                    dve.wait_ge(sem(f"ht_{l}"), h + 1)
                    if h >= 2:
                        dve.wait_ge(sem(f"y0_{l}"), h - 1)
                    V.scalar_tensor_tensor(out=yt[:, h % 2, cq:T], in0=ps[:, y0_bank(l, h), cq:T],
                                           scalar=prm[:, l, P_MH + h:P_MH + h + 1], in1=sigo[:, h, cq:T],
                                           op0=ALU.mult, op1=ALU.mult).then_inc(sem(f"yt_{l}"), 1)
                    dve.wait_ge(sem(f"y0h_{l}"), h + 1)
                    V.tensor_tensor(y_lo[0][:, h, cq:T], yt[:, h % 2, cq:T], y_hi[0][:, h, cq:T].bitcast(fp32),
                                    ALU.subtract).then_inc(sem(f"y0_{l}"), 1)

                dve.wait_ge(sem(f"y0_{l}"), MH)
                dve.wait_ge(sem(f"crm_{l}"), 1)
                link(V.reciprocal(crm[:, 0, cq:T], crm[:, 0, cq:T]))
                link(V.reciprocal(crm[:, 1, :], crm[:, 1, :]))
                for i in range(3):
                    c0 = cq if i < 2 else 0
                    ins = V.scalar_tensor_tensor(out=cn[:, i, c0:T], in0=craw[:, i, c0:T],
                                                 scalar=prm[:, l, P_CQ + i:P_CQ + i + 1], in1=crm[:, i // 2, c0:T],
                                                 op0=ALU.mult, op1=ALU.mult)
                ins.then_inc(sem(f"cn_{l}"), 1)
                dve.wait_ge(sem(f"cn_hi_{l}"), 1)
                V.tensor_tensor(cn_lo[:, 0:2, cq:T], cn[:, 0:2, cq:T], cn_hi[:, 0:2, cq:T].bitcast(fp32), ALU.subtract)
                V.tensor_tensor(cn_lo[:, 2, :], cn[:, 2, :], cn_hi[:, 2, :].bitcast(fp32),
                                ALU.subtract).then_inc(sem(f"cn_lo_{l}"), 1)
                advance(6)
                fill = merge_steps(l, 0)
                qk_norm(l, 0, fill)
                attention(l, 0, fill)
                for _ in fill:
                    pass
                advance(2 * KT)
                fill = merge_steps(l, 1)
                qk_norm(l, 1, fill)
                attention(l, 1, fill)
                for _ in fill:
                    pass
                for _ in merge_steps(l, 2):
                    pass
                for m in range(2):
                    advance(KT)
                    residual(l, m, plan[l, "wout"][1], cq, 5)
                norm(l, 2)
                ffn(l, 1)

        @block.tensor
        def _(pe):
            M = nc.tensor.matmul
            TR = nc.tensor.transpose

            def all_free(g):
                for b in last_groups(g):
                    pe.wait_ge(*freed(b))

            def banks(g, it=None, per=0):
                v = place[g][1]
                if v:
                    pe.wait_ge(banks_free[place[g][0]], v if it is None else v + it * per)
                return bank(g)

            def ready(u, it=None, per=0):
                pe.wait_ge(lo_done, u + 1 if it is None else u + 1 + it * per)
                return u % RING

            def passes(dst, pairs, first, final, **kw_):
                for i, (a, b) in enumerate(pairs):
                    ins = M(dst, a, b, start=first and i == 0, stop=final and i == len(pairs) - 1, **kw_)
                return ins

            def three(w, r):
                return ((w[0], r[0]), (w[0], r[1]), (w[1], r[0]))

            def weight(slot, a, b):
                return w_hi[:, slot, a:b], w_lo[:, slot, a:b]

            def tiles4(b0, slot, rhs, n, first, final, count=4, width=128):
                for m in range(count):
                    ins = passes(ps[0:width, b0 + m, 0:n], three(weight(slot, m * width, (m + 1) * width), rhs),
                                 first, final)
                return ins

            def h_rhs(k, c0):
                return h_hi[:, k, c0:T], h_lo[:, k, c0:T]

            def feature_group(key, g, c0, norm_no=None, count=4):
                u0 = plan[key][0]
                b0 = banks(g)
                for k in range(KT):
                    if norm_no is not None:
                        pe.wait_ge(sem("h"), KT * norm_no + k + 1)
                    ins = tiles4(b0, ready(u0 + k), h_rhs(k, c0), T - c0, k == 0, k == KT - 1, count)
                    if k < KT - 1 or key[1] == "cqkv":
                        ins.then_inc(unit_used, 1)
                return ins

            def norm_stats(l, j, g):
                m_ = 3 * l + j
                c0 = first_col(l, j == 2)
                all_free(g)
                pe.wait_ge(sem("sq_added"), (KT - 1) * (m_ + 1))
                M(ps[:, 0, c0:T], tb("ones"), acc[:, c0:T], start=True, stop=True).then_inc(sem("ss"), 1)
                pe.wait_ge(sem("rms"), m_ + 1)

            def ffn(l, f):
                done = FT // 2 * (2 * l + f)
                c0 = first_col(l, f == 1)
                n = T - c0
                u0, g0 = plan[l, "in", f]

                def group(b, first, it=None):
                    b0 = banks(g0 + b, it, 1)
                    for k in range(KT):
                        if first:
                            pe.wait_ge(sem("h"), KT * (3 * l + 2 * f) + k + 1)
                        slot = ready(u0 + b * KT + k, it, 2 * KT)
                        ins = tiles4(b0, slot, h_rhs(k, c0), n, k == 0, k == KT - 1)
                        if k < KT - 1:
                            ins.then_inc(unit_used, 1)
                    finish(ins, g0 + b)

                group(0, True)
                with pe.Fori(0, FT // 4) as i:
                    for b in (1, 2):
                        group(b, False, i)
                u0, g0 = plan[l, "out", f]
                for g in range(2):
                    b0 = banks(g0 + g)
                    u = u0 + g * FT
                    if g == 0:
                        pe.wait_ge(sem("mid"), done + FT // 2)

                    def unit(slot, rhs, first, final):
                        return tiles4(b0, slot, rhs, n, first, final)

                    unit(ready(u), (mid_hi[:, 0, 0:n], mid_lo[:, 0, 0:n]), True, False).then_inc(unit_used, 1)
                    loops = (FT - 2) // RING
                    with pe.Fori(0, loops) as i:
                        for j in range(RING):
                            slot = ready(u + 1 + j, i, RING)
                            kk = bass.ds(i * RING + (1 + j), 1)
                            unit(slot, (mid_hi[:, kk, 0:n], mid_lo[:, kk, 0:n]), False, False).then_inc(unit_used, 1)
                    ins = unit(ready(u + FT - 1), (mid_hi[:, FT - 1, 0:n], mid_lo[:, FT - 1, 0:n]), False, True)
                    finish(ins, g0 + g)

            def qk_norm_attend(l, a, g_next, fill):
                P, xn, co, si, cos, tiles = rope_setup(l, a)
                nsq = scr[a][0]
                pb, pt, ob = scr[a][5:8]
                tb_, ib_ = before(l, a)
                nrm = scr[a][1]
                rot = tb("rotm" if a == 0 else "rotg")
                rows = STATS if a == 0 else 2 * len(tiles)
                all_free(g_next)
                for i, (_, c0, _) in enumerate(tiles):
                    at = STATS - 1 - i if a == 0 else STATS - 2 - 2 * i
                    pe.wait_ge(sem("qsq"), tb_ + i + 1)
                    M(ps[0:rows, AB, c0:T], tb("sum1" if a == 0 else "sum2")[0:P, at:at + rows], nsq[0:P, i % 2, c0:T],
                      start=i == 0, stop=i == len(tiles) - 1).then_inc(sem("qss"), 1)

                def spread(i):
                    c0 = tiles[i][1]
                    if i >= 2:
                        pe.wait_ge(sem("qn"), tb_ + i - 1)
                    row = ident[0:rows, i:i + 1].to_broadcast([rows, P]) if a == 0 else \
                        tb("spread")[:, i * 128:(i + 1) * 128]
                    M(ps[0:P, AB + i % 2, c0:T], row, nrm[0:rows, c0:T], start=True, stop=True)\
                        .then_inc(sem("qspread"), 1)

                pe.wait_ge(sem("qinv"), 2 * l + a + 1)
                spread(0)
                for i in range(len(tiles)):
                    if i + 1 < len(tiles):
                        spread(i + 1)
                    pe.wait_ge(sem("qn"), tb_ + i + 1)
                    if i >= 2:
                        pe.wait_ge(sem("qsin"), tb_ + i - 1)
                    M(ps[0:P, AB + 2 + i % 2, 0:T - CTX], rot, xn[0:P, i % 2, :], start=True, stop=True)\
                        .then_inc(sem("qrot"), 1)
                    next(fill, None)
                pe.wait_ge(sem("qk_final"), tb_ + len(tiles))

                its = items(l)

                def scores(i):
                    qt, h = its[i]
                    n = key_tiles(qt) * 128
                    if i >= 2:
                        pe.wait_ge(sem("aexp"), ib_ + i - 1)
                    cols = slice(qt * 128, (qt + 1) * 128)
                    if a == 0:
                        q_, k_ = q96[:, h, cols], k96[:, h, 0:n]
                    else:
                        r = slice(64 * (h % 2), 64 * (h % 2) + 64)
                        q_, k_ = qg[r, h // 2, cols], kg[r, h // 4, 0:n]
                    M(ps[:, AB + i % 2, 0:n], q_, k_, start=True, stop=True).then_inc(sem("asc"), 1)

                def turned(i):
                    pe.wait_ge(sem("aexp"), ib_ + i + 1)
                    if i:
                        pe.wait_ge(sem("apt"), ib_ + i)
                    if i % 8 == 1 and i > 8:
                        pe.wait_ge(sem("ay"), ib_ // 8 + i // 8)
                    for kt in range(key_tiles(its[i][0])):
                        c = slice(kt * 128, (kt + 1) * 128)
                        ins = TR(ps[:, AB + 2, c], pb[:, i % 2, c], ident)
                    ins.then_inc(sem("atr"), 1)

                def values(i):
                    qt, h = its[i]
                    pe.wait_ge(sem("apt"), ib_ + i + 1)
                    if h == 0 and i:
                        pe.wait_ge(sem("aob"), ib_ // 8 + i // 8)
                    for kt in range(key_tiles(qt)):
                        v = vm[:, kt, h * AV:(h + 1) * AV] if a == 0 else vg[:, kt, h // 4 * GD:(h // 4 + 1) * GD]
                        ins = M(ps[:, AB + 3, h * 64:(h + 1) * 64], pt[:, i % 2, kt, :], v, start=kt == 0,
                                stop=kt == key_tiles(qt) - 1)
                    ins.then_inc(sem("apv"), 1)

                def turn_output(n):
                    pe.wait_ge(sem("aob"), ib_ // 8 + n + 1)
                    for q in range(4):
                        ins = TR(ps[:, AB + 2, q * 128:(q + 1) * 128],
                                 ob[:, 2 * q:2 * q + 2, :].rearrange("p h e -> p (h e)"), ident)
                    ins.then_inc(sem("aot"), 1)

                scores(0)
                scores(1)
                for i, (qt, h) in enumerate(its):
                    turned(i)
                    if i + 2 < len(its):
                        scores(i + 2)
                    next(fill, None)
                    values(i)
                    if h == 0 and i:
                        turn_output(i // 8 - 1)
                turn_output(len(its) // 8 - 1)
                for _ in fill:
                    pass
                pe.wait_ge(sem("ay"), ib_ // 8 + len(its) // 8)

            def merge_steps(l, n):
                cq = first_col(l, True)
                for s_, (og, name, k) in enumerate(MERGE):
                    if has_unit(s_):
                        u0, g = plan[l, name, og, n]
                        b0 = banks(g) if k == 0 else bank(g)
                        rhs = (h_hi, h_lo) if name == "gate" else (y_hi[n], y_lo[n])
                        tiles4(b0, ready(u0 + k), (rhs[0][:, k, cq:T], rhs[1][:, k, cq:T]), T - cq,
                               k == 0, not has_unit(s_ + 1)).then_inc(unit_used, 1)
                    yield

            def finish(ins, g):
                ins.then_inc(unit_used, 1)

            pe.wait_ge(sem("tab_in"), 16)
            pe.wait_ge(sem("s_act"), 1)
            TR(ps[:, 0, 0:2 * KT], s_act[:, :], ident[0:2 * KT, 0:2 * KT]).then_inc(sem("x_t"), 1)
            pe.wait_ge(sem("x_in"), 16 * NT)
            for i in range(NT):
                b = 2 + 2 * (i % 2)
                if i >= 2:
                    pe.wait_ge(sem("x_ready"), i - 1)
                for k in range(KT):
                    ins = TR(ps[:, b + k // 4, k % 4 * 128:(k % 4 + 1) * 128], xin[:, i, k * 128:(k + 1) * 128], ident)
                ins.then_inc(sem("x_t"), 1)
            pe.wait_ge(sem("vectors_in"), 16 * VECTORS)
            for l in range(DEPTH):
                TR(ps[:, 6, l * P_ROWS:(l + 1) * P_ROWS], vrow[:, l, :], ident[0:P_ROWS, 0:P_ROWS])
                ins = TR(ps[:, 7, l * M_ROWS:(l + 1) * M_ROWS], mvrow[:, l, :], ident[0:M_ROWS, 0:M_ROWS])
            ins.then_inc(sem("vec_t"), 1)
            pe.wait_ge(sem("s4"), 1)
            pe.wait_ge(sem("x_ready"), NT)
            pe.wait_ge(sem("params"), 1)

            for l in range(DEPTH):
                cq = first_col(l, True)
                n_q = T - cq
                u0, g0 = plan[l, "mod"]

                def turn(b, j):
                    for q in range(4):
                        at = slice(j * 8 + 2 * q, j * 8 + 2 * q + 2) if isinstance(j, int) else bass.ds(j * 8 + 2 * q, 2)
                        ins = M(ps[:, 7, at], mrow[0:4, b, q * 128:(q + 1) * 128], tb("comb"),
                                start=True, stop=True)
                    return ins

                def mod_pair(u, g, j, it=None):
                    for b in range(2):
                        b0 = banks(g + b, it, 1)
                        for k in range(KT):
                            slot = ready(u + b * KT + k, it, 2 * KT)
                            M(ps[0:4, b0, :], s4[:, k, :], w_hi[:, slot, :], start=k == 0, stop=False)
                            M(ps[0:4, b0, :], s4[:, k, :], w_lo[:, slot, :], start=False,
                              stop=k == KT - 1).then_inc(unit_used, 1)
                    for b in range(2):
                        fs, fv = freed(g + b)
                        pe.wait_ge(fs, fv if it is None else fv + it)
                        turn(b, j + b).then_inc(sem("mod_t"), 1)

                all_free(g0)
                mod_pair(u0, g0, 0)
                with pe.Fori(0, 8) as i:
                    mod_pair(u0 + 2 * KT, g0 + 2, i * 2 + 2, i)
                norm_stats(l, 0, g0 + 18)
                ffn(l, 0)
                norm_stats(l, 1, plan[l, "q"][1])

                for name, c0 in (("q", cq), ("k", 0)):
                    g = plan[l, name][1]
                    finish(feature_group((l, name), g, c0, 3 * l + 1 if name == "q" else None), g)
                u0, g = plan[l, "v"]
                b0 = banks(g)
                for k in range(KT):
                    slot = ready(u0 + k)
                    for tt in range(NT):
                        c = slice(tt * 128, (tt + 1) * 128)
                        ins = passes(ps[:, b0 + tt, :], three((h_hi[:, k, c], h_lo[:, k, c]), weight(slot, 0, 512)),
                                     k == 0, k == KT - 1)
                    if k < KT - 1:
                        ins.then_inc(unit_used, 1)
                finish(ins, g)
                u0, g = plan[l, "cqkv"]
                b0 = banks(g)
                for k in range(KT):
                    slot = ready(u0 + k)
                    for m in range(3):
                        c0 = cq if m < 2 else 0
                        ins = passes(ps[:, b0 + m, 0:T - c0], three(weight(slot, m * 128, (m + 1) * 128), h_rhs(k, c0)),
                                     k == 0, k == KT - 1)
                    ins.then_inc(unit_used, 1)
                slot = ready(u0 + KT)
                for k in range(KT):
                    ins = passes(ps[0:ROPE, b0 + 3, :], three(weight(slot, k * ROPE, (k + 1) * ROPE), h_rhs(k, 0)),
                                 k == 0, k == KT - 1)
                finish(ins, g)
                u0, g = plan[l, "gates"]
                b0 = banks(g)
                slot = ready(u0)
                for k in range(KT):
                    ins = passes(ps[0:16, b0, :], three(weight(slot, k * 16, (k + 1) * 16), h_rhs(k, 0)),
                                 k == 0, k == KT - 1)
                finish(ins, g)

                all_free(plan[l, "o"][1])
                sel = tb("sel").rearrange("p (a n) -> p a n", n=36)
                back = gz[:, :].rearrange("p (s n) -> p s n", s=2)[:, :, ::-1]
                for b in range(2):
                    M(ps[0:36, b, :], sel[:, 2 * b, :], gz[:, :], start=True, stop=False)
                    ins = M(ps[0:36, b, :], sel[:, 2 * b + 1, :], back, start=False, stop=True)
                ins.then_inc(sem(f"sel_{l}"), 1)
                pe.wait_ge(sem(f"exprow_{l}"), 4)
                pe.wait_ge(sem(f"rown_{l}"), 2)
                for q in range(4):
                    for tt in range(NT):
                        TR(ps[:, 2 + q // 2, ((q % 2) * 4 + tt) * 36:((q % 2) * 4 + tt + 1) * 36],
                           RN[:, q, tt * 128:(tt + 1) * 128], ident[0:36, 0:36])
                for d in range(2):
                    for h in range(MH):
                        r = 32 * d + h
                        ins = M(ps[:, 4, (4 * d + h) * 4:(4 * d + h) * 4 + 4],
                                ident[0:36, r:r + 1].to_broadcast([36, 128]), dlog[:, :], start=True, stop=True)
                ins.then_inc(sem(f"tokt_{l}"), 1)

                t0 = cq // 128
                outs = [j for j in range(NT) if scan_tile(0, j) >= t0]
                pe.wait_ge(sem(f"tok_{l}"), 1)
                pe.wait_ge(sem(f"qk_{l}"), 2 * MH)
                for h in range(MH):
                    if h:
                        pe.wait_ge(sem(f"P_{l}"), 2 * h)
                        pe.wait_ge(sem(f"cupd_{l}"), 6 * h)
                        pe.wait_ge(sem(f"kw_{l}"), h)
                    q_h, k_h = qk[:, h, :], qk[:, MH + h, :]
                    for tt in range(t0, NT):
                        c = slice(tt * 128, (tt + 1) * 128)
                        M(ps[:, 0, c], k_h[:, c], q_h[:, c], start=True, stop=True)
                    for d in range(2):
                        r = 32 * d + h
                        M(ps[:, 1 + d, t0 * 128:], ident[0:36, r:r + 1].to_broadcast([36, 128]), RN[:, 4, t0 * 128:],
                          start=True, stop=True)
                    for tt in range(NT):
                        c = slice(tt * 128, (tt + 1) * 128)
                        ins = TR(ps[:, 3, c], k_h[:, c], ident)
                    ins.then_inc(sem(f"headmm_{l}"), 1)
                    pe.wait_ge(sem(f"P_{l}"), 2 * h + 2)
                    pe.wait_ge(sem(f"kw_{l}"), h + 1)
                    for j in range(NT):
                        for d in range(2):
                            tt = scan_tile(d, j)
                            c = slice(tt * 128, (tt + 1) * 128)
                            if j >= 1:
                                pe.wait_ge(sem(f"cupd_{l}"), 2 * (3 * h + j - 1) + d + 1)
                            if j in outs:
                                n = 2 * (len(outs) * h + outs.index(j)) + d
                                if n >= 2:
                                    pe.wait_ge(sem(f"hn_{l}"), n - 1)
                                ins = M(ps[:, 4 + d, 0:MD + 1], P_[:, d, tt, :], vaug[:, tt, h, :], start=True, stop=True)
                                if j >= 1:
                                    ins = M(ps[:, 6 + d, 0:MD + 1], q_h[:, c], C_[:, d, :], start=True, stop=True)
                                ins.then_inc(sem(f"nmm_{l}"), 1)
                            if j < NT - 1:
                                M(ps[:, 1 + d, 0:MD + 1], kw[:, d, tt, :], vaug[:, tt, h, :],
                                  start=True, stop=True).then_inc(sem(f"dcmm_{l}"), 1)
                pe.wait_ge(sem(f"hn_{l}"), 2 * len(outs) * MH)
                pe.wait_ge(sem(f"hout_{l}"), MH)
                g = plan[l, "o"][1]
                finish(feature_group((l, "o"), g, cq), g)
                for h in range(MH):
                    for tt in range(t0, NT):
                        ins = TR(ps[:, y0_bank(l, h), tt * 128:(tt + 1) * 128], hsn[:, h, tt, :], ident)
                    ins.then_inc(sem(f"ht_{l}"), 1)

                pe.wait_ge(sem(f"y0_{l}"), MH)
                pe.wait_ge(sem(f"csq_{l}"), 1)
                all_free(plan[l, "uq", 0][1])
                M(ps[:, 0, cq:T], tb("ones"), csq[:, 0, cq:T], start=True, stop=False)
                M(ps[:, 0, cq:T], tb("ones"), csq[:, 1, cq:T], start=False, stop=True)
                M(ps[:, 1, :], tb("ones"), csq[:, 2, :], start=True, stop=True).then_inc(sem(f"css_{l}"), 1)
                pe.wait_ge(sem(f"cn_lo_{l}"), 1)
                for half in range(2):
                    u0, g = plan[l, "uq", half]
                    b0 = banks(g)
                    for k in range(2):
                        ins = tiles4(b0, ready(u0 + k), (cn_hi[:, k, cq:T], cn_lo[:, k, cq:T]), n_q, k == 0, k == 1,
                                     4, AQK)
                        if k == 0:
                            ins.then_inc(unit_used, 1)
                    finish(ins, g)
                u0, g = plan[l, "kn"]
                b0 = banks(g)
                finish(tiles4(b0, ready(u0), (cn_hi[:, 2, :], cn_lo[:, 2, :]), T, True, True), g)
                u0, g = plan[l, "kv"]
                b0 = banks(g)
                slot = ready(u0)
                for tt in range(NT):
                    c = slice(tt * 128, (tt + 1) * 128)
                    ins = passes(ps[:, b0 + tt, :], three((cn_hi[:, 2, c], cn_lo[:, 2, c]), weight(slot, 0, 512)),
                                 True, True)
                finish(ins, g)
                qk_norm_attend(l, 0, plan[l, "kv"][1] + 1, merge_steps(l, 0))

                g = plan[l, "gq"][1]
                finish(feature_group((l, "gq"), g, cq), g)
                u0, g = plan[l, "gkv"]
                b0 = banks(g)
                for k in range(KT):
                    slot = ready(u0 + k)
                    passes(ps[:, b0, :], three(weight(slot, 0, 128), h_rhs(k, 0)), k == 0, k == KT - 1)
                    for tt in range(NT):
                        c = slice(tt * 128, (tt + 1) * 128)
                        ins = passes(ps[:, b0 + 1, c], three((h_hi[:, k, c], h_lo[:, k, c]), weight(slot, 128, 256)),
                                     k == 0 and tt == 0, k == KT - 1, skip_group_check=True)
                    if k < KT - 1:
                        ins.then_inc(unit_used, 1)
                finish(ins, g)
                qk_norm_attend(l, 1, g + 1, merge_steps(l, 1))

                for _ in merge_steps(l, 2):
                    pass
                u0, g0 = plan[l, "wout"]
                for og in range(2):
                    b0 = banks(g0 + og)
                    for k in range(KT):
                        if og == 0:
                            pe.wait_ge(sem("g"), 2 * l + k // 4 + 1)
                        ins = tiles4(b0, ready(u0 + og * KT + k), (g_hi[:, k, 0:n_q], g_lo[:, k, 0:n_q]), n_q,
                                     k == 0, k == KT - 1)
                        if k < KT - 1:
                            ins.then_inc(unit_used, 1)
                    finish(ins, g0 + og)
                norm_stats(l, 2, plan[l, "in", 1][1])
                ffn(l, 1)
            all_free(plan["end"][1])
            for i in range(2):
                for k in range(KT):
                    ins = TR(ps[:, 2 * i + k // 4, k % 4 * 128:(k % 4 + 1) * 128],
                             x[:, k, CTX + i * 128:CTX + (i + 1) * 128], ident)
                ins.then_inc(sem("out_t"), 1)





_INS = ["x", "c", "ctx", "c_ctx", "w_mod", "b_mod", "g_norm", "w_ffn_in", "w_ffn_out", "w_in", "b_mgate", "w_conv",
        "g_mhead", "g_cq", "g_ckv", "w_uq", "w_ukv", "g_q_mla", "g_k_mla", "g_q_gqa", "g_k_gqa", "w_branch", "w_out"]


def kernel(**inputs):
    import concourse.bacc as bacc
    from concourse.bass_utils import run_bass_kernel_spmd

    nc = bacc.Bacc("TRN2", target_bir_lowering=False, num_devices=1)
    arrays, t = {}, {}
    table, tab_at = tables()
    for name, a in [(n, np.ascontiguousarray(inputs[n])) for n in _INS] + [("tab", table)]:
        arrays[f"in_{name}"] = a
        t[name] = nc.dram_tensor(f"in_{name}", a.shape, mybir.dt.from_np(a.dtype), kind="ExternalInput").ap()
    out = nc.dram_tensor("out", (1, T - CTX, D), mybir.dt.float32, kind="ExternalOutput").ap()
    build(nc, t, out, tab_at)
    r = run_bass_kernel_spmd(nc, [arrays], core_ids=[0])
    return r.results[0]["out"]
```

```python
from contextlib import ExitStack

import concourse.bass as bass
import numpy as np
from concourse import mybir

D, T, DEPTH = 1024, 512, 2
CTX = 256
KT = D // 128
DFF = 2816
FT = DFF // 128
MH, MD, MW = 4, 128, 512
TAPS = 5
NT = T // 128
QR, KVR = 256, 128
AH, NOPE, ROPE, AV = 8, 64, 32, 64
AQK = NOPE + ROPE
GH, GKV, GD = 8, 2, 64
NBR, BW = 3, 512
EPS = 1e-6
THETA = 10000.0
GRID_W = 64
RING = 4
LOADS = 8
UNIT = 512
FILL = 0
AB = 4 * (1 - FILL)
NEG = -1e30
STATS = 2 * AH
CQ_, CK_, CV_, CO_ = 0, 512, 1024, 1536
CGATE = 2048
CCQ = CGATE + 4 * MH
CCKV = CCQ + QR
CKR = CCKV + KVR
CGQ = CKR + ROPE
CGK = CGQ + GH * GD
CGV = CGK + GKV * GD
CBG = CGV + GKV * GD
P_NORM, P_CONV = 0, 3 * KT
P_MH = P_CONV + TAPS * 2 * MH
P_CQ = P_MH + MH
P_CKV = P_CQ + QR // 128
P_QG, P_KG, P_QM, P_KM = P_CKV + 1, P_CKV + 2, P_CKV + 3, P_CKV + 4
P_ROWS = P_KM + 1
M_ROWS = 9 * KT
VECTORS = DEPTH * (5 + 6 + 1 + 4)


def tables():
    def rope(dim):
        quarter = dim // 4
        inv = np.float32(THETA) ** (-np.arange(quarter, dtype=np.float32) / np.float32(quarter))
        t = np.arange(T - CTX)
        rows, cols = (t // GRID_W).astype(np.float32), (t % GRID_W).astype(np.float32)
        ang = np.concatenate([rows[:, None] * inv, cols[:, None] * inv], -1).astype(np.float32)
        return np.cos(ang).T, np.sin(ang).T

    def full(dim, head, copies):
        c, s = rope(dim)
        half = dim // 2
        cos, sin = np.ones((head, T - CTX), np.float32), np.zeros((head, T - CTX), np.float32)
        cos[head - dim:] = np.concatenate([c, c])
        sin[head - dim:] = np.concatenate([s, s])
        rot = np.zeros((head, head), np.float32)
        for i in range(half):
            a, b = head - dim + i, head - half + i
            rot[b, a] = -1.0
            rot[a, b] = 1.0
        return (np.tile(cos, (copies, 1)), np.tile(sin, (copies, 1)),
                np.kron(np.eye(copies, dtype=np.float32), rot))

    parts = {}
    parts["ident"] = np.eye(128, dtype=np.float32)
    s, t = np.arange(128)[:, None], np.arange(128)[None, :]
    parts["mask"] = np.concatenate([np.where(s <= t, 0.0, NEG), np.where(s >= t, 0.0, NEG)], 1)
    parts["ones"] = np.ones((128, 128))
    parts["sum1"], parts["sum2"] = np.zeros((128, 2 * STATS - 1)), np.zeros((128, 2 * STATS - 2))
    parts["sum1"][:, STATS - 1] = 1
    parts["sum2"][0:64, STATS - 2] = parts["sum2"][64:128, STATS - 1] = 1
    parts["spread"] = np.kron(np.eye(GH + 2 * GKV), np.ones((1, GD)))
    parts["cosg"], parts["sing"], parts["rotg"] = full(GD, GD, 2)
    parts["cosm"], parts["sinm"], parts["rotm"] = full(ROPE, AQK, 1)
    sel = np.zeros((16, 4, 36))
    for h in range(MH):
        sel[h, 0, h] = sel[2 * MH + h, 1, 32 + h] = 1
        sel[MH + h, 2, h] = sel[3 * MH + h, 3, 32 + h] = 1
    parts["sel"] = sel.reshape(16, -1)
    parts["comb"] = np.array([[1, 0], [0, 1], [1, 0], [0, 1]])
    at, width = {}, 0
    for name, a in parts.items():
        at[name] = (width, a.shape[0], a.shape[1])
        width += a.shape[1]
    out = np.zeros((128, width), np.float32)
    for name, a in parts.items():
        w, r, c = at[name]
        out[:r, w:w + c] = a
    return out, at


MODS = 9 * D // UNIT
EDGE, LOOPS = 3, 2
assert 2 * EDGE + LOOPS * LOADS == FT


FIRST_MODS = 3 * D // UNIT


def beside(l, f, g):
    if l == 0 and f == 0:
        n = (MODS - FIRST_MODS) // (2 * LOOPS)
        return n, FIRST_MODS + g * LOOPS * n, l
    if f == 1 and l < DEPTH - 1:
        return 3, g * LOOPS * 3, l + 1
    if l > 0 and f == 0:
        n = (MODS - 2 * LOOPS * 3) // LOOPS
        return (2, 2 * LOOPS * 3, l) if g == 0 else (n - 2, 2 * LOOPS * 3 + LOOPS * 2, l)
    return 0, 0, l


def turn_units(groups):
    out, each = [], groups * KT // LOADS
    for c in range(LOADS):
        units = [divmod(u, KT) for u in range(c * each, (c + 1) * each)]
        out += units + ["ffn"] + ["turn"] * any(k == KT - 1 for _, k in units)
    return out


def make_plan():
    plan, size, ends, place = {}, [], [], []

    def add(key, units, n_groups=1, width=UNIT, where=None):
        plan[key] = (len(size), len(ends))
        for _ in range(n_groups):
            size.extend([width] * (units // n_groups))
            ends.append(len(size))
            half = where if where is not None else 1 - place[-1][0] if place else 0
            place.append((half, sum(p[0] == half for p in place)))

    def merge(l, n, where=None):
        for og in range(2):
            add((l, "gate", og, n), KT, where=where)
            add((l, "branch", og, n), BW // 128, where=where)

    for l in range(DEPTH):
        if l == 0:
            add((l, "mod"), FIRST_MODS * KT, FIRST_MODS)
        add((l, "in", 0), FT // 2 * KT, FT // 2)
        add((l, "out", 0), FT + LOOPS * KT * beside(l, 0, 0)[0])
        add((l, "out's other half", 0), FT + LOOPS * KT * beside(l, 0, 1)[0])
        for name in ("q", "k", "v"):
            add((l, name), KT)
        add((l, "gates"), 1, 1, KT * 4 * MH)
        assert place[-1][0] == 0
        add((l, "cqkv"), KT, 1, QR + KVR)
        size.append(KT * ROPE)
        ends[-1] += 1
        add((l, "o"), KT, where=1)
        add((l, "uq", 0), 2, 1, 4 * AQK)
        add((l, "uq", 1), 2, 1, 4 * AQK)
        add((l, "kn"), 1)
        add((l, "kv"), 1)
        merge(l, 0, FILL)
        add((l, "gq"), KT)
        add((l, "gkv"), KT, 1, 2 * GKV * GD)
        merge(l, 1, FILL)
        merge(l, 2)
        add((l, "wout"), 2 * KT, 2)
        add((l, "in", 1), FT // 2 * KT, FT // 2)
        add((l, "out", 1), FT + LOOPS * KT * beside(l, 1, 0)[0])
        add((l, "out's other half", 1), FT + LOOPS * KT * beside(l, 1, 1)[0])
    plan["end"] = (len(size), len(ends))
    return plan, size, ends, place


MERGE = [(og, name, k) for og in range(2)
         for name, units in (("gate", KT), ("gates out", 2), ("branch", BW // 128), ("branch out", 2))
         for k in range(units)]


def has_unit(step):
    return 0 <= step < len(MERGE) and "out" not in MERGE[step][1]


def build(nc, t, out, tab_at):
    fp32, f32r = mybir.dt.float32, mybir.dt.float32r
    ALU, ACT, AX = mybir.AluOpType, mybir.ActivationFunctionType, mybir.AxisListType
    plan, size, ends, place = make_plan()
    U = len(size)
    ctx = ExitStack()

    with ctx:
        def sb(name, shape, dt=fp32, where=ctx):
            return where.enter_context(nc.sbuf_tensor(name, shape, dt))

        sems = {}

        def sem(name):
            if name not in sems:
                sems[name] = ctx.enter_context(nc.semaphore(name))
            return sems[name]

        x = sb("x", [128, KT, T])
        h_hi = sb("h_hi", [128, KT, T], f32r)
        h_lo = sb("h_lo", [128, KT, T], f32r)
        w_raw = sb("w_raw", [128, LOADS, UNIT])
        w_hi = sb("w_hi", [128, RING, UNIT], f32r)
        w_lo = sb("w_lo", [128, RING, UNIT], f32r)
        tab = sb("tab", [128, t["tab"].shape[1]])
        cst = sb("cst", [128, 3])
        prm = sb("prm", [128, DEPTH, P_ROWS])
        bmod = sb("bmod", [128, DEPTH, M_ROWS])
        bgate = sb("bgate", [36, DEPTH, 2])
        mod = sb("mod", [128, 9, KT, 2])
        modt = sb("modt", [128, M_ROWS, 2])
        gain = sb("gain", [128, 3, KT, 2])
        crm = sb("crm", [128, 2, NT])
        rms = sb("rms", [128, NT])
        s_in = sb("s_in", [2 * KT, 128])
        s_act = sb("s_act", [2 * KT, 128])
        s_fm = sb("s_fm", [128, 2 * KT])
        s4 = sb("s4", [128, KT, 4], f32r)

        y0h = y0l = None
        big = ExitStack()

        def region(stack, specs):
            return [sb(n, s, d, stack) for n, s, d in specs]

        sq, acc, t1, hn, mid_hi, mid_lo = region(big, [
            ("sq", [128, 2, T], fp32), ("acc", [128, T], fp32), ("t1", [128, 2, T], fp32), ("hn", [128, 2, T], fp32),
            ("mid_hi", [128, FT, T], f32r), ("mid_lo", [128, FT, T], f32r)])
        sil, mt, mrow = sq, t1, hn
        big.close()
        big = ExitStack()
        _, xin, vrow, mvrow = region(big, [("beside_hn", [128, 7, T], fp32), ("xin", [128, NT, D], fp32), ("vrow", [P_ROWS, DEPTH, 128], fp32),
                                        ("mvrow", [M_ROWS, DEPTH, 128], fp32)])
        big.close()
        big = ExitStack()
        xout, = region(big, [("xout", [128, 2, D], fp32)])
        big.close()
        mix = ExitStack()
        y_hi, y_lo = [None] * 3, [None] * 3
        y_hi[0], y_lo[0], craw, krs = region(mix, [("y0h", [128, MH, T], f32r), ("y0l", [128, MH, T], f32r),
                                                   ("craw", [128, 3, T], fp32), ("krs", [128, T], fp32)])
        s1 = ExitStack()
        R, tok, dec, mprev, dlog, rn, vaug, RN, hsn, qk = region(s1, [
            ("R", [128, 6, T], fp32), ("tok", [128, 16, 36], fp32), ("dec", [128, 8, 4], fp32),
            ("mprev", [36, 5], fp32), ("dlog", [36, 4], fp32), ("rn", [128, MH, NT], fp32),
            ("vaug", [128, NT, MH, MD + 1], fp32), ("RN", [36, 5, T], fp32), ("hsn", [128, MH, NT, MD], fp32),
            ("qk", [128, 2 * MH, T], fp32)])
        sigo, yt = R[:, 0:MH, :], R[:, MH:6, :]
        s2 = ExitStack()
        cpad, cacc, gz, csq = region(s2, [("cpad", [128, 4, 2, CTX + 4], fp32), ("cacc", [128, 2, 2, CTX], fp32),
                                          ("gz", [16, T], fp32), ("csq", [128, 3, T], fp32)])
        s2.close()
        s2 = ExitStack()
        dt_, P_, kw, HN, an, C_, sqt, dn = region(s2, [
            ("dt_", [128, 2, NT, 128], fp32), ("P_", [128, 2, NT, 128], fp32), ("kw", [128, 2, NT, 128], fp32),
            ("HN", [128, 2, NT, MD + 1], fp32), ("an", [128, 2, MD + 1], fp32), ("C_", [128, 2, MD + 1], fp32),
            ("sqt", [128, NT, MD], fp32), ("dn", [128, 2, 4], fp32)])
        s2.close()
        s1.close()
        y_hi[1], y_lo[1] = region(mix, [("y1h", [128, 4, T], f32r), ("y1l", [128, 4, T], f32r)])
        s1 = ExitStack()
        cn_hi, cn_lo = region(s1, [("cn_hi", [128, 3, T], f32r), ("cn_lo", [128, 3, T], f32r)])
        s1.close()
        mg, sg = region(mix, [("mg", [128, KT, T], fp32), ("sg", [128, 4, T], fp32)])

        def attention_scratch(stack, k):
            two = ExitStack()
            nsq, nrm = region(two, [(f"nsq{k}", [128, 2, T], fp32), (f"nrm{k}", [STATS, T], fp32)])
            two.close()
            rotated = [craw[:, i, :].rearrange("p (a n) -> p a n", a=2) for i in range(3)]
            pb, pt, mx, rs = region(stack, [
                (f"pb{k}", [128, 2, T], fp32), (f"pt{k}", [128, 2, NT, 128], fp32),
                (f"mx{k}", [128, 2, 2], fp32), (f"rs{k}", [128, 2, 8], fp32)])
            ob = krs[:, :].rearrange("p (h e) -> p h e", h=8)
            return [nsq, nrm, *rotated, pb, pt, ob, mx, rs]

        s1 = ExitStack()
        k96, q96, vm = region(s1, [("k96", [AQK, AH, T], fp32), ("q96", [AQK, AH, T], fp32),
                                   ("vm", [128, NT, AH * AV], fp32)])
        scr = [attention_scratch(s1, 0)]
        s1.close()
        s1 = ExitStack()
        y_hi[2], y_lo[2] = region(mix, [("y2h", [128, 4, T], f32r), ("y2l", [128, 4, T], f32r)])
        qg, kg, vg = region(s1, [("qg", [128, 4, T], fp32), ("kg", [128, GKV, T], fp32), ("vg", [128, NT, 128], fp32)])
        scr.append(attention_scratch(s1, 1))
        s1.close()
        s1 = ExitStack()
        g_hi, g_lo = region(s1, [("g_hi", [128, KT, T], f32r), ("g_lo", [128, KT, T], f32r)])
        s1.close()
        mix.close()

        ps = ctx.enter_context(nc.psum_tensor("ps", [128, 8, 512], fp32))

        def tb(name, rows=None):
            w, r, c = tab_at[name]
            return tab[0:r, w:w + c]

        ident = tb("ident")

        landed = [sem(f"landed{i}") for i in range(LOADS)]
        hi_done, lo_done = sem("hi_done"), sem("lo_done")
        unit_used = sem("unit_used")
        banks_free = [sem("banks_free0"), sem("banks_free1")]

        def freed(g):
            return banks_free[place[g][0]], place[g][1] + 1

        def bank(g):
            return 4 * place[g][0]

        def last_groups(g):
            return [max(b for b in range(g) if place[b][0] == half) for half in range(2)
                    if any(place[b][0] == half for b in range(g))]

        def norm_group(l, j):
            return plan[(l, "q") if j == 1 else (l, "in", j // 2)][1]

        def norm_banks(l, j):
            b = bank(norm_group(l, j))
            return b, 5 - b

        def first_col(l, only_latent):
            return CTX if l == DEPTH - 1 and only_latent else 0

        def streams(c0):
            return [(s, a, b) for s, a, b in ((1, 0, CTX), (0, CTX, T)) if a >= c0]

        class Chain:

            def __init__(self, eng, name):
                self.eng, self.order, self.counts = eng, sem(name), {}

            def __call__(self, ins, name=None):
                s = sem(name) if name else self.order
                key = name or "order"
                self.counts[key] = self.counts.get(key, 0) + 1
                ins.then_inc(s, 1)
                self.eng.wait_ge(s, self.counts[key])

        def scan_tile(d, j):
            return j if d == 0 else (1, 0, 3, 2)[j]

        def rope_setup(l, a):
            nsq, nrm, nxn, nco, nsi = scr[a][:5]
            cq = first_col(l, True)
            if a == 0:
                tiles = [(k96[:, h, :], 0, P_KM) for h in range(AH)] + [(q96[:, h, :], cq, P_QM) for h in range(AH)]
                return AQK, nxn, nco, nsi, tb("cosm"), tiles
            tiles = [(kg[:, i, :], 0, P_KG) for i in range(GKV)] + [(qg[:, i, :], cq, P_QG) for i in range(4)]
            return 128, nxn, nco, nsi, tb("cosg"), tiles

        def items(l):
            return [(qt, h) for qt in range(first_col(l, True) // 128, NT) for h in range(8)]

        def before(l, a):
            tiles = l * (2 * AH + 4 + GKV) + a * 2 * AH
            return tiles, sum(2 * len(items(p)) for p in range(l)) + a * len(items(l))

        def fill_beside_tile(i):
            return i % 2 == 0

        def fill_beside_item(l, a, i):
            tiles = len(rope_setup(l, a)[5])
            left = len(MERGE) - (tiles // 4 + 2 + (tiles + 1) // 2)
            n = len(items(l))
            return (i + 1) * left // n > i * left // n

        def key_tiles(qt):
            return 2 if qt < 2 else NT

        def y0_bank(l, h):
            return 4 - bank(plan[l, "uq", 0][1]) + h

        block = ctx.enter_context(nc.Block())

        @block.sync
        def _(sp):
            sp.dma_start(tab[:, :], t["tab"]).then_inc(sem("tab_in"), 16)
            sp.dma_start(s_in[0:KT, :], t["c"].rearrange("b (k p) -> (b k) p", p=128)).then_inc(sem("s_in"), 16)
            sp.dma_start(s_in[KT:2 * KT, :], t["c_ctx"].rearrange("(k p) -> k p", p=128)).then_inc(sem("s_in"), 16)

            def unit(u, src, shape=None, it=None, per=0):
                if u >= LOADS:
                    need = u - LOADS + 1
                    sp.wait_ge(lo_done, need if it is None else need + it * per)
                n = size[u]
                dst = w_raw[:, u % LOADS, 0:n]
                if shape:
                    dst = dst.rearrange(shape[0], **shape[1])
                sp.dma_start(dst, src).then_inc(landed[u % LOADS], 16)

            def ffn_loads(l, f):
                u0, _ = plan[l, "in", f]
                w = t["w_ffn_in"][l, f].rearrange("k (s n) -> k s n", s=2)
                with sp.Fori(0, FT // 2) as g:
                    for k in range(KT):
                        unit(u0 + k, w[k * 128:(k + 1) * 128, :, bass.ds(g * 256, 256)],
                             ("p (s n) -> p s n", {"s": 2}), g, KT)
                u0, _ = plan[l, "out", f]
                w = t["w_ffn_out"][l, f].rearrange("(k p) n -> p k n", p=128)
                at = u0
                for g in range(2):
                    groups, first, ml = beside(l, f, g)
                    cols = slice(g * 512, g * 512 + 512)
                    for k in range(EDGE):
                        unit(at + k, w[:, k, cols])
                    at += EDGE
                    with sp.Fori(0, LOOPS) as i:
                        n = [s_ for s_ in turn_units(groups) if s_ != "turn"]
                        ffn_before = 0
                        for j, what in enumerate(n):
                            if what == "ffn":
                                unit(at + j, w[:, bass.ds(i * LOADS + (EDGE + ffn_before), 1), cols],
                                     ("p (a n) -> p a n", {"a": 1}), i, len(n))
                                ffn_before += 1
                            else:
                                m, k = what
                                col = (first + m) * UNIT
                                unit(at + j, t["w_mod"][ml, k * 128:(k + 1) * 128,
                                                        bass.ds(i * (groups * UNIT) + col, UNIT)], None, i, len(n))
                    at += LOOPS * len(n)
                    for k in range(EDGE):
                        unit(at + k, w[:, FT - EDGE + k, cols])
                    at += EDGE

            def in_units(l, key, col, width, **kw_):
                u0, _ = plan[(l,) + key]
                for k in range(KT):
                    unit(u0 + k, t["w_in"][l, k * 128:(k + 1) * 128, col:col + width], **kw_)

            def merge_loads(l, n):
                for og in range(2):
                    in_units(l, ("gate", og, n), CBG + n * D + og * 512, 512)
                    for k in range(BW // 128):
                        unit(plan[l, "branch", og, n][0] + k,
                             t["w_branch"][l, n, k * 128:(k + 1) * 128, og * 512:og * 512 + 512])

            for l in range(DEPTH):
                if l == 0:
                    u0, _ = plan[l, "mod"]
                    for k in range(KT):
                        unit(u0 + k, t["w_mod"][l, k * 128:(k + 1) * 128, 0:UNIT])
                    with sp.Fori(0, FIRST_MODS - 1) as g:
                        for k in range(KT):
                            unit(u0 + KT + k, t["w_mod"][l, k * 128:(k + 1) * 128, bass.ds(g * UNIT + UNIT, UNIT)],
                                 None, g, KT)
                ffn_loads(l, 0)
                in_units(l, ("q",), CQ_, 512)
                in_units(l, ("k",), CK_, 512)
                in_units(l, ("v",), CV_, 512)
                by_k = t["w_in"][l].rearrange("(k p) n -> p k n", p=128)
                unit(plan[l, "gates"][0], by_k[:, :, CGATE:CGATE + 4 * MH], ("p (k n) -> p k n", {"k": KT}))
                in_units(l, ("cqkv",), CCQ, QR + KVR)
                unit(plan[l, "cqkv"][0] + KT, by_k[:, :, CKR:CKR + ROPE], ("p (k n) -> p k n", {"k": KT}))
                in_units(l, ("o",), CO_, 512)
                for half in range(2):
                    for k in range(2):
                        unit(plan[l, "uq", half][0] + k,
                             t["w_uq"][l, k * 128:(k + 1) * 128, half * 4 * AQK:(half + 1) * 4 * AQK])
                kvw = t["w_ukv"][l].rearrange("k (h s e) -> k s h e", h=AH, s=2)
                unit(plan[l, "kn"][0], kvw[:, 0], ("p (h e) -> p h e", {"h": AH}))
                unit(plan[l, "kv"][0], kvw[:, 1], ("p (h e) -> p h e", {"h": AH}))
                merge_loads(l, 0)
                in_units(l, ("gq",), CGQ, 512)
                in_units(l, ("gkv",), CGK, 2 * GKV * GD)
                merge_loads(l, 1)
                merge_loads(l, 2)
                for og in range(2):
                    for k in range(KT):
                        unit(plan[l, "wout"][0] + og * KT + k,
                             t["w_out"][l, k * 128:(k + 1) * 128, og * 512:og * 512 + 512])
                ffn_loads(l, 1)
            for i in range(2):
                sp.wait_ge(sem("out_ready"), 2 * (i + 1))
                sp.dma_start(out[0, i * 128:(i + 1) * 128, :], xout[:, i, :]).then_inc(sem("stored"), 16)
            sp.wait_ge(sem("stored"), 32)

        @block.gpsimd
        def _(pool):
            link = Chain(pool, "pool_order")
            link(nc.gpsimd.memset(vrow[:, :, :], 0.0))
            link(nc.gpsimd.memset(bgate[:, :, :], 0.0))
            vec = sem("vectors_in")
            for i in range(2):
                pool.dma_start(xin[:, i, :], t["ctx"][0, i * 128:(i + 1) * 128, :]).then_inc(sem("x_in"), 16)
                pool.dma_start(xin[:, 2 + i, :], t["x"][0, i * 128:(i + 1) * 128, :]).then_inc(sem("x_in"), 16)
            n = 0
            for l in range(DEPTH):
                for row, src in (
                    (P_NORM, t["g_norm"][l].rearrange("j (k p) -> (j k) p", p=128)),
                    (P_CONV, t["w_conv"][l].rearrange("j o (k p) -> (j o k) p", p=128)),
                    (P_MH, t["g_mhead"][l].rearrange("(k p) -> k p", p=128)),
                    (P_CQ, t["g_cq"][l].rearrange("(k p) -> k p", p=128)),
                    (P_CKV, t["g_ckv"][l].rearrange("(k p) -> k p", p=128)),
                ):
                    pool.dma_start(vrow[row:row + src.shape[0], l, :], src).then_inc(vec, 16)
                    n += 1
                for row, name, width, copies in ((P_QG, "g_q_gqa", GD, 2), (P_KG, "g_k_gqa", GD, 2),
                                                 (P_QM, "g_q_mla", AQK, 1), (P_KM, "g_k_mla", AQK, 1)):
                    for c in range(copies):
                        pool.dma_start(vrow[row:row + 1, l, c * width:(c + 1) * width],
                                       t[name][l].rearrange("(a n) -> a n", a=1)).then_inc(vec, 16)
                        n += 1
                pool.dma_start(mvrow[:, l, :], t["b_mod"][l].rearrange("(k p) -> k p", p=128)).then_inc(vec, 16)
                n += 1
                for q in range(4):
                    at = 32 * (q // 2)
                    pool.dma_start(bgate[at:at + MH, l, q % 2:q % 2 + 1],
                                   t["b_mgate"][l, q].rearrange("(h a) -> h a", a=1)).then_inc(vec, 16)
                    n += 1
            assert n == VECTORS

            for l in range(DEPTH):
                pool.wait_ge(*freed(plan[l, "out", 0][1] + 1))
                link(nc.gpsimd.memset(RN[:, :, :], 0.0))
                link(nc.gpsimd.memset(vaug[:, :, :, MD:MD + 1], 1.0), f"mixer_filled_{l}")
                pool.wait_ge(sem(f"ht_{l}"), MH)
                link(nc.gpsimd.tensor_copy(k96[NOPE:AQK, :, :],
                                           krs[NOPE:AQK, :].rearrange("p (a n) -> p a n", a=1)
                                           .to_broadcast([ROPE, AH, T])), f"kr_spread_{l}")
                for a in (0, 1):
                    P, xn, co, si, cos, tiles = rope_setup(l, a)
                    for i, (dst, c0, _) in enumerate(tiles):
                        tb_, ib_ = before(l, a)
                        pool.wait_ge(sem("qn"), tb_ + i + 1)
                        nc.gpsimd.tensor_tensor(co[0:P, i % 2, :], xn[0:P, i % 2, :], cos,
                                                ALU.mult).then_inc(sem("qcos"), 1)
                        pool.wait_ge(sem("qcos"), tb_ + i + 1)
                        pool.wait_ge(sem("qsin"), tb_ + i + 1)
                        nc.gpsimd.tensor_tensor(dst[:, CTX:T], co[0:P, i % 2, :], si[0:P, i % 2, :],
                                                ALU.add).then_inc(sem("qk_final"), 1)
                        pool.wait_ge(sem("qk_final"), tb_ + i + 1)
                n_q = T - first_col(l, True)
                for og in range(2):
                    pool.wait_ge(*freed(plan[l, "branch", og, 1][1]))
                    nc.gpsimd.tensor_tensor(mg[:, og * 4:og * 4 + 4, 0:n_q], mg[:, og * 4:og * 4 + 4, 0:n_q],
                                            sg[:, :, 0:n_q], ALU.add).then_inc(sem("summed_1"), 1)

        @block.scalar
        def _(act):
            A = nc.scalar.activation
            link = Chain(act, "act_order")
            pos = [0]

            def split(u, it=None, per=0):
                off = (lambda v, m: v if it is None else v + it * m)
                act.wait_ge(landed[u % LOADS], off(16 * (u // LOADS + 1), 16 * per // LOADS))
                if u >= RING:
                    act.wait_ge(unit_used, off(u - RING + 1, per))
                n = size[u]
                A(w_hi[:, u % RING, 0:n], w_raw[:, u % LOADS, 0:n], ACT.Copy).then_inc(hi_done, 1)

            def advance(n):
                for _ in range(n):
                    if pos[0] < U:
                        split(pos[0])
                    pos[0] += 1

            def wait_group(g, it=None, per=0):
                act.wait_ge(unit_used, ends[g] if it is None else ends[g] + it * (per * KT))

            def squares(l, j, tiles):
                m_ = 3 * l + j
                c0 = first_col(l, j == 2)
                g_prev = None if m_ == 0 else plan[(l - 1, "out", 1) if j == 0 else (l, "out", 0) if j == 1 else
                                                   (l, "wout")][1]
                for i in tiles:
                    if g_prev is None:
                        act.wait_ge(sem("x_ready"), NT)
                    elif i % 4 < 3:
                        act.wait_ge(sem("x_new"), 6 * (m_ - 1) + 3 * (i // 4) + i % 4 + 1)
                    else:
                        act.wait_ge(*freed(g_prev + i // 4))
                    if i >= 3:
                        act.wait_ge(sem("sq_added"), (KT - 1) * m_ + i - 2)
                    dst = acc[:, c0:T] if i == 0 else sq[:, i % 2, c0:T]
                    A(dst, x[:, i, c0:T], ACT.Square).then_inc(sem("sq"), 1)

            def norm(l, j):
                m_ = 3 * l + j
                c0 = first_col(l, j == 2)
                act.wait_ge(sem("ss"), m_ + 1)
                A(rms[:, c0 // 128:NT], ps[:, norm_banks(l, j)[0], c0 // 128:NT], ACT.Sqrt, bias=cst[:, 0:1],
                  scale=1.0 / D).then_inc(sem("rms"), 1)
                if m_:
                    advance(1)
                for i in range(KT):
                    act.wait_ge(sem("scaled"), KT * m_ + i + 1)
                    if i >= 2:
                        act.wait_ge(sem("h"), KT * m_ + i - 1)
                    for s, a, b in streams(c0):
                        ins = A(hn[:, i % 2, a:b], t1[:, i % 2, a:b], ACT.Identity, bias=mod[:, 3 * j, i, s:s + 1])
                    ins.then_inc(sem("hn"), 1)
                    act.wait_ge(sem("hn"), KT * m_ + i + 1)
                    A(h_hi[:, i, c0:T], hn[:, i % 2, c0:T], ACT.Copy).then_inc(sem("h_hi"), 1)

            def ffn(l, f):
                done = FT // 2 * (2 * l + f)
                c0 = first_col(l, f == 1)
                n = T - c0
                u0, g0 = plan[l, "in", f]
                after = (l, 1) if f == 0 else (l + 1, 0) if l < DEPTH - 1 else None

                def evac(b, g, it=None):
                    wait_group(g0 + b, it, 2)
                    s4_ = bank(g0 + b)
                    A(sil[:, :, 0:n], ps[:, s4_:s4_ + 2, 0:n], ACT.Silu).then_inc(sem("sil"), 1)
                    fs, fv = freed(g0 + b)
                    act.wait_ge(fs, fv if it is None else fv + it)
                    A(mid_hi[:, bass.ds(2 * g, 2) if it is not None else slice(2 * g, 2 * g + 2), 0:n],
                      mt[:, :, 0:n], ACT.Copy).then_inc(sem("mid_hi"), 1)

                advance(KT)
                evac(0, 0)
                with act.Fori(0, FT // 4) as i:
                    for b in (1, 2):
                        for j in range(KT):
                            split(pos[0] + (b - 1) * KT + j, i, 2 * KT)
                        evac(b, i * 2 + b, i)
                pos[0] += 2 * KT * (FT // 4)
                _, g0 = plan[l, "out", f]
                for g in range(2):
                    groups = beside(l, f, g)[0]
                    last = (l, f, g) == (DEPTH - 1, 1, 1)
                    per = LOADS + groups * KT
                    advance(EDGE)
                    with act.Fori(0, LOOPS - last) as i:
                        j = 0
                        for what in turn_units(groups):
                            if what == "turn":
                                continue
                            split(pos[0] + j, i, per)
                            j += 1
                            if what != "ffn" and what[1] == KT - 1:
                                act.wait_ge(unit_used, pos[0] - RING + j + i * per)
                                A(mrow[0:4, 0, :], ps[0:4, 4 - bank(g0 + g) + what[0] % 2, :], ACT.Copy).then_inc(sem("mod_rows"), 1)
                    pos[0] += (LOOPS - last) * per
                    if after and g == 1:
                        squares(*after, range(4))
                    advance(EDGE + last * per - (after is not None and g == 1))

            def qk_norm(l, a, fill):
                P, xn, co, si, cos, tiles = rope_setup(l, a)
                nsq, nrm = scr[a][:2]
                tb_, ib_ = before(l, a)
                per, rows = (AQK, STATS) if a == 0 else (GD, 2 * len(tiles))
                if a == 0:
                    act.wait_ge(sem(f"kr_spread_{l}"), 1)
                for i, (dst, c0, _) in enumerate(tiles):
                    if i >= 2:
                        act.wait_ge(sem("qss"), tb_ + i - 1)
                    A(nsq[0:P, i % 2, c0:T], dst[:, c0:T], ACT.Square).then_inc(sem("qsq"), 1)
                    if i % 4 == 3:
                        next(fill, None)
                act.wait_ge(sem("qss"), tb_ + len(tiles))
                A(nrm[0:rows, :], ps[0:rows, AB, :], ACT.Sqrt, bias=cst[0:rows, 0:1],
                  scale=1.0 / per).then_inc(sem("qrms"), 1)
                next(fill, None)
                next(fill, None)
                for i in range(len(tiles)):
                    if fill_beside_tile(i):
                        next(fill, None)

            def attention(l, a, fill):
                pb, pt, ob, mx, rs = scr[a][5:]
                tb_, ib_ = before(l, a)
                scale = (AQK if a == 0 else GD) ** -0.5
                its = items(l)

                def weights(i):
                    qt, h = its[i]
                    n = key_tiles(qt) * 128
                    act.wait_ge(sem("amax"), ib_ + i + 1)
                    A(pb[:, i % 2, 0:n], ps[:, AB + i % 2, 0:n], ACT.Exp, bias=mx[:, i % 2, 1:2], scale=scale,
                      accum_out=rs[:, qt % 2, h:h + 1]).then_inc(sem("aexp"), 1)

                def output(qt, n):
                    act.wait_ge(sem("aot"), ib_ // 8 + n + 1)
                    A(y_hi[1 + a][:, :, qt * 128:(qt + 1) * 128],
                      ps[:, AB + 2, :].rearrange("p (k n) -> p k n", n=128), ACT.Copy).then_inc(sem("ayh"), 1)

                weights(0)
                weights(1)
                for i, (qt, h) in enumerate(its):
                    if i + 2 < len(its):
                        weights(i + 2)
                    if fill_beside_item(l, a, i):
                        next(fill, None)
                    if h == 0 and i:
                        output(qt - 1, i // 8 - 1)
                output(its[-1][0], len(its) // 8 - 1)

            def merge_steps(l, n):
                n_q = T - first_col(l, True)
                for s_, (og, name, k) in enumerate(MERGE):
                    if has_unit(s_ - 1):
                        advance(1)
                    if name == "gates out":
                        g = plan[l, "gate", og, n][1]
                        if k == 0:
                            wait_group(g)
                            if (n, og) in ((0, 1), (1, 0)):
                                act.wait_ge(*freed(plan[l, "branch", 1 - og, 0][1]))
                            elif n and (n, og) != (2, 1):
                                act.wait_ge(sem("summed_1"), 2 * l + 1 + (n == 2))
                            elif n:
                                act.wait_ge(sem("summed_2"), 2 * l + 1)
                        ins = A(sg[:, 2 * k:2 * k + 2, 0:n_q], ps[:, bank(g) + 2 * k:bank(g) + 2 * k + 2, 0:n_q],
                                ACT.Sigmoid)
                        ins.then_inc(sem("half_gates") if k == 0 else banks_free[place[g][0]], 1)
                    if n == NBR - 1 and (og, name, k) == (1, "gate", 3):
                        merged(l, 0, n_q)
                    yield
                if n == NBR - 1:
                    merged(l, 1, n_q)

            def merged(l, og, n_q):
                act.wait_ge(sem("summed_2"), 2 * l + 1 + og)
                A(g_hi[:, og * 4:og * 4 + 4, 0:n_q], mg[:, og * 4:og * 4 + 4, 0:n_q], ACT.Copy).then_inc(sem("g_hi"), 1)

            act.wait_ge(sem("cst"), 1)
            act.wait_ge(sem("s_in"), 32)
            A(s_act[:, :], s_in[:, :], ACT.Silu).then_inc(sem("s_act"), 1)
            act.wait_ge(sem("x_t"), 1)
            A(s_fm[:, :], ps[:, 0, 0:2 * KT], ACT.Copy).then_inc(sem("s_fm"), 1)
            act.wait_ge(sem("s_fm"), 1)
            A(s4[:, :, 0:2].rearrange("p k s -> p s k"), s_fm[:, :].rearrange("p (s k) -> p s k", s=2),
              ACT.Copy).then_inc(sem("s_hi"), 1)
            advance(RING)

            def x_start():
                for i in range(NT):
                    act.wait_ge(sem("x_t"), 2 + i)
                    b = 2 if i % 2 == 0 else 5
                    A(x[:, :, i * 128:(i + 1) * 128], ps[:, b:b + 2, :].rearrange("p a (k n) -> p (a k) n", n=128),
                      ACT.Copy).then_inc(sem("x_ready"), 1)

            for l in range(DEPTH):
                if l == 0:
                    _, g0 = plan[l, "mod"]

                    def mod_rows(it=None):
                        for b in range(2):
                            for j in range(KT):
                                split(pos[0] + b * KT + j, it, 2 * KT)
                            wait_group(g0 + 2 * (it is not None) + b, it, 2)
                            A(mrow[0:4, b, :], ps[0:4, bank(g0 + b), :],
                              ACT.Copy).then_inc(banks_free[place[g0 + b][0]], 1)

                    mod_rows()
                    pos[0] += 2 * KT
                    x_start()
                    squares(l, 0, range(KT))
                    with act.Fori(0, FIRST_MODS // 2 - 1) as i:
                        mod_rows(i)
                    pos[0] += (FIRST_MODS - 2) * KT
                else:
                    squares(l, 0, range(4, KT))
                norm(l, 0)
                ffn(l, 0)
                squares(l, 1, range(4, KT))
                norm(l, 1)

                cq = first_col(l, True)
                act.wait_ge(sem(f"pads_{l}"), 1)
                for part, name in enumerate(("q", "k")):
                    c0 = cq if part == 0 else 0
                    s0 = c0 // CTX
                    advance(KT if part == 0 else KT - 4)
                    g = plan[l, name][1]
                    wait_group(g)
                    for i in range(4):
                        if part == 1:
                            act.wait_ge(sem(f"conv_{l}"), i + 1)
                        ins = A(cpad[:, i, s0:2, 2:2 + CTX],
                                ps[:, bank(g) + i, 0:T - c0].rearrange("p (s n) -> p s n", n=CTX), ACT.Copy)
                        ins.then_inc(banks_free[place[g][0]] if i == 3 else sem(f"cpad_{l}"), 1)
                    for i in range(4):
                        n = part * 4 + i
                        act.wait_ge(sem(f"conv_{l}"), n + 1)
                        A(qk[:, n, c0:T].rearrange("p (s n) -> p s n", n=CTX), cacc[:, n % 2, s0:2, :],
                          ACT.Silu).then_inc(sem(f"qk_{l}"), 1)
                        advance(1)
                advance(KT - 4)
                g = plan[l, "v"][1]
                wait_group(g)
                act.wait_ge(sem(f"mixer_filled_{l}"), 1)
                A(vaug[:, :, :, 0:MD], ps[:, bank(g):bank(g) + 4, :].rearrange("p t (h e) -> p t h e", h=MH),
                  ACT.Copy).then_inc(banks_free[place[g][0]], 1)
                advance(1)
                g = plan[l, "gates"][1]
                wait_group(g)
                A(gz[:, :], ps[0:16, bank(g), :], ACT.Copy).then_inc(banks_free[place[g][0]], 1)

                act.wait_ge(sem(f"rows_{l}"), 2)
                link(A(R[0:36, 4, :], R[0:36, 1, :], ACT.Abs))
                link(A(R[0:36, 4, :], R[0:36, 4, :], ACT.Exp, scale=-1.0))
                A(R[0:36, 4, :], R[0:36, 4, :], ACT.Ln, bias=cst[0:36, 2:3]).then_inc(sem(f"softplus_{l}"), 1)
                advance(5)

                def natural(q, src, **kw_):
                    A(RN[0:MH, q, :], src[0:MH, :], ACT.Exp, **{a: v[0:MH] if a == "bias" else v for a, v in kw_.items()})
                    return A(RN[32:36, q, :].rearrange("p (s n) -> p s n", s=2)[:, :, ::-1],
                             src[32:36, :].rearrange("p (s n) -> p s n", s=2), ACT.Exp,
                             **{a: v[32:36] if a == "bias" else v for a, v in kw_.items()})

                for q in range(3):
                    act.wait_ge(sem(f"explog_{l}"), q + 1)
                    if q == 0:
                        natural(1, R[0:36, 4, :], scale=-1.0).then_inc(sem(f"exprow_{l}"), 1)
                    elif q == 1:
                        natural(2, R[0:36, 5, :]).then_inc(sem(f"exprow_{l}"), 1)
                    else:
                        natural(3, R[0:36, 0, :], scale=-1.0, bias=cst[0:36, 1:2]).then_inc(sem(f"exprow_{l}"), 1)
                act.wait_ge(sem(f"explog_{l}"), 4)
                A(dlog[:, :], dlog[:, :], ACT.Exp).then_inc(sem(f"exprow_{l}"), 1)
                advance(KT - 4)
                g = plan[l, "cqkv"][1]
                b0 = bank(g)
                wait_group(g)
                link(A(craw[:, 0:2, cq:T], ps[:, b0:b0 + 2, 0:T - cq], ACT.Copy))
                link(A(craw[:, 2, :], ps[:, b0 + 2, :], ACT.Copy))
                A(krs[NOPE:AQK, :], ps[0:ROPE, b0 + 3, :], ACT.Copy).then_inc(banks_free[place[g][0]], 1)
                A(csq[:, 0:2, cq:T], craw[:, 0:2, cq:T], ACT.Square)
                A(csq[:, 2, :], craw[:, 2, :], ACT.Square).then_inc(sem(f"csq_{l}"), 1)
                act.wait_ge(sem(f"tokt_{l}"), 1)
                A(tok[:, 0:8, :], ps[:, 2, 0:288].rearrange("p (a b) -> p a b", b=36), ACT.Copy)
                link(A(tok[:, 8:16, :], ps[:, 3, 0:288].rearrange("p (a b) -> p a b", b=36), ACT.Copy))
                A(dec[:, :, :], ps[:, 3, 288:320].rearrange("p (a b) -> p a b", b=4), ACT.Copy).then_inc(sem(f"tok_{l}"), 1)
                advance(4)
                act.wait_ge(sem(f"css_{l}"), 1)
                A(crm[:, 0, cq // 128:NT], ps[:, 0, cq // 128:NT], ACT.Sqrt, bias=cst[:, 0:1], scale=1.0 / QR)
                A(crm[:, 1, :], ps[:, 0, NT:2 * NT], ACT.Sqrt, bias=cst[:, 0:1],
                  scale=1.0 / KVR).then_inc(sem(f"crm_{l}"), 1)
                advance(KT - 4)
                g = plan[l, "o"][1]
                wait_group(g)
                A(sigo[:, :, cq:T], ps[:, bank(g):bank(g) + 4, 0:T - cq], ACT.Sigmoid).then_inc(banks_free[place[g][0]], 1)

                t0 = cq // 128
                outs = [j for j in range(NT) if scan_tile(0, j) >= t0]
                for h in range(MH):
                    for d in range(2):
                        act.wait_ge(sem(f"dlog_{l}"), 2 * h + d + 1)
                        A(dt_[:, d, t0:, :], dt_[:, d, t0:, :], ACT.Exp).then_inc(sem(f"dexp_{l}"), 1)
                    if h:
                        act.wait_ge(sem(f"cupd_{l}"), 6 * h)
                    act.wait_ge(sem(f"headmm_{l}"), h + 1)
                    for d in range(2):
                        for j in range(NT - 1):
                            tt = scan_tile(d, j)
                            ins = A(kw[:, d, tt, :], ps[:, 3, tt * 128:(tt + 1) * 128], ACT.Copy,
                                    scale=tok[:, 8 + tt, 32 * d + h:32 * d + h + 1])
                    ins.then_inc(sem(f"kw_{l}"), 1)
                    for j in range(1, NT):
                        for d in range(2):
                            if j not in outs:
                                continue
                            tt = scan_tile(d, j)
                            n = 2 * (len(outs) * h + outs.index(j)) + d + 1
                            act.wait_ge(sem(f"nmm_{l}"), n)
                            A(an[:, d, :], ps[:, 6 + d, 0:MD + 1], ACT.Copy,
                              scale=tok[:, 4 + tt, 32 * d + h:32 * d + h + 1]).then_inc(sem(f"an_{l}"), 1)
                    if h == MH - 1:
                        A(cn_hi[:, 0:2, cq:T], craw[:, 0:2, cq:T], ACT.Copy)
                        A(cn_hi[:, 2, :], craw[:, 2, :], ACT.Copy).then_inc(sem(f"cn_hi_{l}"), 1)
                    act.wait_ge(sem(f"hsum_{l}"), h + 1)
                    for tt in range(t0, NT):
                        ins = A(sqt[:, tt, :], hsn[:, h, tt, :], ACT.Square, accum_out=rn[:, h, tt:tt + 1])
                    link(ins, f"hsq_{l}")
                A(rn[:, :, t0:], rn[:, :, t0:], ACT.Sqrt, bias=cst[:, 0:1], scale=1.0 / MD).then_inc(sem(f"hrms_{l}"), 1)
                def queries(half):
                    g = plan[l, "uq", half][1]
                    wait_group(g)
                    A(q96[:, half * 4:half * 4 + 4, cq:T], ps[0:AQK, bank(g):bank(g) + 4, 0:T - cq],
                      ACT.Copy).then_inc(banks_free[place[g][0]], 1)

                advance(2)
                queries(0)
                for h in range(MH):
                    act.wait_ge(sem(f"yt_{l}"), h + 1)
                    A(y_hi[0][:, h, cq:T], yt[:, h % 2, cq:T], ACT.Copy).then_inc(sem(f"y0h_{l}"), 1)
                advance(2)
                queries(1)
                advance(1)
                g = plan[l, "kn"][1]
                b0 = bank(g)
                wait_group(g)
                k2 = k96[0:NOPE].rearrange("p (i s) n -> p i s n", s=2)
                link(A(k2[:, :, 0, :], ps[0:NOPE, b0:b0 + 4, :], ACT.Copy))
                A(k2[:, :, 1, :], ps[NOPE:128, b0:b0 + 4, :], ACT.Copy).then_inc(banks_free[place[g][0]], 1)
                advance(1)
                g = plan[l, "kv"][1]
                wait_group(g)
                A(vm[:, :, :], ps[:, bank(g):bank(g) + 4, :], ACT.Copy).then_inc(banks_free[place[g][0]], 1)
                act.wait_ge(*freed(g))
                fill = merge_steps(l, 0)
                qk_norm(l, 0, fill)
                attention(l, 0, fill)
                for _ in fill:
                    pass

                act.wait_ge(sem("ay"), before(l, 0)[1] // 8 + len(items(l)) // 8)
                advance(KT)
                g = plan[l, "gq"][1]
                wait_group(g)
                A(qg[:, :, cq:T], ps[:, bank(g):bank(g) + 4, 0:T - cq], ACT.Copy).then_inc(banks_free[place[g][0]], 1)
                advance(KT)
                g = plan[l, "gkv"][1]
                b0 = bank(g)
                wait_group(g)
                for m in range(GKV):
                    for r in (0, GD):
                        link(A(kg[r:r + GD, m, :], ps[m * GD:(m + 1) * GD, b0, :], ACT.Copy))
                A(vg[:, :, :], ps[:, b0 + 1, :].rearrange("p (t n) -> p t n", n=128), ACT.Copy).then_inc(banks_free[place[g][0]], 1)
                act.wait_ge(*freed(g))
                fill = merge_steps(l, 1)
                qk_norm(l, 1, fill)
                attention(l, 1, fill)
                for _ in fill:
                    pass

                for _ in merge_steps(l, 2):
                    pass
                advance(KT + 4)
                squares(l, 2, range(4))
                advance(KT - 5)
                squares(l, 2, range(4, KT))
                norm(l, 2)
                ffn(l, 1)
            for i in range(2):
                for b in range(2):
                    act.wait_ge(sem("out_t"), i + 1)
                    A(xout[:, i, b * 512:(b + 1) * 512], ps[:, 2 * i + b, :], ACT.Copy).then_inc(sem("out_ready"), 1)

        @block.vector
        def _(dve):
            V = nc.vector
            link = Chain(dve, "dve_order")
            pos = [0]

            def split(u, it=None, per=0):
                n = size[u]
                dve.wait_ge(hi_done, u + 1 if it is None else u + 1 + it * per)
                V.tensor_tensor(w_lo[:, u % RING, 0:n], w_raw[:, u % LOADS, 0:n],
                                w_hi[:, u % RING, 0:n].bitcast(fp32), ALU.subtract).then_inc(lo_done, 1)

            def advance(n):
                for _ in range(n):
                    if pos[0] < U:
                        split(pos[0])
                    pos[0] += 1

            def add_squares(l, j, tiles):
                m_ = 3 * l + j
                c0 = first_col(l, j == 2)
                for i in tiles:
                    if i:
                        dve.wait_ge(sem("sq"), KT * m_ + i + 1)
                        link(V.tensor_tensor(acc[:, c0:T], acc[:, c0:T], sq[:, i % 2, c0:T], ALU.add), "sq_added")

            def norm(l, j):
                m_ = 3 * l + j
                c0 = first_col(l, j == 2)
                inv = norm_banks(l, j)[1]
                dve.wait_ge(sem("rms"), m_ + 1)
                V.reciprocal(rms[:, c0 // 128:NT], rms[:, c0 // 128:NT]).then_inc(sem("rms_inv"), 1)
                if m_:
                    advance(1)
                dve.wait_ge(sem("rms_spread"), m_ + 1)
                for i in range(KT + 1):
                    if i < KT:
                        if i >= 2:
                            dve.wait_ge(sem("hn"), KT * m_ + i - 1)
                        for s, a, b in streams(c0):
                            ins = V.scalar_tensor_tensor(out=t1[:, i % 2, a:b], in0=x[:, i, a:b],
                                                         scalar=gain[:, j, i, s:s + 1], in1=ps[:, inv, a:b],
                                                         op0=ALU.mult, op1=ALU.mult)
                        ins.then_inc(sem("scaled"), 1)
                    if i >= 1:
                        dve.wait_ge(sem("h_hi"), KT * m_ + i)
                        V.tensor_tensor(h_lo[:, i - 1, c0:T], hn[:, (i - 1) % 2, c0:T],
                                        h_hi[:, i - 1, c0:T].bitcast(fp32), ALU.subtract).then_inc(sem("h"), 1)

            copied = [0]

            def mod_copy(l, a, b, bank_):
                copied[0] += b - a
                dve.wait_ge(sem("mod_t"), copied[0])
                at = slice(a * 4, b * 4)
                link(V.tensor_copy(modt[:, at, :], ps[:, bank_, a * 8:b * 8].rearrange("p (a s) -> p a s", s=2)),
                     "mod_copied")

            def mods(l, a, b):
                rows = slice(a * KT, b * KT)
                m3 = mod[:, :, :, :].rearrange("p a k s -> p (a k) s")
                link(V.tensor_tensor(m3[:, rows, :], modt[:, rows, :],
                                     bmod[:, l, rows].rearrange("p (a s) -> p a s", s=1)
                                     .to_broadcast([128, (b - a) * KT, 2]), ALU.add))
                for j in [j for j in range(3) if a <= 3 * j + 1 < b]:
                    link(V.scalar_tensor_tensor(
                        out=gain[:, j, :, :], in0=mod[:, 3 * j + 1, :, :], scalar=1.0,
                        in1=prm[:, l, P_NORM + j * KT:P_NORM + (j + 1) * KT].rearrange("p (k s) -> p k s", s=1)
                        .to_broadcast([128, KT, 2]), op0=ALU.add, op1=ALU.mult))
                for gate in (2, 8):
                    if a <= gate < b:
                        link(V.tensor_scalar(mod[:, gate, :, :], mod[:, gate, :, :], 0.5, None, ALU.mult))

            def residual(l, m, g0, c0, gate, after=None):
                g = g0 + m
                for i in range(4):
                    if after and i < 3:
                        dve.wait_ge(sem("tile_sum"), 3 * (3 * after[0] + after[1] - 1) + i + 1)
                    elif i == 3 or i == 0:
                        dve.wait_ge(unit_used, ends[g])
                    for s, a, b in streams(c0):
                        ins = V.scalar_tensor_tensor(out=x[:, 4 * m + i, a:b], in0=ps[:, bank(g) + i, a - c0:b - c0],
                                                     scalar=mod[:, gate, 4 * m + i, s:s + 1],
                                                     in1=x[:, 4 * m + i, a:b], op0=ALU.mult, op1=ALU.add)
                    ins.then_inc(banks_free[place[g][0]] if i == 3 else sem("x_new"), 1)
                    if after and i:
                        add_squares(*after, [4 * m + i - 1])
                if after:
                    add_squares(*after, [4 * m + 3])

            def ffn(l, f):
                done = FT // 2 * (2 * l + f)
                c0 = first_col(l, f == 1)
                n = T - c0
                u0, g0 = plan[l, "in", f]
                after = (l, 1) if f == 0 else (l + 1, 0) if l < DEPTH - 1 else None

                def evac(b, g, it=None):
                    off = (lambda v: v if it is None else v + it * 2)
                    s4_ = bank(g0 + b)
                    dve.wait_ge(sem("sil"), off(done + b + 1))
                    if b:
                        dve.wait_ge(sem("mid"), off(done + b))
                    V.tensor_tensor(mt[:, :, 0:n], ps[:, s4_ + 2:s4_ + 4, 0:n], sil[:, :, 0:n],
                                    ALU.mult).then_inc(banks_free[place[g0 + b][0]], 1)
                    dve.wait_ge(sem("mid_hi"), off(done + b + 1))
                    at = bass.ds(2 * g, 2) if it is not None else slice(2 * g, 2 * g + 2)
                    V.tensor_tensor(mid_lo[:, at, 0:n], mt[:, :, 0:n], mid_hi[:, at, 0:n].bitcast(fp32),
                                    ALU.subtract).then_inc(sem("mid"), 1)

                advance(KT)
                evac(0, 0)
                with dve.Fori(0, FT // 4) as i:
                    for b in (1, 2):
                        for j in range(KT):
                            split(pos[0] + (b - 1) * KT + j, i, 2 * KT)
                        evac(b, i * 2 + b, i)
                pos[0] += 2 * KT * (FT // 4)
                _, g0 = plan[l, "out", f]
                for g in range(2):
                    groups, first, ml = beside(l, f, g)
                    last = (l, f, g) == (DEPTH - 1, 1, 1)
                    per = LOADS + groups * KT
                    advance(EDGE)
                    with dve.Fori(0, LOOPS - last) as i:
                        for j in range(per):
                            split(pos[0] + j, i, per)
                    pos[0] += (LOOPS - last) * per
                    if groups:
                        mod_copy(ml, first, first + LOOPS * groups, 4 - bank(g0 + g) + 2)
                    if g == 1 and f == 0:
                        mods(l, 3 if l == 0 else 6, 9)
                    elif g == 1 and l < DEPTH - 1:
                        mods(l + 1, 0, 6)
                    if after and g == 1:
                        add_squares(*after, range(4))
                    advance(EDGE + last * per - (after is not None and g == 1))
                    residual(l, g, g0, c0, 2 if f == 0 else 8, after if g == 1 else None)

            def qk_norm(l, a, fill):
                P, xn, co, si, cos, tiles = rope_setup(l, a)
                nrm = scr[a][1]
                sin = tb("sinm" if a == 0 else "sing")
                tb_, ib_ = before(l, a)
                rows = STATS if a == 0 else 2 * len(tiles)

                def normed(i):
                    dst, c0, row = tiles[i]
                    dve.wait_ge(sem("qspread"), tb_ + i + 1)
                    if i >= 2:
                        dve.wait_ge(sem("qcos"), tb_ + i - 1)
                        dve.wait_ge(sem("qsin"), tb_ + i - 1)
                    if c0 < CTX:
                        V.scalar_tensor_tensor(out=dst[:, 0:CTX], in0=dst[:, 0:CTX], scalar=prm[0:P, l, row:row + 1],
                                               in1=ps[0:P, AB + i % 2, 0:CTX], op0=ALU.mult, op1=ALU.mult)
                    V.scalar_tensor_tensor(out=xn[0:P, i % 2, :], in0=dst[:, CTX:T], scalar=prm[0:P, l, row:row + 1],
                                           in1=ps[0:P, AB + i % 2, CTX:T], op0=ALU.mult,
                                           op1=ALU.mult).then_inc(sem("qn"), 1)

                for i in range(len(tiles) // 4):
                    next(fill, None)
                dve.wait_ge(sem("qrms"), 2 * l + a + 1)
                V.reciprocal(nrm[0:rows, :], nrm[0:rows, :]).then_inc(sem("qinv"), 1)
                next(fill, None)
                next(fill, None)
                normed(0)
                for i in range(len(tiles)):
                    if fill_beside_tile(i):
                        next(fill, None)
                    if i + 1 < len(tiles):
                        normed(i + 1)
                    dve.wait_ge(sem("qrot"), tb_ + i + 1)
                    if i >= 2:
                        dve.wait_ge(sem("qk_final"), tb_ + i - 1)
                    V.tensor_tensor(si[0:P, i % 2, :], ps[0:P, AB + 2 + i % 2, 0:T - CTX], sin,
                                    ALU.mult).then_inc(sem("qsin"), 1)

            def attention(l, a, fill):
                pb, pt, ob, mx, rs = scr[a][5:]
                tb_, ib_ = before(l, a)
                scale = (AQK if a == 0 else GD) ** -0.5
                its = items(l)
                dve.wait_ge(sem("qk_final"), tb_ + len(rope_setup(l, a)[5]))

                def maxima(i):
                    n = key_tiles(its[i][0]) * 128
                    dve.wait_ge(sem("asc"), ib_ + i + 1)
                    link(V.reduce_max(mx[:, i % 2, 0:1], ps[:, AB + i % 2, 0:n], AX.X))
                    V.tensor_scalar(mx[:, i % 2, 1:2], mx[:, i % 2, 0:1], -scale, None, ALU.mult).then_inc(sem("amax"), 1)

                def divide(qt, last_item):
                    dve.wait_ge(sem("apv"), ib_ + last_item + 1)
                    link(V.reciprocal(rs[:, qt % 2, :], rs[:, qt % 2, :]))
                    V.tensor_tensor(ob[:, :, :], ps[:, AB + 3, :].rearrange("p (h e) -> p h e", h=8),
                                    rs[:, qt % 2, :].rearrange("p (h a) -> p h a", a=1).to_broadcast([128, 8, 64]),
                                    ALU.mult).then_inc(sem("aob"), 1)

                def output(qt, n):
                    dve.wait_ge(sem("ayh"), ib_ // 8 + n + 1)
                    cols = slice(qt * 128, (qt + 1) * 128)
                    V.tensor_tensor(y_lo[1 + a][:, :, cols], ps[:, AB + 2, :].rearrange("p (k n) -> p k n", n=128),
                                    y_hi[1 + a][:, :, cols].bitcast(fp32), ALU.subtract).then_inc(sem("ay"), 1)

                maxima(0)
                maxima(1)
                for i, (qt, h) in enumerate(its):
                    n = key_tiles(qt)
                    dve.wait_ge(sem("atr"), ib_ + i + 1)
                    V.tensor_copy(pt[:, i % 2, 0:n, :], ps[:, AB + 2, 0:n * 128].rearrange("p (k n) -> p k n", n=128))\
                        .then_inc(sem("apt"), 1)
                    if h == 0 and i:
                        divide(qt - 1, i - 1)
                    if i + 2 < len(its):
                        maxima(i + 2)
                    if fill_beside_item(l, a, i):
                        next(fill, None)
                    if h == 0 and i:
                        output(qt - 1, i // 8 - 1)
                divide(its[-1][0], len(its) - 1)
                output(its[-1][0], len(its) // 8 - 1)

            def merge_steps(l, n):
                n_q = T - first_col(l, True)

                def weighted(og, k):
                    g = plan[l, "branch", og, n][1]
                    two = slice(2 * k, 2 * k + 2)
                    src = ps[:, bank(g) + 2 * k:bank(g) + 2 * k + 2, 0:n_q]
                    out4 = mg[:, og * 4:og * 4 + 4, 0:n_q]
                    if k == 0:
                        dve.wait_ge(unit_used, ends[g])
                        dve.wait_ge(*freed(plan[l, "gate", og, n][1]))
                    ins = V.tensor_tensor(sg[:, two, 0:n_q] if n else out4[:, two, :], src, sg[:, two, 0:n_q], ALU.mult)
                    if k == 0:
                        ins.then_inc(sem("half_weighted"), 1)
                    else:
                        ins.then_inc(banks_free[place[g][0]], 1)
                    if n == 2 and k == 1:
                        dve.wait_ge(*freed(g))
                        dve.wait_ge(sem("summed_1"), 2 * l + 2)
                        link(V.tensor_tensor(out4, out4, sg[:, :, 0:n_q], ALU.add), "summed_2")

                def low(og):
                    dve.wait_ge(sem("g_hi"), 2 * l + og + 1)
                    V.tensor_tensor(g_lo[:, og * 4:og * 4 + 4, 0:n_q], mg[:, og * 4:og * 4 + 4, 0:n_q],
                                    g_hi[:, og * 4:og * 4 + 4, 0:n_q].bitcast(fp32), ALU.subtract).then_inc(sem("g"), 1)

                for s_, (og, name, k) in enumerate(MERGE):
                    if name == "branch out":
                        weighted(og, k)
                    if has_unit(s_ - 2):
                        advance(1)
                    if n == NBR - 1 and (og, name, k) == (1, "gate", 5):
                        low(0)
                    yield
                if n == NBR - 1:
                    low(1)

            link(V.memset(cst[:, 0:1], EPS))
            link(V.memset(cst[:, 1:2], 0.5 * float(np.log(MD))))
            V.memset(cst[:, 2:3], 1.0).then_inc(sem("cst"), 1)
            dve.wait_ge(sem("s_hi"), 1)
            V.tensor_tensor(s4[:, :, 2:4].rearrange("p k s -> p s k"), s_fm[:, :].rearrange("p (s k) -> p s k", s=2),
                            s4[:, :, 0:2].rearrange("p k s -> p s k").bitcast(fp32), ALU.subtract).then_inc(sem("s4"), 1)
            advance(RING)

            for l in range(DEPTH):
                cq = first_col(l, True)
                if l == 0:
                    advance(2 * KT)
                    add_squares(l, 0, range(KT))
                    with dve.Fori(0, FIRST_MODS // 2 - 1) as i:
                        for j in range(2 * KT):
                            split(pos[0] + j, i, 2 * KT)
                    pos[0] += (FIRST_MODS - 2) * KT
                    dve.wait_ge(sem("vec_t"), 1)
                    V.tensor_copy(prm[:, :, :], ps[:, 2, 0:DEPTH * P_ROWS].rearrange("p (l n) -> p l n", l=DEPTH))
                    V.tensor_copy(bmod[:, :, :], ps[:, 3, 0:DEPTH * M_ROWS].rearrange("p (l n) -> p l n", l=DEPTH))\
                        .then_inc(sem("params"), 1)
                    dve.wait_ge(sem("params"), 1)
                    mod_copy(l, 0, FIRST_MODS, 7)
                    mods(l, 0, 3)
                norm(l, 0)
                ffn(l, 0)
                norm(l, 1)

                dve.wait_ge(*freed(plan[l, "out", 0][1] + 1))
                V.memset(cpad[:, :, :, 0:2], 0.0)
                V.memset(cpad[:, :, :, 2 + CTX:4 + CTX], 0.0).then_inc(sem(f"pads_{l}"), 1)
                for part, name in enumerate(("q", "k")):
                    c0 = cq if part == 0 else 0
                    s0 = c0 // CTX
                    g = plan[l, name][1]
                    advance(KT if part == 0 else KT - 4)
                    for i in range(4):
                        n = part * 4 + i
                        if i < 3:
                            dve.wait_ge(sem(f"cpad_{l}"), 3 * part + i + 1)
                        else:
                            dve.wait_ge(*freed(g))
                        if n >= 2:
                            dve.wait_ge(sem(f"qk_{l}"), n - 1)
                        dst = cacc[:, n % 2, s0:2, :]
                        w = [prm[:, l, P_CONV + j * 2 * MH + n:P_CONV + j * 2 * MH + n + 1] for j in range(TAPS)]
                        link(V.tensor_scalar(dst, cpad[:, i, s0:2, 0:CTX], w[0], None, ALU.mult))
                        for j in range(1, TAPS):
                            ins = V.scalar_tensor_tensor(out=dst, in0=cpad[:, i, s0:2, j:j + CTX], scalar=w[j],
                                                         in1=dst, op0=ALU.mult, op1=ALU.add)
                            link(ins, f"conv_{l}" if j == TAPS - 1 else None)
                        advance(1)
                advance(KT - 4)
                advance(1)

                dve.wait_ge(sem(f"sel_{l}"), 1)
                link(V.tensor_scalar(R[0:36, 0, :], ps[0:36, 0, :], bgate[:, l, 0:1], None, ALU.add), f"rows_{l}")
                link(V.tensor_scalar(R[0:36, 1, :], ps[0:36, 1, :], bgate[:, l, 1:2], None, ALU.add), f"rows_{l}")
                dve.wait_ge(sem(f"softplus_{l}"), 1)
                link(V.scalar_tensor_tensor(out=R[0:36, 1, :], in0=R[0:36, 1, :], scalar=0.0, in1=R[0:36, 4, :],
                                            op0=ALU.min, op1=ALU.subtract))
                advance(1)
                for j in range(NT):
                    c = slice(j * 128, (j + 1) * 128)
                    link(V.tensor_tensor_scan(R[0:36, 2, c], tb("ones")[0:36, :], R[0:36, 1, c], 0.0, ALU.mult, ALU.add))
                link(V.tensor_tensor(R[0:36, 3, :], R[0:36, 0, :], R[0:36, 2, :], ALU.subtract))
                advance(2)
                link(V.memset(mprev[:, :], 0.0))
                for j in range(NT):
                    c = slice(j * 128, (j + 1) * 128)
                    e = (j + 1) * 128 - 1
                    link(V.tensor_tensor_scan(R[0:36, 1, c], R[0:36, 3, c], R[0:36, 3, c], mprev[:, j:j + 1], ALU.max, ALU.max))
                    link(V.tensor_tensor(mprev[:, j + 1:j + 2], R[0:36, 1, e:e + 1], R[0:36, 2, e:e + 1], ALU.add))

                advance(2)

                def chunks(row):
                    return R[0:36, row, :].rearrange("p (j n) -> p j n", n=128)

                def spread(ap):
                    return ap.to_broadcast([36, NT, 128])

                last_m = chunks(1)[:, :, 127:128]
                starts = mprev[:, 0:NT].rearrange("p (j a) -> p j a", a=1)
                link(V.tensor_tensor(chunks(4), chunks(1), spread(starts), ALU.subtract), f"explog_{l}")
                link(V.tensor_tensor(chunks(5), chunks(3), spread(last_m), ALU.subtract), f"explog_{l}")
                link(V.tensor_tensor(R[0:36, 0, :], R[0:36, 2, :], R[0:36, 1, :], ALU.add), f"explog_{l}")
                link(V.tensor_tensor(dlog[:, :].rearrange("p (j a) -> p j a", a=1), starts, last_m, ALU.subtract),
                     f"explog_{l}")
                dve.wait_ge(sem(f"mixer_filled_{l}"), 1)
                for q, row, by in ((0, 3, 1.0), (4, 1, -1.0)):
                    V.tensor_scalar(RN[0:MH, q, :], R[0:MH, row, :], by, None, ALU.mult)
                    ins = V.tensor_scalar(RN[32:36, q, :].rearrange("p (s n) -> p s n", s=2)[:, :, ::-1],
                                          R[32:36, row, :].rearrange("p (s n) -> p s n", s=2), by, None, ALU.mult)
                    link(ins, f"rown_{l}")

                t0 = cq // 128
                nt = NT - t0
                outs = [j for j in range(NT) if scan_tile(0, j) >= t0]
                advance(KT - 4)
                advance(4)
                dve.wait_ge(sem(f"crm_{l}"), 1)
                V.reciprocal(crm[:, 0, t0:], crm[:, 0, t0:])
                V.reciprocal(crm[:, 1, :], crm[:, 1, :]).then_inc(sem(f"crm_inv_{l}"), 1)
                advance(KT - 4)
                dve.wait_ge(sem(f"crm_spread_{l}"), 1)
                for i in range(3):
                    c0 = cq if i < 2 else 0
                    ins = V.scalar_tensor_tensor(out=craw[:, i, c0:T], in0=craw[:, i, c0:T],
                                                 scalar=prm[:, l, P_CQ + i:P_CQ + i + 1],
                                                 in1=ps[:, 1 - i // 2, c0:T], op0=ALU.mult, op1=ALU.mult)
                ins.then_inc(sem(f"cn_{l}"), 1)
                dve.wait_ge(sem(f"tok_{l}"), 1)
                mask = tb("mask").rearrange("p (d n) -> p d n", d=2)
                for h in range(MH):
                    dve.wait_ge(sem(f"headmm_{l}"), h + 1)
                    for d in range(2):
                        col = 32 * d + h
                        for tt in range(t0, NT):
                            ins = V.scalar_tensor_tensor(out=dt_[:, d, tt, :], in0=ps[:, 1 + d, tt * 128:(tt + 1) * 128],
                                                         scalar=tok[:, tt, col:col + 1], in1=mask[:, d],
                                                         op0=ALU.add, op1=ALU.min)
                        ins.then_inc(sem(f"dlog_{l}"), 1)
                    for d in range(2):
                        dve.wait_ge(sem(f"dexp_{l}"), 2 * h + d + 1)
                        link(V.tensor_tensor(P_[:, d, t0:, :], dt_[:, d, t0:, :],
                                             ps[:, 0, t0 * 128:].rearrange("p (t n) -> p t n", n=128), ALU.mult),
                             f"P_{l}")
                    an_n = [j for j in outs if j >= 1]
                    for j in range(NT):
                        for d in range(2):
                            tt = scan_tile(d, j)
                            if j in outs:
                                n = 2 * (len(outs) * h + outs.index(j)) + d + 1
                                dve.wait_ge(sem(f"nmm_{l}"), n)
                                if j == 0:
                                    link(V.tensor_copy(HN[:, d, tt, :], ps[:, 4 + d, 0:MD + 1]), f"hn_{l}")
                                else:
                                    dve.wait_ge(sem(f"an_{l}"), 2 * (len(an_n) * h + an_n.index(j)) + d + 1)
                                    link(V.tensor_tensor(HN[:, d, tt, :], ps[:, 4 + d, 0:MD + 1], an[:, d, :], ALU.add),
                                         f"hn_{l}")
                            if j < NT - 1:
                                dve.wait_ge(sem(f"dcmm_{l}"), 2 * (3 * h + j) + d + 1)
                                if j == 0:
                                    link(V.tensor_copy(C_[:, d, :], ps[:, 1 + d, 0:MD + 1]), f"cupd_{l}")
                                else:
                                    link(V.scalar_tensor_tensor(out=C_[:, d, :], in0=C_[:, d, :],
                                                                scalar=dec[:, 4 * d + h, j:j + 1],
                                                                in1=ps[:, 1 + d, 0:MD + 1], op0=ALU.mult, op1=ALU.add),
                                         f"cupd_{l}")
                    den = HN[:, :, t0:, MD:MD + 1].rearrange("p d t a -> p d (t a)")
                    dnt = dn[:, :, t0:]
                    floor = tok[:, 12 + t0:16, :].rearrange("p t c -> p c t")[:, h:h + 33:32, :]
                    link(V.scalar_tensor_tensor(out=dnt, in0=den, scalar=-1.0, in1=den, op0=ALU.mult, op1=ALU.max))
                    link(V.tensor_tensor(dnt, dnt, floor, ALU.max))
                    link(V.reciprocal(dnt, dnt))
                    link(V.tensor_tensor(hsn[:, h, t0:, :], HN[:, 0, t0:, 0:MD],
                                         dn[:, 0, t0:].rearrange("p (t a) -> p t a", a=1).to_broadcast([128, nt, MD]),
                                         ALU.mult))
                    for tt in range(t0, NT):
                        ins = V.scalar_tensor_tensor(out=hsn[:, h, tt, :], in0=HN[:, 1, tt, 0:MD],
                                                     scalar=dn[:, 1, tt:tt + 1], in1=hsn[:, h, tt, :],
                                                     op0=ALU.mult, op1=ALU.add)
                    link(ins, f"hsum_{l}")
                dve.wait_ge(sem(f"cn_hi_{l}"), 1)
                V.tensor_tensor(cn_lo[:, 0:2, cq:T], craw[:, 0:2, cq:T], cn_hi[:, 0:2, cq:T].bitcast(fp32), ALU.subtract)
                V.tensor_tensor(cn_lo[:, 2, :], craw[:, 2, :], cn_hi[:, 2, :].bitcast(fp32),
                                ALU.subtract).then_inc(sem(f"cn_lo_{l}"), 1)
                dve.wait_ge(sem(f"hrms_{l}"), 1)
                link(V.reciprocal(rn[:, :, t0:], rn[:, :, t0:]))
                for h in range(MH):
                    V.tensor_tensor(hsn[:, h, t0:, :], hsn[:, h, t0:, :],
                                    rn[:, h, t0:].rearrange("p (t a) -> p t a", a=1).to_broadcast([128, nt, MD]),
                                    ALU.mult).then_inc(sem(f"hout_{l}"), 1)
                dve.wait_ge(*freed(plan[l, "o"][1]))
                for h in range(MH + 1):
                    if h < MH:
                        dve.wait_ge(sem(f"ht_{l}"), h + 1)
                        if h >= 2:
                            dve.wait_ge(sem(f"y0_{l}"), h - 1)
                        V.scalar_tensor_tensor(out=yt[:, h % 2, cq:T], in0=ps[:, y0_bank(l, h), cq:T],
                                               scalar=prm[:, l, P_MH + h:P_MH + h + 1], in1=sigo[:, h, cq:T],
                                               op0=ALU.mult, op1=ALU.mult).then_inc(sem(f"yt_{l}"), 1)
                    if h:
                        dve.wait_ge(sem(f"y0h_{l}"), h)
                        V.tensor_tensor(y_lo[0][:, h - 1, cq:T], yt[:, (h - 1) % 2, cq:T],
                                        y_hi[0][:, h - 1, cq:T].bitcast(fp32), ALU.subtract).then_inc(sem(f"y0_{l}"), 1)

                advance(6)
                fill = merge_steps(l, 0)
                qk_norm(l, 0, fill)
                attention(l, 0, fill)
                for _ in fill:
                    pass
                advance(2 * KT)
                fill = merge_steps(l, 1)
                qk_norm(l, 1, fill)
                attention(l, 1, fill)
                for _ in fill:
                    pass
                for _ in merge_steps(l, 2):
                    pass
                advance(KT)
                residual(l, 0, plan[l, "wout"][1], cq, 5)
                advance(4)
                add_squares(l, 2, range(4))
                advance(KT - 5)
                residual(l, 1, plan[l, "wout"][1], cq, 5, (l, 2))
                norm(l, 2)
                ffn(l, 1)

        @block.tensor
        def _(pe):
            M = nc.tensor.matmul
            TR = nc.tensor.transpose

            def all_free(g):
                for b in last_groups(g):
                    pe.wait_ge(*freed(b))

            def banks(g, it=None, per=0):
                v = place[g][1]
                if v:
                    pe.wait_ge(banks_free[place[g][0]], v if it is None else v + it * per)
                return bank(g)

            def ready(u, it=None, per=0):
                pe.wait_ge(lo_done, u + 1 if it is None else u + 1 + it * per)
                return u % RING

            def passes(dst, pairs, first, final, **kw_):
                for i, (a, b) in enumerate(pairs):
                    ins = M(dst, a, b, start=first and i == 0, stop=final and i == len(pairs) - 1, **kw_)
                return ins

            def three(w, r):
                return ((w[0], r[0]), (w[0], r[1]), (w[1], r[0]))

            def weight(slot, a, b):
                return w_hi[:, slot, a:b], w_lo[:, slot, a:b]

            def tiles4(b0, slot, rhs, n, first, final, count=4, width=128, each=None):
                for m in range(count):
                    if each and m:
                        ins.then_inc(each, 1)
                    ins = passes(ps[0:width, b0 + m, 0:n], three(weight(slot, m * width, (m + 1) * width), rhs),
                                 first, final)
                return ins

            def h_rhs(k, c0):
                return h_hi[:, k, c0:T], h_lo[:, k, c0:T]

            def feature_group(key, g, c0, norm_no=None, count=4):
                u0 = plan[key][0]
                b0 = banks(g)
                for k in range(KT):
                    if norm_no is not None:
                        pe.wait_ge(sem("h"), KT * norm_no + k + 1)
                    ins = tiles4(b0, ready(u0 + k), h_rhs(k, c0), T - c0, k == 0, k == KT - 1, count)
                    if k < KT - 1 or key[1] == "cqkv":
                        ins.then_inc(unit_used, 1)
                return ins

            rows_before, mod_copies = [0], [0]

            def norm_stats(l, j):
                m_ = 3 * l + j
                t0 = first_col(l, j == 2) // 128
                stats, inv = norm_banks(l, j)
                v = place[norm_group(l, j)][1]
                pe.wait_ge(banks_free[place[norm_group(l, j)][0]], v)
                pe.wait_ge(sem("sq_added"), (KT - 1) * (m_ + 1))
                for tt in range(t0, NT):
                    ins = M(ps[:, stats, tt:tt + 1], acc[:, tt * 128:(tt + 1) * 128], tb("ones")[:, 0:1],
                            start=True, stop=True)
                ins.then_inc(sem("ss"), 1)
                all_free(norm_group(l, j))
                pe.wait_ge(sem("rms_inv"), m_ + 1)
                for tt in range(t0, NT):
                    ins = M(ps[:, inv, tt * 128:(tt + 1) * 128], rms[:, tt:tt + 1].to_broadcast([128, 128]), ident,
                            start=True, stop=True)
                ins.then_inc(sem("rms_spread"), 1)

            def ffn(l, f):
                done = FT // 2 * (2 * l + f)
                c0 = first_col(l, f == 1)
                n = T - c0
                u0, g0 = plan[l, "in", f]

                def group(b, first, it=None):
                    b0 = banks(g0 + b, it, 1)
                    for k in range(KT):
                        if first:
                            pe.wait_ge(sem("h"), KT * (3 * l + 2 * f) + k + 1)
                        slot = ready(u0 + b * KT + k, it, 2 * KT)
                        ins = tiles4(b0, slot, h_rhs(k, c0), n, k == 0, k == KT - 1)
                        if k < KT - 1:
                            ins.then_inc(unit_used, 1)
                    finish(ins, g0 + b)

                group(0, True)
                with pe.Fori(0, FT // 4) as i:
                    for b in (1, 2):
                        group(b, False, i)
                u0, g0 = plan[l, "out", f]
                for g in range(2):
                    groups, first, ml = beside(l, f, g)
                    b0 = banks(g0 + g)
                    if g == 0:
                        pe.wait_ge(sem("mid"), done + FT // 2)

                    def unit(u, k, it=None, per=0):
                        slot = ready(u, it, per)
                        kk = k if it is None else bass.ds(it * LOADS + k, 1)
                        final = it is None and k == FT - 1
                        return tiles4(b0, slot, (mid_hi[:, kk, 0:n], mid_lo[:, kk, 0:n]), n, k == 0, final,
                                      each=sem("tile_sum") if final and g and (l, f) != (DEPTH - 1, 1) else None)

                    if g and beside(l, f, 0)[0]:
                        pe.wait_ge(sem("mod_copied"), mod_copies[0])
                    for k in range(EDGE):
                        unit(u0 + k, k).then_inc(unit_used, 1)
                    u0 += EDGE
                    per = LOADS + groups * KT
                    free = 4 - b0
                    with pe.Fori(0, LOOPS) as i:
                        j = f_ = turned = 0
                        for what in turn_units(groups):
                            if what == "ffn":
                                unit(u0 + j, EDGE + f_, i, per).then_inc(unit_used, 1)
                                f_ += 1
                            elif what == "turn":
                                m = turned
                                turned += 1
                                pe.wait_ge(sem("mod_rows"), rows_before[0] + m + 1 + i * groups)
                                at = (first + m) * 8
                                for q in range(4):
                                    ins = M(ps[:, free + 2, bass.ds(i * (8 * groups) + (at + 2 * q), 2)],
                                            mrow[0:4, 0, q * 128:(q + 1) * 128], tb("comb"), start=True, stop=True)
                                ins.then_inc(sem("mod_t"), 1)
                                continue
                            else:
                                m, k = what
                                if (m, k) == (0, 0):
                                    pe.wait_ge(*freed(g0 + g - 1))
                                slot = ready(u0 + j, i, per)
                                M(ps[0:4, free + m % 2, :], s4[:, k, :], w_hi[:, slot, :], start=k == 0, stop=False)
                                M(ps[0:4, free + m % 2, :], s4[:, k, :], w_lo[:, slot, :], start=False,
                                  stop=k == KT - 1).then_inc(unit_used, 1)
                            j += 1
                    u0 += LOOPS * per
                    rows_before[0] += LOOPS * groups
                    if groups:
                        mod_copies[0] += 1
                    for k in range(EDGE):
                        ins = unit(u0 + k, FT - EDGE + k)
                        if k < EDGE - 1:
                            ins.then_inc(unit_used, 1)
                    u0 += EDGE
                    finish(ins, g0 + g)
                if groups:
                    pe.wait_ge(sem("mod_copied"), mod_copies[0])

            def qk_norm_attend(l, a, g_next, fill):
                P, xn, co, si, cos, tiles = rope_setup(l, a)
                nsq = scr[a][0]
                pb, pt, ob = scr[a][5:8]
                tb_, ib_ = before(l, a)
                nrm = scr[a][1]
                rot = tb("rotm" if a == 0 else "rotg")
                rows = STATS if a == 0 else 2 * len(tiles)
                all_free(g_next)
                for i, (_, c0, _) in enumerate(tiles):
                    at = STATS - 1 - i if a == 0 else STATS - 2 - 2 * i
                    pe.wait_ge(sem("qsq"), tb_ + i + 1)
                    M(ps[0:rows, AB, c0:T], tb("sum1" if a == 0 else "sum2")[0:P, at:at + rows], nsq[0:P, i % 2, c0:T],
                      start=i == 0, stop=i == len(tiles) - 1).then_inc(sem("qss"), 1)
                    if i % 4 == 3:
                        next(fill, None)
                next(fill, None)
                next(fill, None)

                def spread(i):
                    c0 = tiles[i][1]
                    if i >= 2:
                        pe.wait_ge(sem("qn"), tb_ + i - 1)
                    row = ident[0:rows, i:i + 1].to_broadcast([rows, P]) if a == 0 else \
                        tb("spread")[:, i * 128:(i + 1) * 128]
                    M(ps[0:P, AB + i % 2, c0:T], row, nrm[0:rows, c0:T], start=True, stop=True)\
                        .then_inc(sem("qspread"), 1)

                pe.wait_ge(sem("qinv"), 2 * l + a + 1)
                spread(0)
                for i in range(len(tiles)):
                    if i + 1 < len(tiles):
                        spread(i + 1)
                    pe.wait_ge(sem("qn"), tb_ + i + 1)
                    if i >= 2:
                        pe.wait_ge(sem("qsin"), tb_ + i - 1)
                    M(ps[0:P, AB + 2 + i % 2, 0:T - CTX], rot, xn[0:P, i % 2, :], start=True, stop=True)\
                        .then_inc(sem("qrot"), 1)
                    if fill_beside_tile(i):
                        next(fill, None)
                pe.wait_ge(sem("qk_final"), tb_ + len(tiles))

                its = items(l)

                def scores(i):
                    qt, h = its[i]
                    n = key_tiles(qt) * 128
                    if i >= 2:
                        pe.wait_ge(sem("aexp"), ib_ + i - 1)
                    cols = slice(qt * 128, (qt + 1) * 128)
                    if a == 0:
                        q_, k_ = q96[:, h, cols], k96[:, h, 0:n]
                    else:
                        r = slice(64 * (h % 2), 64 * (h % 2) + 64)
                        q_, k_ = qg[r, h // 2, cols], kg[r, h // 4, 0:n]
                    M(ps[:, AB + i % 2, 0:n], q_, k_, start=True, stop=True).then_inc(sem("asc"), 1)

                def turned(i):
                    pe.wait_ge(sem("aexp"), ib_ + i + 1)
                    if i:
                        pe.wait_ge(sem("apt"), ib_ + i)
                    if i % 8 == 1 and i > 8:
                        pe.wait_ge(sem("ay"), ib_ // 8 + i // 8)
                    for kt in range(key_tiles(its[i][0])):
                        c = slice(kt * 128, (kt + 1) * 128)
                        ins = TR(ps[:, AB + 2, c], pb[:, i % 2, c], ident)
                    ins.then_inc(sem("atr"), 1)

                def values(i):
                    qt, h = its[i]
                    pe.wait_ge(sem("apt"), ib_ + i + 1)
                    if h == 0 and i:
                        pe.wait_ge(sem("aob"), ib_ // 8 + i // 8)
                    for kt in range(key_tiles(qt)):
                        v = vm[:, kt, h * AV:(h + 1) * AV] if a == 0 else vg[:, kt, h // 4 * GD:(h // 4 + 1) * GD]
                        ins = M(ps[:, AB + 3, h * 64:(h + 1) * 64], pt[:, i % 2, kt, :], v, start=kt == 0,
                                stop=kt == key_tiles(qt) - 1)
                    ins.then_inc(sem("apv"), 1)

                def turn_output(n):
                    pe.wait_ge(sem("aob"), ib_ // 8 + n + 1)
                    for q in range(4):
                        ins = TR(ps[:, AB + 2, q * 128:(q + 1) * 128],
                                 ob[:, 2 * q:2 * q + 2, :].rearrange("p h e -> p (h e)"), ident)
                    ins.then_inc(sem("aot"), 1)

                scores(0)
                scores(1)
                for i, (qt, h) in enumerate(its):
                    turned(i)
                    if i + 2 < len(its):
                        scores(i + 2)
                    if fill_beside_item(l, a, i):
                        next(fill, None)
                    values(i)
                    if h == 0 and i:
                        turn_output(i // 8 - 1)
                turn_output(len(its) // 8 - 1)
                for _ in fill:
                    pass
                pe.wait_ge(sem("ay"), ib_ // 8 + len(its) // 8)

            def merge_steps(l, n):
                cq = first_col(l, True)
                for s_, (og, name, k) in enumerate(MERGE):
                    if has_unit(s_):
                        u0, g = plan[l, name, og, n]
                        b0 = banks(g) if k == 0 else bank(g)
                        rhs = (h_hi, h_lo) if name == "gate" else (y_hi[n], y_lo[n])
                        tiles4(b0, ready(u0 + k), (rhs[0][:, k, cq:T], rhs[1][:, k, cq:T]), T - cq,
                               k == 0, not has_unit(s_ + 1)).then_inc(unit_used, 1)
                    yield

            def finish(ins, g):
                ins.then_inc(unit_used, 1)

            pe.wait_ge(sem("tab_in"), 16)
            pe.wait_ge(sem("s_act"), 1)
            TR(ps[:, 0, 0:2 * KT], s_act[:, :], ident[0:2 * KT, 0:2 * KT]).then_inc(sem("x_t"), 1)
            pe.wait_ge(sem("s4"), 1)

            def x_start():
                pe.wait_ge(sem("x_in"), 16 * NT)
                for i in range(NT):
                    b = 2 if i % 2 == 0 else 5
                    if i >= 2:
                        pe.wait_ge(sem("x_ready"), i - 1)
                    for k in range(KT):
                        ins = TR(ps[:, b + k // 4, k % 4 * 128:(k % 4 + 1) * 128], xin[:, i, k * 128:(k + 1) * 128],
                                 ident)
                    ins.then_inc(sem("x_t"), 1)

            def vector_start():
                pe.wait_ge(sem("x_ready"), NT)
                pe.wait_ge(sem("vectors_in"), 16 * VECTORS)
                for l in range(DEPTH):
                    TR(ps[:, 2, l * P_ROWS:(l + 1) * P_ROWS], vrow[:, l, :], ident[0:P_ROWS, 0:P_ROWS])
                    ins = TR(ps[:, 3, l * M_ROWS:(l + 1) * M_ROWS], mvrow[:, l, :], ident[0:M_ROWS, 0:M_ROWS])
                ins.then_inc(sem("vec_t"), 1)

            for l in range(DEPTH):
                cq = first_col(l, True)
                n_q = T - cq
                u0, g0 = plan[0, "mod"]

                def turn(b, j):
                    for q in range(4):
                        at = slice(j * 8 + 2 * q, j * 8 + 2 * q + 2) if isinstance(j, int) else bass.ds(j * 8 + 2 * q, 2)
                        ins = M(ps[:, 7, at], mrow[0:4, b, q * 128:(q + 1) * 128], tb("comb"),
                                start=True, stop=True)
                    return ins

                def mod_pair(u, g, j, it=None):
                    for b in range(2):
                        b0 = banks(g + b, it, 1)
                        for k in range(KT):
                            slot = ready(u + b * KT + k, it, 2 * KT)
                            M(ps[0:4, b0, :], s4[:, k, :], w_hi[:, slot, :], start=k == 0, stop=False)
                            M(ps[0:4, b0, :], s4[:, k, :], w_lo[:, slot, :], start=False,
                              stop=k == KT - 1).then_inc(unit_used, 1)
                    for b in range(2):
                        fs, fv = freed(g + b)
                        pe.wait_ge(fs, fv if it is None else fv + it)
                        turn(b, j + b).then_inc(sem("mod_t"), 1)

                if l == 0:
                    mod_pair(u0, g0, 0)
                    x_start()
                    with pe.Fori(0, FIRST_MODS // 2 - 1) as i:
                        mod_pair(u0 + 2 * KT, g0 + 2, i * 2 + 2, i)
                    mod_copies[0] += 1
                    vector_start()
                norm_stats(l, 0)
                ffn(l, 0)
                norm_stats(l, 1)

                for name, c0 in (("q", cq), ("k", 0)):
                    g = plan[l, name][1]
                    finish(feature_group((l, name), g, c0, 3 * l + 1 if name == "q" else None), g)
                u0, g = plan[l, "v"]
                b0 = banks(g)
                for k in range(KT):
                    slot = ready(u0 + k)
                    for tt in range(NT):
                        c = slice(tt * 128, (tt + 1) * 128)
                        ins = passes(ps[:, b0 + tt, :], three((h_hi[:, k, c], h_lo[:, k, c]), weight(slot, 0, 512)),
                                     k == 0, k == KT - 1)
                    if k < KT - 1:
                        ins.then_inc(unit_used, 1)
                finish(ins, g)
                u0, g = plan[l, "gates"]
                b0 = banks(g)
                slot = ready(u0)
                for k in range(KT):
                    ins = passes(ps[0:16, b0, :], three(weight(slot, k * 16, (k + 1) * 16), h_rhs(k, 0)),
                                 k == 0, k == KT - 1)
                finish(ins, g)

                pe.wait_ge(*freed(plan[l, "gates"][1]))
                sel = tb("sel").rearrange("p (a n) -> p a n", n=36)
                back = gz[:, :].rearrange("p (s n) -> p s n", s=2)[:, :, ::-1]
                for b in range(2):
                    M(ps[0:36, b, :], sel[:, 2 * b, :], gz[:, :], start=True, stop=False)
                    ins = M(ps[0:36, b, :], sel[:, 2 * b + 1, :], back, start=False, stop=True)
                ins.then_inc(sem(f"sel_{l}"), 1)
                u0, g = plan[l, "cqkv"]
                b0 = banks(g)
                for k in range(KT):
                    slot = ready(u0 + k)
                    for m in range(3):
                        c0 = cq if m < 2 else 0
                        ins = passes(ps[:, b0 + m, 0:T - c0], three(weight(slot, m * 128, (m + 1) * 128), h_rhs(k, c0)),
                                     k == 0, k == KT - 1)
                    ins.then_inc(unit_used, 1)
                slot = ready(u0 + KT)
                for k in range(KT):
                    ins = passes(ps[0:ROPE, b0 + 3, :], three(weight(slot, k * ROPE, (k + 1) * ROPE), h_rhs(k, 0)),
                                 k == 0, k == KT - 1)
                finish(ins, g)
                pe.wait_ge(sem(f"exprow_{l}"), 4)
                pe.wait_ge(sem(f"rown_{l}"), 2)
                for q in range(4):
                    for tt in range(NT):
                        TR(ps[:, 2 + q // 2, ((q % 2) * 4 + tt) * 36:((q % 2) * 4 + tt + 1) * 36],
                           RN[:, q, tt * 128:(tt + 1) * 128], ident[0:36, 0:36])
                for d in range(2):
                    for h in range(MH):
                        r = 32 * d + h
                        ins = M(ps[:, 3, 288 + (4 * d + h) * 4:288 + (4 * d + h) * 4 + 4],
                                ident[0:36, r:r + 1].to_broadcast([36, 128]), dlog[:, :], start=True, stop=True)
                ins.then_inc(sem(f"tokt_{l}"), 1)
                g = plan[l, "o"][1]
                u0, b0 = plan[l, "o"][0], banks(g)
                for k in range(KT):
                    tiles4(b0, ready(u0 + k), h_rhs(k, cq), n_q, k == 0, k == KT - 1).then_inc(unit_used, 1)
                    if k == 3:
                        pe.wait_ge(sem(f"csq_{l}"), 1)
                        for tt in range(cq // 128, NT):
                            c = slice(tt * 128, (tt + 1) * 128)
                            M(ps[:, 0, tt:tt + 1], csq[:, 0, c], tb("ones")[:, 0:1], start=True, stop=False)
                            M(ps[:, 0, tt:tt + 1], csq[:, 1, c], tb("ones")[:, 0:1], start=False, stop=True)
                        for tt in range(NT):
                            ins = M(ps[:, 0, NT + tt:NT + tt + 1], csq[:, 2, tt * 128:(tt + 1) * 128], tb("ones")[:, 0:1],
                                    start=True, stop=True)
                        ins.then_inc(sem(f"css_{l}"), 1)
                    if k == 5:
                        pe.wait_ge(sem(f"crm_inv_{l}"), 1)
                        for i in range(2):
                            for tt in range(cq // 128 if i == 0 else 0, NT):
                                ins = M(ps[:, 1 - i, tt * 128:(tt + 1) * 128], crm[:, i, tt:tt + 1].to_broadcast([128, 128]),
                                        ident, start=True, stop=True)
                        ins.then_inc(sem(f"crm_spread_{l}"), 1)

                t0 = cq // 128
                outs = [j for j in range(NT) if scan_tile(0, j) >= t0]
                pe.wait_ge(sem(f"tok_{l}"), 1)
                pe.wait_ge(sem(f"cn_{l}"), 1)
                pe.wait_ge(*freed(plan[l, "o"][1]))
                pe.wait_ge(sem(f"qk_{l}"), 2 * MH)
                for h in range(MH):
                    if h:
                        pe.wait_ge(sem(f"P_{l}"), 2 * h)
                        pe.wait_ge(sem(f"cupd_{l}"), 6 * h)
                        pe.wait_ge(sem(f"kw_{l}"), h)
                    q_h, k_h = qk[:, h, :], qk[:, MH + h, :]
                    for tt in range(t0, NT):
                        c = slice(tt * 128, (tt + 1) * 128)
                        M(ps[:, 0, c], k_h[:, c], q_h[:, c], start=True, stop=True)
                    for d in range(2):
                        r = 32 * d + h
                        M(ps[:, 1 + d, t0 * 128:], ident[0:36, r:r + 1].to_broadcast([36, 128]), RN[:, 4, t0 * 128:],
                          start=True, stop=True)
                    for tt in range(NT):
                        c = slice(tt * 128, (tt + 1) * 128)
                        ins = TR(ps[:, 3, c], k_h[:, c], ident)
                    ins.then_inc(sem(f"headmm_{l}"), 1)
                    pe.wait_ge(sem(f"P_{l}"), 2 * h + 2)
                    pe.wait_ge(sem(f"kw_{l}"), h + 1)
                    for j in range(NT):
                        for d in range(2):
                            tt = scan_tile(d, j)
                            c = slice(tt * 128, (tt + 1) * 128)
                            if j >= 1:
                                pe.wait_ge(sem(f"cupd_{l}"), 2 * (3 * h + j - 1) + d + 1)
                            if j in outs:
                                n = 2 * (len(outs) * h + outs.index(j)) + d
                                if n >= 2:
                                    pe.wait_ge(sem(f"hn_{l}"), n - 1)
                                ins = M(ps[:, 4 + d, 0:MD + 1], P_[:, d, tt, :], vaug[:, tt, h, :], start=True, stop=True)
                                if j >= 1:
                                    ins = M(ps[:, 6 + d, 0:MD + 1], q_h[:, c], C_[:, d, :], start=True, stop=True)
                                ins.then_inc(sem(f"nmm_{l}"), 1)
                            if j < NT - 1:
                                M(ps[:, 1 + d, 0:MD + 1], kw[:, d, tt, :], vaug[:, tt, h, :],
                                  start=True, stop=True).then_inc(sem(f"dcmm_{l}"), 1)
                pe.wait_ge(sem(f"hn_{l}"), 2 * len(outs) * MH)
                def queries(half):
                    u0, g = plan[l, "uq", half]
                    b0 = banks(g)
                    for k in range(2):
                        ins = tiles4(b0, ready(u0 + k), (cn_hi[:, k, cq:T], cn_lo[:, k, cq:T]), n_q, k == 0, k == 1,
                                     4, AQK)
                        if k == 0:
                            ins.then_inc(unit_used, 1)
                    finish(ins, g)

                pe.wait_ge(sem(f"cn_lo_{l}"), 1)
                queries(0)
                for h in range(MH):
                    pe.wait_ge(sem(f"hout_{l}"), h + 1)
                    for tt in range(t0, NT):
                        ins = TR(ps[:, y0_bank(l, h), tt * 128:(tt + 1) * 128], hsn[:, h, tt, :], ident)
                    ins.then_inc(sem(f"ht_{l}"), 1)
                pe.wait_ge(sem(f"yt_{l}"), MH)
                queries(1)
                u0, g = plan[l, "kn"]
                b0 = banks(g)
                finish(tiles4(b0, ready(u0), (cn_hi[:, 2, :], cn_lo[:, 2, :]), T, True, True), g)
                u0, g = plan[l, "kv"]
                b0 = banks(g)
                slot = ready(u0)
                for tt in range(NT):
                    c = slice(tt * 128, (tt + 1) * 128)
                    ins = passes(ps[:, b0 + tt, :], three((cn_hi[:, 2, c], cn_lo[:, 2, c]), weight(slot, 0, 512)),
                                 True, True)
                finish(ins, g)
                qk_norm_attend(l, 0, plan[l, "kv"][1] + 1, merge_steps(l, 0))

                g = plan[l, "gq"][1]
                finish(feature_group((l, "gq"), g, cq), g)
                u0, g = plan[l, "gkv"]
                b0 = banks(g)
                for k in range(KT):
                    slot = ready(u0 + k)
                    passes(ps[:, b0, :], three(weight(slot, 0, 128), h_rhs(k, 0)), k == 0, k == KT - 1)
                    for tt in range(NT):
                        c = slice(tt * 128, (tt + 1) * 128)
                        ins = passes(ps[:, b0 + 1, c], three((h_hi[:, k, c], h_lo[:, k, c]), weight(slot, 128, 256)),
                                     k == 0 and tt == 0, k == KT - 1, skip_group_check=True)
                    if k < KT - 1:
                        ins.then_inc(unit_used, 1)
                finish(ins, g)
                qk_norm_attend(l, 1, g + 1, merge_steps(l, 1))

                for _ in merge_steps(l, 2):
                    pass
                u0, g0 = plan[l, "wout"]
                for og in range(2):
                    b0 = banks(g0 + og)
                    for k in range(KT):
                        if og == 0:
                            pe.wait_ge(sem("g"), 2 * l + k // 4 + 1)
                        ins = tiles4(b0, ready(u0 + og * KT + k), (g_hi[:, k, 0:n_q], g_lo[:, k, 0:n_q]), n_q,
                                     k == 0, k == KT - 1, each=sem("tile_sum") if og and k == KT - 1 else None)
                        if k < KT - 1:
                            ins.then_inc(unit_used, 1)
                    finish(ins, g0 + og)
                norm_stats(l, 2)
                ffn(l, 1)
            all_free(plan["end"][1])
            for i in range(2):
                for k in range(KT):
                    ins = TR(ps[:, 2 * i + k // 4, k % 4 * 128:(k % 4 + 1) * 128],
                             x[:, k, CTX + i * 128:CTX + (i + 1) * 128], ident)
                ins.then_inc(sem("out_t"), 1)





_INS = ["x", "c", "ctx", "c_ctx", "w_mod", "b_mod", "g_norm", "w_ffn_in", "w_ffn_out", "w_in", "b_mgate", "w_conv",
        "g_mhead", "g_cq", "g_ckv", "w_uq", "w_ukv", "g_q_mla", "g_k_mla", "g_q_gqa", "g_k_gqa", "w_branch", "w_out"]


def kernel(**inputs):
    import concourse.bacc as bacc
    from concourse.bass_utils import run_bass_kernel_spmd

    nc = bacc.Bacc("TRN2", target_bir_lowering=False, num_devices=1)
    arrays, t = {}, {}
    table, tab_at = tables()
    for name, a in [(n, np.ascontiguousarray(inputs[n])) for n in _INS] + [("tab", table)]:
        arrays[f"in_{name}"] = a
        t[name] = nc.dram_tensor(f"in_{name}", a.shape, mybir.dt.from_np(a.dtype), kind="ExternalInput").ap()
    out = nc.dram_tensor("out", (1, T - CTX, D), mybir.dt.float32, kind="ExternalOutput").ap()
    build(nc, t, out, tab_at)
    r = run_bass_kernel_spmd(nc, [arrays], core_ids=[0])
    return r.results[0]["out"]
```
